# Optimizing a Trainium2 kernel written in Bass

```python
import math
import jax, jax.numpy as jnp
from jax import lax
import numpy as np

D_MODEL = 1024
BATCH = 1
SEQ = 256
DEPTH = 2

RMS_EPS = 1e-5

SSD_EXPAND = 2
SSD_INNER = SSD_EXPAND * D_MODEL
SSD_HEAD_DIM = 64
SSD_HEADS = SSD_INNER // SSD_HEAD_DIM
SSD_STATE = 128
SSD_GROUPS = 4
SSD_HPG = SSD_HEADS // SSD_GROUPS
SSD_CONV = 4
SSD_CHUNK = 128
SSD_CONV_CH = SSD_INNER + 2 * SSD_GROUPS * SSD_STATE

ATTN_HEAD_DIM = 128
ATTN_KV_HEADS = D_MODEL // ATTN_HEAD_DIM
ATTN_PATTERNS = ((128, 1), (512, 4), (2048, 16))
ATTN_N_PAT = len(ATTN_PATTERNS)
ATTN_Q_HEADS = ATTN_N_PAT * ATTN_KV_HEADS
ATTN_OUT = ATTN_KV_HEADS * ATTN_HEAD_DIM
ATTN_BLOCK = 128
ROPE_THETA = 500000.0
ROPE_DIM = ATTN_HEAD_DIM // 4

FFN_HIDDEN = -(-8 * D_MODEL // (3 * 256)) * 256

_SEGMENTS = (SSD_INNER, SSD_CONV_CH, SSD_HEADS, ATTN_Q_HEADS * ATTN_HEAD_DIM,
             ATTN_OUT, ATTN_OUT, D_MODEL, D_MODEL)
IN_SPLITS = tuple(int(s) for s in np.cumsum(_SEGMENTS)[:-1])
N_IN = int(sum(_SEGMENTS))


def rms_norm(x, w):
    xf = x.astype(jnp.float32)
    y = xf * lax.rsqrt(jnp.mean(xf * xf, axis=-1, keepdims=True) + RMS_EPS)
    return (y * w.astype(jnp.float32)).astype(x.dtype)

def rope_tables(seq):
    inv = ROPE_THETA ** (-jnp.arange(0, ROPE_DIM, 2, dtype=jnp.float32) / ROPE_DIM)
    ang = jnp.arange(seq, dtype=jnp.float32)[:, None] * inv[None, :]
    return jnp.cos(ang), jnp.sin(ang)

def apply_partial_rope(t, cos, sin):
    half = ROPE_DIM // 2
    shape = (cos.shape[0],) + (1,) * (t.ndim - 3) + (half,)
    c, s = cos.reshape(shape), sin.reshape(shape)
    t1, t2 = t[..., :half], t[..., half:ROPE_DIM]
    return jnp.concatenate([t1 * c - t2 * s, t2 * c + t1 * s, t[..., ROPE_DIM:]], axis=-1).astype(t.dtype)

def causal_depthwise_conv(u, w, b):
    out = lax.conv_general_dilated(
        u, w[:, None, :].astype(u.dtype), window_strides=(1,), padding=((SSD_CONV - 1, 0),),
        dimension_numbers=("NWC", "WIO", "NWC"), feature_group_count=u.shape[-1])
    return out + b.astype(u.dtype)

def ssd_chunked(xh, dt, a, bm, cm):
    bsz, s, _, p = xh.shape
    nc = s // SSD_CHUNK
    x = (xh * dt[..., None]).reshape(bsz, nc, SSD_CHUNK, SSD_GROUPS, SSD_HPG, p)
    a_dt = (dt * a).reshape(bsz, nc, SSD_CHUNK, SSD_GROUPS, SSD_HPG).transpose(0, 3, 4, 1, 2)
    bc = bm.reshape(bsz, nc, SSD_CHUNK, SSD_GROUPS, SSD_STATE)
    cc = cm.reshape(bsz, nc, SSD_CHUNK, SSD_GROUPS, SSD_STATE)
    a_cum = jnp.cumsum(a_dt, axis=-1)
    causal = jnp.tril(jnp.ones((SSD_CHUNK, SSD_CHUNK), dtype=bool))
    decay = jnp.exp(jnp.where(causal, a_cum[..., :, None] - a_cum[..., None, :], -jnp.inf))
    cb = jnp.einsum("bclgn,bcsgn->bgcls", cc, bc)
    y_diag = jnp.einsum("bgecls,bcsgep->bclgep", cb[:, :, None] * decay, x)
    decay_states = jnp.exp(a_cum[..., -1:] - a_cum).transpose(0, 3, 4, 1, 2)
    states = jnp.einsum("bclgn,bclgep->bcgepn", bc, x * decay_states[..., None])
    chunk_decay = jnp.exp(a_cum[..., -1]).transpose(3, 0, 1, 2)

    def step(h, inp):
        s_c, d_c = inp
        return h * d_c[..., None, None] + s_c, h

    h0 = jnp.zeros((bsz, SSD_GROUPS, SSD_HPG, p, SSD_STATE), x.dtype)
    _, states_in = lax.scan(step, h0, (states.transpose(1, 0, 2, 3, 4, 5), chunk_decay))
    state_decay = jnp.exp(a_cum).transpose(0, 3, 4, 1, 2)[..., None]
    y_off = jnp.einsum("bclgn,cbgepn->bclgep", cc, states_in) * state_decay
    return (y_diag + y_off).reshape(bsz, s, SSD_HEADS, p)

def ssd_mixer(z, xbc, dt_raw, conv_w, conv_b, dt_bias, a_log, d_skip, norm_w):
    bsz, s, _ = z.shape
    f32 = jnp.float32
    xbc = jax.nn.silu(causal_depthwise_conv(xbc, conv_w, conv_b)).astype(f32)
    xs, bm, cm = jnp.split(xbc, [SSD_INNER, SSD_INNER + SSD_GROUPS * SSD_STATE], axis=-1)
    xs = xs.reshape(bsz, s, SSD_HEADS, SSD_HEAD_DIM)
    bm = bm.reshape(bsz, s, SSD_GROUPS, SSD_STATE)
    cm = cm.reshape(bsz, s, SSD_GROUPS, SSD_STATE)
    dt = jax.nn.softplus(dt_raw.astype(f32) + dt_bias.astype(f32))
    a = -jnp.exp(a_log.astype(f32))
    y = ssd_chunked(xs, dt, a, bm, cm) + d_skip.astype(f32)[:, None] * xs
    y = y.reshape(bsz, s, SSD_INNER) * jax.nn.silu(z.astype(f32))
    yg = y.reshape(bsz, s, SSD_GROUPS, SSD_INNER // SSD_GROUPS)
    yg = yg * lax.rsqrt(jnp.mean(yg * yg, axis=-1, keepdims=True) + RMS_EPS)
    return (yg.reshape(bsz, s, SSD_INNER) * norm_w.astype(f32)).astype(z.dtype)

def dilated_window_attention(q, k, v, dilation, steps):
    bsz, s, h, dh = q.shape
    length = s // dilation
    nb = -(-length // ATTN_BLOCK)
    lp = nb * ATTN_BLOCK

    def strided(t):
        t = t.reshape(bsz, length, dilation, h, dh).transpose(0, 2, 3, 1, 4)
        return jnp.pad(t, ((0, 0), (0, 0), (0, 0), (0, lp - length), (0, 0)))

    def banded(t):
        tp = jnp.pad(t, ((0, 0), (0, 0), (0, 0), (ATTN_BLOCK, 0), (0, 0)))
        prev = tp[..., :lp, :].reshape(bsz, dilation, h, nb, ATTN_BLOCK, dh)
        cur = t.reshape(bsz, dilation, h, nb, ATTN_BLOCK, dh)
        return jnp.concatenate([prev, cur], axis=-2)

    qb = strided(q).reshape(bsz, dilation, h, nb, ATTN_BLOCK, dh)
    kb, vb = banded(strided(k)), banded(strided(v))
    scores = jnp.einsum("brhnqe,brhnke->brhnqk", qb, kb, preferred_element_type=jnp.float32) * (dh ** -0.5)
    blk = jnp.arange(nb)[:, None, None]
    qi = jnp.arange(ATTN_BLOCK)[None, :, None] + ATTN_BLOCK
    kj = jnp.arange(2 * ATTN_BLOCK)[None, None, :]
    dist = qi - kj
    mask = (dist >= 0) & (dist <= steps) & (blk * ATTN_BLOCK + kj >= ATTN_BLOCK)
    scores = jnp.where(mask, scores, -jnp.inf)
    lse = jax.nn.logsumexp(scores, axis=-1)
    probs = jnp.exp(scores - lse[..., None])
    out = jnp.einsum("brhnqk,brhnke->brhnqe", probs.astype(v.dtype), vb, preferred_element_type=jnp.float32)

    def unstrided(t):
        tail = t.shape[5:]
        t = t.reshape((bsz, dilation, h, lp) + tail)[:, :, :, :length]
        return jnp.moveaxis(t, 3, 1).reshape((bsz, s, h) + tail)

    return unstrided(out), unstrided(lse)

def dilated_attention_mixer(q, k, v, cos, sin):
    bsz, s, _ = q.shape
    q = apply_partial_rope(q.reshape(bsz, s, ATTN_N_PAT, ATTN_KV_HEADS, ATTN_HEAD_DIM), cos, sin)
    k = apply_partial_rope(k.reshape(bsz, s, ATTN_KV_HEADS, ATTN_HEAD_DIM), cos, sin)
    v = v.reshape(bsz, s, ATTN_KV_HEADS, ATTN_HEAD_DIM)
    outs, lses = [], []
    for g, (window, dilation) in enumerate(ATTN_PATTERNS):
        o, l = dilated_window_attention(q[:, :, g], k, v, dilation, window // dilation)
        outs.append(o)
        lses.append(l)
    weights = jax.nn.softmax(jnp.stack(lses), axis=0)
    o = jnp.sum(weights[..., None] * jnp.stack(outs), axis=0)
    return o.reshape(bsz, s, ATTN_OUT).astype(v.dtype)

def first_inputs(seed: int = 0) -> dict:
    key = jax.random.key(seed)
    ks = jax.random.split(key, 16)
    f32 = jnp.float32

    def dense(k, shape, fan_in):
        return jax.random.normal(k, shape, f32) * fan_in ** -0.5

    def gain(k, shape):
        return 1.0 + 0.02 * jax.random.normal(k, shape, f32)

    dt0 = jnp.exp(jax.random.uniform(ks[5], (DEPTH, SSD_HEADS), f32, math.log(1e-3), math.log(1e-1)))
    return {
        "x": jax.random.normal(ks[0], (BATCH, SEQ, D_MODEL), f32),
        "norm_mix": gain(ks[1], (DEPTH, D_MODEL)),
        "w_in": dense(ks[2], (DEPTH, D_MODEL, N_IN), D_MODEL),
        "conv_w": dense(ks[3], (DEPTH, SSD_CONV, SSD_CONV_CH), SSD_CONV),
        "conv_b": 0.02 * jax.random.normal(ks[4], (DEPTH, SSD_CONV_CH), f32),
        "dt_bias": dt0 + jnp.log(-jnp.expm1(-dt0)),
        "a_log": jnp.log(jax.random.uniform(ks[6], (DEPTH, SSD_HEADS), f32, 1.0, 16.0)),
        "d_skip": gain(ks[7], (DEPTH, SSD_HEADS)),
        "ssd_norm": gain(ks[8], (DEPTH, SSD_INNER)),
        "w_ssd_branch": dense(ks[9], (DEPTH, SSD_INNER, D_MODEL), SSD_INNER),
        "w_attn_branch": dense(ks[10], (DEPTH, ATTN_OUT, D_MODEL), ATTN_OUT),
        "w_out": dense(ks[11], (DEPTH, D_MODEL, D_MODEL), D_MODEL),
        "norm_ffn": gain(ks[12], (DEPTH, D_MODEL)),
        "w_gate_up": dense(ks[13], (DEPTH, D_MODEL, 2 * FFN_HIDDEN), D_MODEL),
        "w_down": dense(ks[14], (DEPTH, FFN_HIDDEN, D_MODEL), FFN_HIDDEN),
        "norm_final": gain(ks[15], (D_MODEL,)),
    }

def first_block(x, norm_mix, w_in, conv_w, conv_b, dt_bias, a_log, d_skip, ssd_norm,
              w_ssd_branch, w_attn_branch, w_out, norm_ffn, w_gate_up, w_down, norm_final):
    cos, sin = rope_tables(x.shape[1])
    h = x
    for layer in range(DEPTH):
        u = rms_norm(h, norm_mix[layer])
        proj = u @ w_in[layer]
        z, xbc, dt_raw, q, k, v, g_ssd, g_attn = jnp.split(proj, IN_SPLITS, axis=-1)
        y_ssd = ssd_mixer(z, xbc, dt_raw, conv_w[layer], conv_b[layer], dt_bias[layer],
                          a_log[layer], d_skip[layer], ssd_norm[layer])
        y_attn = dilated_attention_mixer(q, k, v, cos, sin)
        merged = (jax.nn.sigmoid(g_ssd) * (y_ssd @ w_ssd_branch[layer])
                  + jax.nn.sigmoid(g_attn) * (y_attn @ w_attn_branch[layer]))
        h = h + merged @ w_out[layer]
        u = rms_norm(h, norm_ffn[layer])
        gate, up = jnp.split(u @ w_gate_up[layer], 2, axis=-1)
        h = h + (jax.nn.silu(gate) * up) @ w_down[layer]
    return rms_norm(h, norm_final)


PLE_DIM = 256
MIX_WIDTH = D_MODEL
RET_HEAD_DIM = 128
RET_HEADS = (MIX_WIDTH // 2) // RET_HEAD_DIM
RET_WIDTH = RET_HEADS * RET_HEAD_DIM
MOBA_HEAD_DIM = 128
MOBA_HEADS = (MIX_WIDTH - RET_WIDTH) // MOBA_HEAD_DIM
MOBA_WIDTH = MOBA_HEADS * MOBA_HEAD_DIM
SPLIT_SIZES = [RET_WIDTH] * 4 + [MOBA_WIDTH] * 4
IN_WIDTH = sum(SPLIT_SIZES)
RET_CHUNK = 128
MOBA_BLOCK = 256
MOBA_TOPK = 3
MOBA_Q_CHUNK = 64
N_BUCKETS = 32
MAX_DISTANCE = 2048
ROPE_THETA_2 = 10000.0
EPS = 1e-6
NEG_INF = -1e30


def rms_norm_2(x, g=None):
    xf = x.astype(jnp.float32)
    y = xf * lax.rsqrt(jnp.mean(xf * xf, axis=-1, keepdims=True) + EPS)
    if g is not None:
        y = y * g.astype(jnp.float32)
    return y.astype(x.dtype)

def rotary(x, pos):
    half = x.shape[-1] // 2
    inv = ROPE_THETA_2 ** (-jnp.arange(half, dtype=jnp.float32) / half)
    ang = pos.astype(jnp.float32)[:, None] * inv[None, :]
    cos = jnp.cos(ang)[None, :, None, :]
    sin = jnp.sin(ang)[None, :, None, :]
    x1, x2 = x[..., :half], x[..., half:]
    return jnp.concatenate([x1 * cos - x2 * sin, x1 * sin + x2 * cos], axis=-1)

def t5_bucket(n):
    max_exact = N_BUCKETS // 2
    nf = jnp.maximum(n, 1).astype(jnp.float32)
    large = max_exact + (jnp.log(nf / max_exact) / math.log(MAX_DISTANCE / max_exact)
                         * (N_BUCKETS - max_exact)).astype(jnp.int32)
    large = jnp.minimum(large, N_BUCKETS - 1)
    return jnp.where(n < max_exact, n, large)

def retention(q, k, v, gain):
    B, S, H, d = q.shape
    C = RET_CHUNK
    nc = S // C
    log_g = jnp.log1p(-jnp.power(2.0, -5.0 - jnp.arange(H, dtype=jnp.float32)))

    def chunks(t):
        return t.reshape(B, nc, C, H, d).transpose(0, 3, 1, 2, 4)

    qc, kc, vc = chunks(q), chunks(k * (d ** -0.5)), chunks(v)
    j = jnp.arange(C, dtype=jnp.float32)
    rel = j[:, None] - j[None, :]
    decay = jnp.where(rel >= 0, jnp.exp(log_g[:, None, None] * jnp.maximum(rel, 0.0)[None]), 0.0)
    s = jnp.einsum('bhcnd,bhcmd->bhcnm', qc, kc) * decay[None, :, None]
    inner = jnp.einsum('bhcnm,bhcme->bhcne', s, vc)
    k_dec = kc * jnp.exp(log_g[:, None] * (C - 1 - j)[None])[None, :, None, :, None]
    kv = jnp.einsum('bhcmd,bhcme->cbhde', k_dec, vc)
    chunk_decay = jnp.exp(log_g * C)[None, :, None, None]

    def step(state, kv_c):
        return state * chunk_decay + kv_c, state

    _, prev = lax.scan(step, jnp.zeros((B, H, d, d), jnp.float32), kv)
    q_dec = qc * jnp.exp(log_g[:, None] * (j + 1.0)[None])[None, :, None, :, None]
    cross = jnp.einsum('bhcnd,cbhde->bhcne', q_dec, prev)
    o = (inner + cross).transpose(0, 2, 3, 1, 4).reshape(B, S, H, d)
    mu = jnp.mean(o, axis=-1, keepdims=True)
    var = jnp.mean(jnp.square(o - mu), axis=-1, keepdims=True)
    o = (o - mu) * lax.rsqrt(var + EPS)
    return o.reshape(B, S, H * d) * gain.astype(jnp.float32)

def moba(q, k, v, rel_bias):
    B, S, H, d = q.shape
    BLK, QC = MOBA_BLOCK, MOBA_Q_CHUNK
    nb = -(-S // BLK)
    pad = nb * BLK - S
    q = q.transpose(0, 2, 1, 3) * (d ** -0.5)
    kp = jnp.pad(k.transpose(0, 2, 1, 3), ((0, 0), (0, 0), (0, pad), (0, 0)))
    vp = jnp.pad(v.transpose(0, 2, 1, 3), ((0, 0), (0, 0), (0, pad), (0, 0)))
    kb = kp.reshape(B, H, nb, BLK, d)
    vb = vp.reshape(B, H, nb, BLK, d)
    kmean = jnp.mean(kb, axis=3)

    qpos = jnp.arange(S)
    qblock = qpos // BLK
    gate = jnp.einsum('bhsd,bhnd->bhsn', q, kmean)
    past = jnp.arange(nb)[None, :] < qblock[:, None]
    gate = jnp.where(past[None, None], gate, NEG_INF)
    n_sel = min(MOBA_TOPK, nb)
    _, top_idx = lax.top_k(gate, n_sel)

    nq = S // QC
    qx = q.reshape(B, H, nq, QC, d).transpose(2, 0, 1, 3, 4)
    ix = top_idx.reshape(B, H, nq, QC, n_sel).transpose(2, 0, 1, 3, 4)
    bi = jnp.arange(B)[:, None, None, None]
    hi = jnp.arange(H)[None, :, None, None]
    offs = jnp.arange(BLK)
    bias_h = rel_bias.astype(jnp.float32).T

    def one_chunk(args):
        c, qc, ic = args
        qp = c * QC + jnp.arange(QC)
        qblk = (c * QC) // BLK
        ksel = kb[bi, hi, ic]
        vsel = vb[bi, hi, ic]
        kpos = ic[..., None] * BLK + offs
        dist = qp[None, None, :, None, None] - kpos
        ok = (ic < qblk)[..., None]
        s_sel = (jnp.einsum('bhqd,bhqnkd->bhqnk', qc, ksel)
                 + bias_h[hi[..., None], t5_bucket(jnp.maximum(dist, 0))])
        s_sel = jnp.where(ok, s_sel, NEG_INF).reshape(B, H, QC, n_sel * BLK)
        kown = lax.dynamic_index_in_dim(kb, qblk, axis=2, keepdims=False)
        vown = lax.dynamic_index_in_dim(vb, qblk, axis=2, keepdims=False)
        dist_own = qp[:, None] - (qblk * BLK + offs)[None, :]
        s_own = (jnp.einsum('bhqd,bhkd->bhqk', qc, kown)
                 + bias_h[:, t5_bucket(jnp.maximum(dist_own, 0))][None])
        s_own = jnp.where(dist_own >= 0, s_own, NEG_INF)
        pr = jax.nn.softmax(jnp.concatenate([s_sel, s_own], axis=-1), axis=-1)
        p_sel = pr[..., :n_sel * BLK].reshape(B, H, QC, n_sel, BLK)
        p_own = pr[..., n_sel * BLK:]
        return (jnp.einsum('bhqnk,bhqnkd->bhqd', p_sel, vsel)
                + jnp.einsum('bhqk,bhkd->bhqd', p_own, vown))

    out = lax.map(one_chunk, (jnp.arange(nq), qx, ix))
    return out.transpose(1, 0, 3, 2, 4).reshape(B, S, H * d)

def second_inputs(seed: int = 0) -> dict:
    key = jax.random.key(seed)
    ks = jax.random.split(key, 12)
    f = jnp.float32
    nrm = jax.random.normal
    return {
        "x": nrm(ks[0], (BATCH, SEQ, D_MODEL), f),
        "p": nrm(ks[1], (DEPTH, BATCH, SEQ, PLE_DIM), f),
        "norm_g": 1.0 + 0.02 * nrm(ks[2], (DEPTH, D_MODEL), f),
        "w_in": nrm(ks[3], (DEPTH, D_MODEL, IN_WIDTH), f) * D_MODEL ** -0.5,
        "ret_norm_g": 1.0 + 0.02 * nrm(ks[4], (DEPTH, RET_WIDTH), f),
        "q_norm_g": 1.0 + 0.02 * nrm(ks[5], (DEPTH, MOBA_HEAD_DIM), f),
        "k_norm_g": 1.0 + 0.02 * nrm(ks[6], (DEPTH, MOBA_HEAD_DIM), f),
        "rel_bias": 0.5 * nrm(ks[7], (N_BUCKETS, MOBA_HEADS), f),
        "w_out": nrm(ks[8], (DEPTH, MIX_WIDTH, D_MODEL), f) * MIX_WIDTH ** -0.5,
        "w_ple": nrm(ks[9], (DEPTH, PLE_DIM, D_MODEL), f) * PLE_DIM ** -0.5,
        "ple_norm_g": 1.0 + 0.02 * nrm(ks[10], (DEPTH, D_MODEL), f),
        "w_ple_gate": nrm(ks[11], (DEPTH, D_MODEL, D_MODEL), f) * D_MODEL ** -0.5,
    }

def second_block(x, p, norm_g, w_in, ret_norm_g, q_norm_g, k_norm_g, rel_bias,
              w_out, w_ple, ple_norm_g, w_ple_gate):
    B, S, _ = x.shape
    f32 = jnp.float32
    pos = jnp.arange(S)
    cuts = list(np.cumsum(SPLIT_SIZES)[:-1])

    def heads(t, H):
        return t.astype(f32).reshape(B, S, H, -1)

    for i in range(DEPTH):
        h = rms_norm_2(x, norm_g[i])
        proj = h @ w_in[i]
        rq, rk, rv, rz, mq, mk, mv, mz = jnp.split(proj, cuts, axis=-1)
        r_out = retention(rotary(heads(rq, RET_HEADS), pos), rotary(heads(rk, RET_HEADS), pos),
                          heads(rv, RET_HEADS), ret_norm_g[i])
        r_out = jax.nn.silu(rz.astype(f32)) * r_out
        q_m = rms_norm_2(heads(mq, MOBA_HEADS), q_norm_g[i])
        k_m = rms_norm_2(heads(mk, MOBA_HEADS), k_norm_g[i])
        m_out = moba(q_m, k_m, heads(mv, MOBA_HEADS), rel_bias)
        m_out = jax.nn.silu(mz.astype(f32)) * m_out
        y = jnp.concatenate([r_out, m_out], axis=-1).astype(x.dtype) @ w_out[i]
        x = x + y
        gate = jax.nn.sigmoid((rms_norm_2(x) @ w_ple_gate[i]).astype(f32))
        e = rms_norm_2(p[i] @ w_ple[i], ple_norm_g[i]).astype(f32)
        x = x + (gate * e).astype(x.dtype)
    return x


def setup_inputs(seed=0):
    out = dict(first_inputs(seed))
    for name, value in second_inputs(seed + 1).items():
        if name != "x":
            out[name + "_2"] = value
    return out


def reference(
    x, norm_mix, w_in, conv_w, conv_b, dt_bias, a_log, d_skip, ssd_norm, w_ssd_branch,
    w_attn_branch, w_out, norm_ffn, w_gate_up, w_down, norm_final, p_2, norm_g_2, w_in_2,
    ret_norm_g_2, q_norm_g_2, k_norm_g_2, rel_bias_2, w_out_2, w_ple_2, ple_norm_g_2,
    w_ple_gate_2,
):
    x = first_block(
        x, norm_mix, w_in, conv_w, conv_b, dt_bias, a_log, d_skip, ssd_norm, w_ssd_branch,
        w_attn_branch, w_out, norm_ffn, w_gate_up, w_down, norm_final,
    )
    return second_block(
        x, p_2, norm_g_2, w_in_2, ret_norm_g_2, q_norm_g_2, k_norm_g_2, rel_bias_2, w_out_2,
        w_ple_2, ple_norm_g_2, w_ple_gate_2,
    )


_drawn_inputs = setup_inputs


def setup_inputs(seed=0):
    import zlib

    import numpy as np

    out = dict(_drawn_inputs(seed))
    spreads = {}
    factors = {'d_skip': 4.931,
     'ssd_norm': 2.779,
     'ret_norm_g_2': 5.82,
     'q_norm_g_2': 8.0,
     'k_norm_g_2': 8.0,
     'ple_norm_g_2': 4.488,
     'rel_bias_2': 6.977}
    for name, (base, spread) in spreads.items():
        noise = np.random.default_rng([zlib.crc32(name.encode()), seed]).standard_normal(out[name].shape)
        drawn = base * np.exp(spread * noise) if base else spread * noise
        out[name] = __import__('jax').numpy.asarray(drawn.astype(out[name].dtype))
    for name, factor in factors.items():
        out[name] = (out[name] * factor).astype(out[name].dtype)
    return out
```

```python
from contextlib import ExitStack

import numpy as np

import concourse.bass as bass
from concourse import mybir

F32 = mybir.dt.float32
F32R = mybir.dt.float32r
ALU = mybir.AluOpType
ACT = mybir.ActivationFunctionType
AX = mybir.AxisListType

P = 128
D = 1024
KD = D // P
S = 256
T = S // P
L = 2
INNER, GROUPS, STATE = 2048, 4, 128
HEADS = 32
HPG = HEADS // GROUPS
HD = INNER // HEADS
TAPS = 4
FFN = 2816
KF = FFN // P
EPS1, EPS2 = 1e-5, 1e-6
NEG = -1e30
SCALE = float(P) ** -0.5
PATTERNS = ((128, 1), (512, 4), (2048, 16))
NPAT = len(PATTERNS)
BUCKETS, MAX_DIST = 32, 2048
REV = S + P

RING = 3
CH = 2048
W_COLS = 512

TILES1 = ["B", "C", "x0", "k0", "v0", "x1", "z0", "q0", "x2", "z1", "q2", "x3", "z2", "q4", "z3",
          "gs0", "gs1", "k1", "v1", "q1", "q3", "q5", "ga0", "ga1"]
START1 = {"z": 0, "x": INNER, "B": 2 * INNER, "C": 2 * INNER + 512, "q": 5152, "k": 8224, "v": 9248,
          "gs": 10272, "ga": 11296}
DT_AT = 5120
NT1 = len(TILES1)
SSD_AT = 2 * NT1
ATT_AT = SSD_AT + INNER // 256
OUT_AT = ATT_AT + D // 256
GU_AT = OUT_AT + D // 256
NGU = FFN // 256
DOWN_AT = GU_AT + 2 * NGU
SINGLES = 4
DOWN_FULL = (KF - SINGLES) // 2
CHUNKS1 = DOWN_AT + DOWN_FULL + SINGLES
BLOCKS1 = DOWN_AT + KF // 2
assert CHUNKS1 % RING == 0
FULL1 = DOWN_AT + DOWN_FULL
PAIRED1 = (OUT_AT - 1, GU_AT - 1, CHUNKS1 - 1)

TILES2 = ["rk", "rq", "rv", "mk", "mq", "mv", "rz", "mz"]
START2 = {"rq": 0, "rk": 512, "rv": 1024, "rz": 1536, "mq": 2048, "mk": 2560, "mv": 3072, "mz": 3584}
NT2 = len(TILES2)
PLE_AT = 2 * NT2
SIZE2 = {PLE_AT: D, PLE_AT + 1: 512, PLE_AT + 2: 512}
OUT2_AT = PLE_AT + 3
GATE_AT = OUT2_AT + D // 256
CHUNKS2 = GATE_AT + D // 256
BLOCKS2 = CHUNKS2 - 2
assert CHUNKS2 % RING == 0
PAIRED2 = (GATE_AT - 1, CHUNKS2 - 1)
BASE2 = L * CHUNKS1

C_MIX, C_FFN, C_CW, C_CB, C_SN = 0, 8, 16, 112, 136
C_DTB, C_AL, C_DS, C_WDT = 152, 184, 216, 248
N_PAR1 = C_WDT + KD * HEADS
C_NG, C_YW, C_QN, C_KN, C_PT = 0, 8, 16, 17, 18
N_PAR2 = C_PT + 2 * S
N_PAR = max(N_PAR1, N_PAR2)

K_ID, K_TRI, K_LATER, K_MASK = 0, 128, 256, 384
K_ROPE1 = K_MASK + NPAT * S
K_KDEC = K_ROPE1 + 2 * T * 32
K_HEAD = K_KDEC + 4
N_CONST1 = K_HEAD + HEADS
K_ROPE2 = 0
K_DECAY = K_ROPE2 + 2 * T * P
K_QPOW = K_DECAY + 4 * P
N_CONST2 = K_QPOW + 4 * P

VCH1, SCH1 = 78, 8
VCH2, SCH2 = 23, 5


class Chain:

    def __init__(self, sem):
        self.sem, self.base, self.n = sem, 0, 0

    def start(self, base):
        self.base, self.n = base, 0

    def then(self, eng, ins):
        ins.then_inc(self.sem, 1)
        self.n += 1
        eng.wait_ge(self.sem, self.base + self.n)


class Signal:

    def __init__(self, sem, per):
        self.sem, self.per = sem, per

    def wait(self, eng, layer, n):
        eng.wait_ge(self.sem, layer * self.per + n)


def bc(ap, *shape):
    return ap.to_broadcast([P, *shape])


def build(nc, stream1, stream2, pars, const1, const2, onehot, relb, final_g, ple_g, w_x, out, rev):
    ctx = ExitStack()
    with ctx:
        def sb(name, shape, dt=F32):
            return ctx.enter_context(nc.sbuf_tensor(name, shape, dt))

        def sem(name):
            return ctx.enter_context(nc.semaphore(name))

        W = sb("w_raw", [P, RING, CH])
        WH = sb("w_high", [P, RING, CH], F32R)
        WL = sb("w_low", [P, RING, CH], F32R)
        h = sb("h", [P, T, D])
        uH = sb("u_high", [P, KD, S], F32R)
        uL = sb("u_low", [P, KD, S], F32R)
        b_at = nc.sbuf_base
        bH = sb("b_high", [P, 24, S], F32R)
        bL = sb("b_low", [P, 24, S], F32R)
        con_at = nc.sbuf_base
        con = sb("con", [P, N_CONST1])
        par = sb("par", [P, N_PAR])
        small = sb("small", [P, 1024])
        tri_r = nc.alloc_sbuf_tensor_at("tri_r", [P, P], F32R, offset=con_at + K_TRI * 4)
        later_r = nc.alloc_sbuf_tensor_at("later_r", [P, P], F32R, offset=con_at + K_LATER * 4)
        ident_r = sb("ident_r", [P, P], F32R)
        never_r = sb("never_r", [P, P], F32R)
        dtw_h = sb("dtw_h", [P, KD * HEADS], F32R)
        dtw_l = sb("dtw_l", [P, KD * HEADS], F32R)
        adt_h = sb("adt_h", [P, T * HEADS], F32R)
        adt_l = sb("adt_l", [P, T * HEADS], F32R)
        x_at = nc.sbuf_base
        X = sb("scratch", [P, 16384])
        ps = ctx.enter_context(nc.psum_tensor("ps", [P, 8, 512], F32))

        ident = con[:, K_ID:K_ID + P]
        tri = con[:, K_TRI:K_TRI + P]
        later = con[:, K_LATER:K_LATER + P]
        mask = con[:, K_MASK:K_MASK + NPAT * S].rearrange("p (g k) -> p g k", g=NPAT)
        rope_c = con[:, K_ROPE1:K_ROPE1 + T * 32].rearrange("p (t j) -> p t j", t=T)
        rope_s = con[:, K_ROPE1 + T * 32:K_ROPE1 + 2 * T * 32].rearrange("p (t j) -> p t j", t=T)

        head_of = con[:, K_HEAD:K_HEAD + HEADS]
        at = [0]

        def cut(n, start=None):
            if start is None:
                start, at[0] = at[0], at[0] + n
            return X[:, start:start + n]

        def early(name, part, tile, n, dt=F32):
            at_byte = b_at + (part * 24 + tile) * S * 4
            return nc.alloc_sbuf_tensor_at(name, [P, n], dt, offset=at_byte)

        xpad = early("xpad", 0, 8, 4 * (S + TAPS))[:, :].rearrange("p (j s) -> p j s", j=4)
        xdt = early("xdt", 0, 16, T * 512)[:, :].rearrange("p (t n) -> p t n", t=T)
        conv = early("conv", 0, 20, 4 * S)[:, :].rearrange("p (j s) -> p j s", j=4)
        EM = [early(f"ssd_decay{i}", 1, 16 + 4 * i, HPG * P)[:, :].rearrange("p (e l) -> p e l", e=HPG)
              for i in range(2)]
        DR = early("decay_rows", 1, 12, HPG * P, F32R)

        BC0 = cut(2048)
        BC = BC0.rearrange("p (j s) -> p j s", j=8)
        gate_s = BC0.rearrange("p (t n) -> p t n", t=T)
        Y0 = cut(2048)
        Y = [Y0[:, i * 1024:(i + 1) * 1024].rearrange("p (t n) -> p t n", t=T) for i in range(2)]
        gate_a = Y0.rearrange("p (t n) -> p t n", t=T)
        btok = cut(512).rearrange("p (g n) -> p g n", g=GROUPS)
        state = cut(512)
        xds = cut(512)
        yoff = cut(512)
        Q0 = cut(3072)
        qT = Q0.rearrange("p (g h s) -> p g h s", g=NPAT, h=4)
        sg = Q0[:, 0:1024].rearrange("p (i t n) -> p i t n", i=2, t=T)
        ac = Q0[:, 1024:2048].rearrange("p (i t n) -> p i t n", i=2, t=T)
        rev_rows = Q0[:, 0:4 * REV].rearrange("p (h j) -> p h j", h=4)
        E_AT = at[0]
        E0 = cut(1536)
        dtT = E0[:, 1024:1280]
        cumT = E0[:, 1024:1024 + P]
        cum_hl = nc.alloc_sbuf_tensor_at("cum_high_low", [P, T, 2 * HEADS], F32R, offset=x_at + (E_AT + 1280) * 4)
        sc1, sc0 = E0[:, 0:768], E0[:, 768:1152]
        pT = E0[:, 1152:1536]
        V0 = cut(2048)
        ev = [V0[:, i * 1024:(i + 1) * 1024].rearrange("p (t n) -> p t n", t=T) for i in range(2)]
        ev.append(Y[0])
        colsF = V0.rearrange("p (j n) -> p j n", j=4)
        R0 = cut(2048)
        rows = R0.rearrange("p (t n) -> p t n", t=T)
        kT = R0[:, 0:1024].rearrange("p (h s) -> p h s", h=4)
        M0 = cut(1024)
        vv = [R0[:, 1024:2048].rearrange("p (t n) -> p t n", t=T),
              M0.rearrange("p (t n) -> p t n", t=T)]
        cbm = M0.rearrange("p (t g l) -> p t g l", t=T, g=GROUPS)
        rope_a = cut(256).rearrange("p (t h j) -> p t h j", t=T, h=4)
        rope_b = cut(256).rearrange("p (t h j) -> p t h j", t=T, h=4)
        used1 = at[0]

        at[0] = 0
        c2 = cut(N_CONST2)
        rot_c = c2[:, K_ROPE2:K_ROPE2 + T * P].rearrange("p (t j) -> p t j", t=T)
        rot_s = c2[:, K_ROPE2 + T * P:K_ROPE2 + 2 * T * P].rearrange("p (t j) -> p t j", t=T)
        decay = c2[:, K_DECAY:K_DECAY + 4 * P].rearrange("p (h n) -> p h n", h=4)
        qpow = c2[:, K_QPOW:K_QPOW + 4 * P].rearrange("p (h n) -> p h n", h=4)
        kdec_c = con[:, K_KDEC:K_KDEC + 4]
        bias = cut(4 * S).rearrange("p (h k) -> p h k", h=4)
        RK0 = cut(2048)
        rkT = RK0[:, 0:1024].rearrange("p (h s) -> p h s", h=4)
        rqT = RK0[:, 1024:2048].rearrange("p (h s) -> p h s", h=4)
        emb = RK0.rearrange("p (t n) -> p t n", t=T)
        mkT = cut(1024).rearrange("p (h s) -> p h s", h=4)
        mqT = cut(1024).rearrange("p (h s) -> p h s", h=4)
        rv = cut(1024).rearrange("p (t n) -> p t n", t=T)
        mv = cut(1024).rearrange("p (t n) -> p t n", t=T)
        kdec = cut(512)
        qdT = cut(512).rearrange("p (h n) -> p h n", h=4)
        kvs = cut(512).rearrange("p (h n) -> p h n", h=4)
        sT = cut(1024).rearrange("p (t h n) -> p t h n", t=T, h=4)
        V2 = cut(2048)
        ev2 = [V2[:, i * 1024:(i + 1) * 1024].rearrange("p (t n) -> p t n", t=T) for i in range(2)]
        cols2 = V2.rearrange("p (j n) -> p j n", j=4)
        rt = cut(1024).rearrange("p (t n) -> p t n", t=T)
        rows2 = cut(2048).rearrange("p (t n) -> p t n", t=T)
        msc = early("block_scores", 0, 4, 4 * (S + P))
        msc1 = msc[:, 0:4 * S].rearrange("p (h k) -> p h k", h=4)
        msc0 = msc[:, 4 * S:4 * (S + P)].rearrange("p (h k) -> p h k", h=4)
        mpT = early("block_probs_t", 0, 10, 4 * (S + P))
        mpT1 = mpT[:, 0:4 * S].rearrange("p (h k) -> p h k", h=4)
        mpT0 = mpT[:, 4 * S:4 * (S + P)].rearrange("p (h k) -> p h k", h=4)
        sg2 = early("embed_gate", 0, 16, T * D)[:, :].rearrange("p (t n) -> p t n", t=T)
        ple_gain = early("ple_gain", 1, 4, D)[:, :]
        sq = early("squares", 1, 8, T * D)[:, :].rearrange("p (t n) -> p t n", t=T)
        assert max(used1, at[0]) <= 16384, (used1, at[0])

        sat = [0]

        def tiny(n):
            sat[0] += n
            return small[:, sat[0] - n:sat[0]]

        eps1, eps2 = tiny(1), tiny(1)
        ssum = tiny(T)
        rinv = tiny(T)
        gsum = tiny(T)
        ginv = tiny(T)
        dt = tiny(T * HEADS)
        dtx, dta, dte, dtu, dtd, dtz, dtl = (tiny(T * HEADS) for _ in range(7))
        nega = tiny(HEADS)
        adt = tiny(T * HEADS)
        acum = tiny(3 * HEADS)
        nacum = tiny(T * HEADS)
        spare = tiny(8)
        dec_in = tiny(HEADS)
        dec_out = tiny(HEADS)
        amax = tiny(T)
        anb = tiny(T)
        az = tiny(T)
        azi = tiny(T)
        head_ss = [tiny(T * 4) for _ in range(3)]
        head_mean = tiny(T * 4)
        mmax, mneg, mz = tiny(T * 4), tiny(T * 4), tiny(T * 4)
        ple_ss = tiny(T)
        assert sat[0] <= 1024

        w_loaded = [sem(f"w_loaded{i}") for i in range(RING)]
        high_ready = sem("high_ready")
        split_done = sem("split_done")
        products_done = sem("products_done")


        def signal(name, per):
            return Signal(sem(name), per)

        cols_ps = signal("cols_ps", 12)
        dtt_ps = signal("dtt_ps", 1)
        dt_ps = signal("dt_ps", 1)
        cumt_ps = signal("cumt_ps", 1)
        cum_ps = signal("cum_ps", 1)
        btok_ps = signal("btok_ps", 1)
        cb_ps = signal("cb_ps", 1)
        xt_ps = signal("xt_ps", GROUPS)
        row_ps = signal("row_ps", 2 * GROUPS)
        state_ps = signal("state_ps", GROUPS)
        yd_ps = signal("yd_ps", 2 * GROUPS)
        off_ps = signal("off_ps", GROUPS)
        yt_ps = signal("yt_ps", 2 * GROUPS)
        qk_ps = signal("qk_ps", 8)
        score_ps = signal("score_ps", 8)
        pt_ps = signal("pt_ps", 8)
        o_ps = signal("o_ps", 8)
        act_ps = signal("act_ps", NGU)
        t0_done = signal("t0_done", 4)
        tile_out = signal("tile_out", NT1)
        cols_high = signal("cols_high", 12)
        roots = signal("roots", 4)
        conv_act = signal("conv_act", 6)
        dt_steps = signal("dt_steps", 2)
        dtt_out = signal("dtt_out", 1)
        cumt_out = signal("cumt_out", 1)
        btok_out = signal("btok_out", 1)
        decays = signal("decays", 1)
        ssd_exp = signal("ssd_exp", 2 * GROUPS)
        state_out = signal("state_out", GROUPS)
        group_root = signal("group_root", GROUPS)
        y_high = signal("y_high", 2 * GROUPS)
        qk_out = signal("qk_out", 8)
        att_exp = signal("att_exp", 8)
        pt_out = signal("pt_out", 8)
        o_high = signal("o_high", 8)
        gate_act = signal("gate_act", NGU)
        act_high = signal("act_high", NGU)
        set_up = sem("set_up")
        h_ready = signal("h_ready", 4)
        rows_ready = signal("rows_ready", 6)
        cols_weighted = signal("cols_weighted", 8)
        cols_ready = signal("cols_ready", 12)
        dtw_ready = signal("dtw_ready", 1)
        dt_given = signal("dt_given", 2)
        adt_ready = signal("adt_ready", 1)
        cum_out = signal("cum_out", 1)
        cb_masked = signal("cb_masked", 1)
        xdt_ready = signal("xdt_ready", GROUPS)
        ssd_m = signal("ssd_m", 2 * GROUPS)
        ssd_y = signal("ssd_y", 2 * GROUPS)
        y_scaled = signal("y_scaled", GROUPS)
        y_weighted = signal("y_weighted", 2 * GROUPS)
        conv_done = signal("conv_done", 6)
        y_ready = signal("y_ready", 2 * GROUPS)
        roped = signal("roped", 8)
        att_masked = signal("att_masked", 8)
        att_p = signal("att_p", 8)
        o_ready = signal("o_ready", 8)
        ssd_gated = signal("ssd_gated", T)
        act_ready = signal("act_ready", NGU)
        act_rows = signal("act_rows", NGU)
        decay_rows = signal("decay_rows", GROUPS)
        xds_ready = signal("xds_ready", GROUPS)
        y_gated = signal("y_gated", GROUPS)
        cols2_ps = signal("cols2_ps", 12)
        ret_t_ps = signal("ret_t_ps", 2)
        kv_ps = signal("kv_ps", 1)
        s_ps = signal("s_ps", 1)
        inner_ps = signal("inner_ps", 1)
        mo_t_ps = signal("mo_t_ps", 2)
        msc_ps = signal("msc_ps", 1)
        mpt_ps = signal("mpt_ps", 1)
        mo_ps = signal("mo_ps", 1)
        t0_done2 = signal("t0_done2", 2)
        final_root = sem("final_root")
        tile2_out = signal("tile2_out", NT2)
        cols2_high = signal("cols2_high", 12)
        roots2 = signal("roots2", 4)
        ret_t_out = signal("ret_t_out", 2)
        kv_out = signal("kv_out", 1)
        ret_squared = signal("ret_squared", 1)
        head_root = signal("head_root", 3)
        m_exp = signal("m_exp", 1)
        mpt_out = signal("mpt_out", 1)
        emb_out = signal("emb_out", T)
        ple_root = signal("ple_root", 1)
        gate2_out = signal("gate2_out", T)
        h2_ready = signal("h2_ready", 4)
        rows2_ready = signal("rows2_ready", 6)
        cols2_weighted = signal("cols2_weighted", 8)
        cols2_ready = signal("cols2_ready", 12)
        ple_split = signal("ple_split", 1)
        rotated = signal("rotated", 2)
        s_decayed = signal("s_decayed", 1)
        head_sum = signal("head_sum", 3)
        normed = signal("normed", 3)
        mo_t_out = signal("mo_t_out", 2)
        centred = signal("centred", 1)
        m_masked = signal("m_masked", 1)
        emb_ready = signal("emb_ready", 1)
        kdec_ready = signal("kdec_ready", 1)
        qd_ready = signal("qd_ready", 1)
        ret_gated = signal("ret_gated", 1)
        final_loaded = sem("final_loaded")
        tables_loaded = sem("tables_loaded")
        gain_loaded = sem("gain_loaded")
        par_loaded = sem("par_loaded")
        con_loaded = sem("con_loaded")
        late_loaded = sem("late_loaded")
        rev_stored = sem("rev_stored")
        stored = sem("stored")
        rev_steps = sem("rev_steps")
        vector_chain, scalar_chain = Chain(sem("vector_chain")), Chain(sem("scalar_chain"))

        block = ctx.enter_context(nc.Block())

        XT = (2, 5, 8, 11)
        ZT = (6, 9, 12, 14)
        QK = (("k0", 3, 1, 15), ("q0", 7, 1, 21), ("q2", 10, 1, 27), ("q4", 13, 1, 33),
              ("k1", 17, 1, 44), ("q1", 19, 0, 46), ("q3", 20, 2, 46), ("q5", 21, 1, 47))
        QK_BANK = (6, 6, 6, 6, 4, 6, 4, 6)
        QK_OUT = (17, 23, 29, 35, 46, 48, 48, 49)
        CONV_AT = 4
        HEAD_AT = (36, 38, 40, 42, 48, 50, 52, 54)
        assert [TILES1.index(q[0]) for q in QK] == [q[1] for q in QK]
        assert all(TILES1[i] == f"x{g}" for g, i in enumerate(XT)) and all(TILES1[i] == f"z{g}" for g, i in enumerate(ZT))

        def tok(t):
            return slice(t * P, (t + 1) * P)

        def four(ap):
            return ap.rearrange("p (j n) -> p j n", j=4)

        @block.sync
        def _(sp):
            sp.dma_start(h[:, :, :], w_x.rearrange("(t p) n -> p t n", p=P)).then_inc(con_loaded, 16)
            sp.dma_start(con[:, :], const1).then_inc(late_loaded, 16)
            sp.dma_start(par[:, :], pars[0:P, :]).then_inc(par_loaded, 16)
            sp.dma_start(R0[0:BUCKETS + 1, 0:REV], onehot).then_inc(rev_stored, 16)
            sp.dma_start(M0[0:BUCKETS + 1, 0:4], relb).then_inc(rev_steps, 16)

            def load(idx, slot, src, n):
                sp.wait_ge(split_done, idx + 1)
                sp.dma_start(W[:, slot, 0:n], src).then_inc(w_loaded[slot], 16)

            with sp.Fori(0, L) as l:
                with sp.Fori(0, 23) as r:
                    for j in range(RING):
                        load(l * CHUNKS1 + r * RING + j, j,
                             stream1[bass.ds((l * BLOCKS1 + r * RING + j) * P, P), :], CH)
                cols_weighted.wait(sp, l, 8)
                sp.dma_start(par[:, :], pars[bass.ds((l + 1) * P, P), :]).then_inc(par_loaded, 16)
                with sp.Fori(0, 8) as r:
                    for j in range(RING):
                        load(l * CHUNKS1 + 69 + r * RING + j, j,
                             stream1[bass.ds((l * BLOCKS1 + 69 + r * RING + j) * P, P), :], CH)
                for c in range(93, CHUNKS1):
                    half = max(0, c - FULL1)
                    b, n, off = (c, CH, 0) if c < FULL1 else (FULL1 + half // 2, D, half % 2 * D)
                    load(l * CHUNKS1 + c, c % RING,
                         stream1[bass.ds((l * BLOCKS1 + b) * P, P), off:off + n], n)
            rows_ready.wait(sp, L - 1, 4)
            sp.dma_start(M0, final_g).then_inc(final_loaded, 16)
            sp.dma_start(c2, const2).then_inc(tables_loaded, 16)
            sp.wait_ge(rev_stored, 32)
            sp.dma_start(bias, bass.AP(rev.tensor, P - 1, [[4 * REV - 1, P], [REV, 4], [1, S]])).then_inc(tables_loaded, 16)
            with sp.Fori(0, L) as l:
                with sp.Fori(0, PLE_AT // RING) as r:
                    for j in range(RING):
                        load(l * CHUNKS2 + BASE2 + r * RING + j, j,
                             stream2[bass.ds((l * BLOCKS2 + r * RING + j) * P, P), :], CH)
                for c in range(PLE_AT // RING * RING, CHUNKS2):
                    n = SIZE2.get(c, CH)
                    b, off = (c, 0) if c <= PLE_AT else (PLE_AT, D + (c - PLE_AT - 1) * 512) if c in SIZE2 else (c - 2, 0)
                    load(l * CHUNKS2 + BASE2 + c, c % RING,
                         stream2[bass.ds((l * BLOCKS2 + b) * P, P), off:off + n], n)
                    if c == GATE_AT + 1:
                        cols2_weighted.wait(sp, l, 8)
                        sp.dma_start(par[:, :], pars[bass.ds((l + L + 1) * P, P), :]).then_inc(par_loaded, 16)
            for t in range(T):
                h2_ready.wait(sp, L, t + 1)
                sp.dma_start(out[t * P:(t + 1) * P, :], h[:, t, :]).then_inc(stored, 16)
            sp.wait_ge(par_loaded, (2 * L + 1) * 16)
            sp.wait_ge(stored, T * 16)

        @block.tensor
        def _(pe):
            def products(o, hi, lo, whi, wlo, start, stop, **kw):
                nc.tensor.matmul(o, hi, whi, start=start, stop=False, **kw)
                nc.tensor.matmul(o, hi, wlo, start=False, stop=False, **kw)
                return nc.tensor.matmul(o, lo, whi, start=False, stop=stop, **kw)

            def turn(o, i):
                return nc.tensor.transpose(o, i, ident)

            pe.wait_ge(late_loaded, 16)
            pe.wait_ge(rev_stored, 16)
            pe.wait_ge(rev_steps, 16)
            for hh in range(4):
                last = nc.tensor.matmul(ps[:, hh, 0:REV], M0[0:BUCKETS + 1, hh:hh + 1].to_broadcast([BUCKETS + 1, P]),
                                        R0[0:BUCKETS + 1, 0:REV], start=True, stop=True)
            last.then_inc(rev_steps, 1)
            pe.wait_ge(set_up, 1)

            def rows_to_cols(l, n, src):
                for t in range(T):
                    rows_ready.wait(pe, l, 2 * n + t + 1)
                    for q in range(2):
                        for j in range(4):
                            last = turn(ps[:, 4 + 2 * t + q, tok(j)], src[:, t, tok(4 * q + j)])
                        last.then_inc(cols_ps.sem, 1)

            def before(l, c):
                if c == 0:
                    rows_to_cols(l, 0, rows)
                    dtw_ready.wait(pe, l, 1)
                    cols_ready.wait(pe, l, 4)
                    for k in range(KD):
                        w = slice(k * HEADS, (k + 1) * HEADS)
                        last = products(ps[0:HEADS, 4, 0:S], dtw_h[:, w], dtw_l[:, w], uH[:, k, :], uL[:, k, :],
                                        k == 0, k == KD - 1)
                    last.then_inc(dtt_ps.sem, 1)
                if c == 1:
                    dtt_out.wait(pe, l, 1)
                    for t in range(T):
                        last = nc.tensor.matmul(ps[:, 5, t * HEADS:(t + 1) * HEADS], dtT[0:HEADS, tok(t)],
                                                ident[0:HEADS, 0:HEADS], start=True, stop=True)
                    last.then_inc(dt_ps.sem, 1)
                if c == 3:
                    adt_ready.wait(pe, l, 1)
                    for i, (m, t) in enumerate(((tri_r, 0), (tri_r, 1), (later_r, 0))):
                        o, a = ps[:, 5, i * HEADS:(i + 1) * HEADS], slice(t * HEADS, (t + 1) * HEADS)
                        nc.tensor.matmul(o, m[:, :], adt_h[:, a], start=True, stop=False)
                        last = nc.tensor.matmul(o, m[:, :], adt_l[:, a], start=False, stop=True)
                    last.then_inc(cum_ps.sem, 1)
                if c == 6:
                    cum_out.wait(pe, l, 1)
                    turn(ps[:, 5, 0:P], cum_hl[:, :, :].rearrange("p t n -> p (t n)").bitcast(F32)).then_inc(cumt_ps.sem, 1)
                if c == 8:
                    conv_act.wait(pe, l, 2)
                    dt_given.wait(pe, l, 1)
                    for g in range(GROUPS):
                        last = turn(ps[:, 4, tok(g)], BC[:, g, tok(0)])
                    last.then_inc(btok_ps.sem, 1)
                    for t in range(T):
                        for g in range(GROUPS):
                            last = nc.tensor.matmul(ps[:, 6 + t, tok(g)], BC[:, g, tok(t)], BC[:, 4 + g, tok(t)],
                                                    start=True, stop=True)
                    last.then_inc(cb_ps.sem, 1)
                for g, i in enumerate(XT):
                    if c == 2 * i + 5:
                        conv_act.wait(pe, l, 3 + g)
                        if g == 0:
                            btok_out.wait(pe, l, 1)
                            cumt_out.wait(pe, l, 1)
                        else:
                            ssd_y.wait(pe, l, 2 * g)
                        for t in range(T):
                            for j in range(4):
                                last = turn(ps[:, 4 + t, tok(j)], conv[:, j, tok(t)])
                        last.then_inc(xt_ps.sem, 1)
                    for t, at_c in ((0, 2 * i + 6), (1, 2 * i + 8)):
                        if c == at_c:
                            if t == 1:
                                state_out.wait(pe, l, g + 1)
                            elif g == 0:
                                cb_masked.wait(pe, l, 1)
                            else:
                                ssd_y.wait(pe, l, 2 * g)
                                qk_out.wait(pe, l, g)
                            decay_rows.wait(pe, l, g + 1)
                            k = slice(t * 2 * HEADS, (t + 1) * 2 * HEADS)
                            ones = tri_r[k, P - 1:P].to_broadcast([2 * HEADS, P])
                            for b in range(2):
                                nc.tensor.matmul(four(ps[:, 6 + b, :]), ident_r[:, :], bc(never_r[:, :].unsqueeze(1), 4, P),
                                                 start=True, stop=False)
                                last = nc.tensor.matmul(ps[:, 6 + b, :], ones, DR[k, b * 512:(b + 1) * 512],
                                                        start=False, stop=True)
                            last.then_inc(row_ps.sem, 1)
                    if c == 2 * i + 7:
                        xds_ready.wait(pe, l, g + 1)
                        ssd_exp.wait(pe, l, 2 * g + 1)
                        nc.tensor.matmul(ps[:, 6, :], btok[:, g, :], xds, start=True, stop=True).then_inc(state_ps.sem, 1)
                for g, i in enumerate(XT):
                    if c == 2 * i + 13:
                        y_scaled.wait(pe, l, g + 1)
                        if g < GROUPS - 1:
                            xdt_ready.wait(pe, l, g + 2)
                        else:
                            ssd_y.wait(pe, l, 2 * GROUPS)
                        for t in range(T):
                            for j in range(4):
                                last = turn(ps[:, 4 + t, tok(j)], Y[g % 2][:, t, tok(j)])
                            last.then_inc(yt_ps.sem, 1)
                for g, i in enumerate(XT):
                    for t, at_c in ((0, 2 * i + 9), (1, 2 * i + 10)):
                        if c == at_c:
                            ssd_m.wait(pe, l, 2 * g + t + 1)
                            if g:
                                y_weighted.wait(pe, l, 2 * g)
                            for e in range(HPG):
                                last = nc.tensor.matmul(ps[:, 4 + t, e * HD:(e + 1) * HD], EM[t][:, e, :],
                                                        xdt[:, t, e * HD:(e + 1) * HD], start=True, stop=True)
                            last.then_inc(yd_ps.sem, 1)
                    if c == 2 * i + 10:
                        ssd_exp.wait(pe, l, 2 * g + 2)
                        nc.tensor.matmul(ps[:, 7, :], BC[:, 4 + g, tok(1)], state, start=True, stop=True).then_inc(off_ps.sem, 1)
                for n, (name, i, e, at_c) in enumerate(QK):
                    if c == at_c:
                        roped.wait(pe, l, n + 1)
                        b = QK_BANK[n]
                        if n < 4:
                            ssd_y.wait(pe, l, 2 * n + 2)
                        elif n == 4:
                            att_masked.wait(pe, l, 4)
                        elif n == 5:
                            o_ready.wait(pe, l, 4)
                        else:
                            qk_out.wait(pe, l, n - 1)
                        for hh in range(4):
                            for t in range(T):
                                last = turn(ps[:, b + hh // 2, (hh % 2) * S + t * P:(hh % 2) * S + (t + 1) * P],
                                            ev[e][:, t, tok(hh)])
                        last.then_inc(qk_ps.sem, 1)
                for n, s in enumerate(HEAD_AT):
                    hh = n % 4
                    if c == s:
                        qk_out.wait(pe, l, 4 if n < 4 else 8)
                        if n == 0:
                            y_weighted.wait(pe, l, 2 * GROUPS)
                        else:
                            att_masked.wait(pe, l, n)
                        if n >= 2:
                            o_ready.wait(pe, l, n - 1)
                        for g in range(NPAT):
                            nc.tensor.matmul(ps[:, 4 + g // 2, (g % 2) * S:(g % 2 + 1) * S], qT[:, g, hh, tok(1)],
                                             kT[:, hh, :], start=True, stop=True)
                            last = nc.tensor.matmul(ps[:, 6, tok(g)], qT[:, g, hh, tok(0)], kT[:, hh, tok(0)],
                                                    start=True, stop=True)
                        last.then_inc(score_ps.sem, 1)
                for n, s in enumerate(HEAD_AT):
                    hh = n % 4
                    if c == s + 2:
                        att_p.wait(pe, l, n + 1)
                        if n:
                            pt_out.wait(pe, l, n)
                        turn(ps[:, 7, tok(0)], sc0[:, tok(0)])
                        turn(ps[:, 7, tok(1)], sc1[:, tok(0)])
                        turn(ps[:, 7, tok(2)], sc1[:, tok(1)]).then_inc(pt_ps.sem, 1)
                    if c == s + 3:
                        pt_out.wait(pe, l, n + 1)
                        if hh < 3:
                            att_masked.wait(pe, l, n + 2)
                        elif n:
                            o_ready.wait(pe, l, n)
                        nc.tensor.matmul(ps[:, 6, 0:S], vv[n // 4][:, 0, tok(hh)], pT[:, 0:S], start=True, stop=False)
                        nc.tensor.matmul(ps[:, 6, P:S], vv[n // 4][:, 1, tok(hh)], pT[:, S:S + P], start=False,
                                         stop=True).then_inc(o_ps.sem, 1)
                if c == OUT_AT:
                    rows_to_cols(l, 1, rows)
                if c == GU_AT:
                    rows_to_cols(l, 2, rows)
                for j in range(NGU):
                    if c == GU_AT + 2 * j + 4:
                        act_rows.wait(pe, l, j + 1)
                        if j >= 2:
                            act_ready.wait(pe, l, j - 1)
                        for i in range(2):
                            for t in range(T):
                                last = turn(ps[:, 4 + j % 2, i * S + t * P:i * S + (t + 1) * P], ac[:, j % 2, t, tok(i)])
                        last.then_inc(act_ps.sem, 1)

            def by_rows(parts, banks, hi, lo, first, last_k, wait_for, t0_done):
                for t in range(T):
                    for slot, ks in parts:
                        wait_for(t, ks)
                        for half in range(2):
                            for kk, k in enumerate(ks):
                                w = slice(kk * D + half * 512, kk * D + half * 512 + 512)
                                last = products(ps[:, banks[2 * t + half], :], hi[:, k, tok(t)], lo[:, k, tok(t)],
                                                WH[:, slot, w], WL[:, slot, w], k == first, k == last_k)
                    if t == 0 and ks[-1] == last_k:
                        last.then_inc(t0_done.sem, 1)
                last.then_inc(products_done, len(parts))

            def tiles_of(c):
                if c < ATT_AT:
                    return 2 * (c - SSD_AT), 2 * (c - SSD_AT) + 1
                if c < OUT_AT:
                    return 16 + 2 * (c - ATT_AT), 17 + 2 * (c - ATT_AT)
                if c < GU_AT:
                    return 2 * (c - OUT_AT), 2 * (c - OUT_AT) + 1
                if c < FULL1:
                    return 2 * (c - DOWN_AT), 2 * (c - DOWN_AT) + 1
                return (2 * DOWN_FULL + c - FULL1,)

            def chunk(l, c):
                slot = c % RING
                if c + 1 in PAIRED1:
                    return
                parts = [(x % RING, tiles_of(x)) for x in ((c - 1, c) if c in PAIRED1 else (c,))] if c >= SSD_AT else None
                pe.wait_ge(split_done, l * CHUNKS1 + c + 1 + RING)
                if c < SSD_AT:
                    i, half = c // 2, c % 2
                    if i >= 2 and half == 0:
                        tile_out.wait(pe, l, i - 1)
                    if c == 0:
                        cols_ready.wait(pe, l, 4)
                    b = 2 * (i % 2)
                    if TILES1[i][0] in "xBC":
                        for j in range(4):
                            for k in range(4):
                                w = slice(k * W_COLS + j * P, k * W_COLS + (j + 1) * P)
                                kk = 4 * half + k
                                o = ps[:, b + j // 2, (j % 2) * S:(j % 2 + 1) * S]
                                first = kk == 0 and j % 2 == 0
                                nc.tensor.matmul(o, WH[:, slot, w], uH[:, kk, :], start=first, stop=False, skip_group_check=True)
                                nc.tensor.matmul(o, WH[:, slot, w], uL[:, kk, :], start=False, stop=False, skip_group_check=True)
                                last = nc.tensor.matmul(o, WL[:, slot, w], uH[:, kk, :], start=False, stop=kk == KD - 1,
                                                        skip_group_check=True)
                    else:
                        for t in range(T):
                            for k in range(4):
                                w = slice(k * W_COLS, (k + 1) * W_COLS)
                                kk = 4 * half + k
                                last = products(ps[:, b + t, :], uH[:, kk, tok(t)], uL[:, kk, tok(t)], WH[:, slot, w],
                                                WL[:, slot, w], kk == 0, kk == KD - 1)
                elif c < ATT_AT:
                    def wait_for(t, ks):
                        if ks[0] == 0:
                            tile_out.wait(pe, l, NT1 - 1 + t)
                        y_ready.wait(pe, l, 2 * (ks[0] // 4) + t + 1)
                    by_rows(parts, (0, 1, 2, 3), bH, bL, 0, 15, wait_for, t0_done)
                elif c < OUT_AT:
                    def wait_for(t, ks):
                        if ks[0] == 16:
                            ssd_gated.wait(pe, l, t + 1)
                        o_ready.wait(pe, l, ks[1] - 15)
                    by_rows(parts, (0, 1, 2, 3), bH, bL, 16, 23, wait_for, t0_done)
                elif c < GU_AT:
                    def wait_for(t, ks):
                        cols_ready.wait(pe, l, 4 + 2 * t + ks[0] // 4 + 1)
                    by_rows(parts, (0, 1, 2, 3), uH, uL, 0, 7, wait_for, t0_done)
                elif c < DOWN_AT:
                    j, half = (c - GU_AT) // 2, (c - GU_AT) % 2
                    b = 2 * (j % 2)
                    if j >= 2 and half == 0:
                        act_rows.wait(pe, l, j - 1)
                    for t in range(T):
                        if c == GU_AT:
                            cols_ready.wait(pe, l, 10 + 2 * t)
                        for k in range(4):
                            w = slice(k * W_COLS, (k + 1) * W_COLS)
                            kk = 4 * half + k
                            last = products(ps[:, b + t, :], uH[:, kk, tok(t)], uL[:, kk, tok(t)], WH[:, slot, w],
                                            WL[:, slot, w], kk == 0, kk == KD - 1)
                else:
                    def wait_for(t, ks):
                        if c == DOWN_AT and t == 1:
                            act_rows.wait(pe, l, NGU - 1)
                        act_ready.wait(pe, l, ks[-1] // 2 + 1)
                    by_rows(parts, (6, 7, 2, 3), bH, bL, 0, KF - 1, wait_for, t0_done)
                if c < SSD_AT or GU_AT <= c < DOWN_AT:
                    last.then_inc(products_done, 1)

            with pe.Fori(0, L) as l:
                for c in range(CHUNKS1):
                    before(l, c)
                    chunk(l, c)

            def heads_to_cols(o, src):
                for hh in range(4):
                    for t in range(T):
                        last = turn(ps[:, o + hh // 2, (hh % 2) * S + t * P:(hh % 2) * S + (t + 1) * P], src[:, t, tok(hh)])
                return last

            def rows2_to_cols(l, n):
                for t in range(T):
                    if n == 1:
                        rows2_ready.wait(pe, l, 4)
                        ret_gated.wait(pe, l, 1)
                    else:
                        rows2_ready.wait(pe, l, 2 * n + t + 1)
                    for q in range(2):
                        for j in range(4):
                            last = turn(ps[:, 4 + 2 * t + q, tok(j)], rows2[:, t, tok(4 * q + j)])
                        last.then_inc(cols2_ps.sem, 1)

            def before2(l, c):
                if c == 0:
                    rows2_to_cols(l, 0)
                if c == 5:
                    rotated.wait(pe, l, 1)
                    heads_to_cols(4, ev2[0]).then_inc(ret_t_ps.sem, 1)
                if c == 7:
                    rotated.wait(pe, l, 2)
                    heads_to_cols(6, ev2[1]).then_inc(ret_t_ps.sem, 1)
                if c == 9:
                    kdec_ready.wait(pe, l, 1)
                    ret_t_out.wait(pe, l, 1)
                    tile2_out.wait(pe, l, 3)
                    for hh in range(4):
                        last = nc.tensor.matmul(ps[:, 4, tok(hh)], kdec[:, tok(hh)], rv[:, 0, tok(hh)], start=True, stop=True)
                    last.then_inc(kv_ps.sem, 1)
                if c == 10:
                    ret_t_out.wait(pe, l, 2)
                    for t in range(T):
                        for hh in range(4):
                            last = nc.tensor.matmul(ps[:, 6 + t, tok(hh)], rkT[:, hh, tok(t)], rqT[:, hh, tok(t)],
                                                    start=True, stop=True)
                    last.then_inc(s_ps.sem, 1)
                if c == 11:
                    normed.wait(pe, l, 1)
                    kv_out.wait(pe, l, 1)
                    heads_to_cols(4, ev2[1]).then_inc(mo_t_ps.sem, 1)
                if c == 12:
                    normed.wait(pe, l, 2)
                    s_decayed.wait(pe, l, 1)
                    heads_to_cols(6, ev2[0]).then_inc(mo_t_ps.sem, 1)
                if c == 13:
                    mo_t_out.wait(pe, l, 1)
                    qd_ready.wait(pe, l, 1)
                    for hh in range(4):
                        nc.tensor.matmul(ps[:, 4, tok(hh)], sT[:, 0, hh, :], rv[:, 0, tok(hh)], start=True, stop=True)
                        nc.tensor.matmul(ps[:, 5, tok(hh)], sT[:, 1, hh, :], rv[:, 1, tok(hh)], start=True, stop=False)
                        last = nc.tensor.matmul(ps[:, 5, tok(hh)], qdT[:, hh, :], kvs[:, hh, :], start=False, stop=True)
                    last.then_inc(inner_ps.sem, 1)
                if c == 14:
                    mo_t_out.wait(pe, l, 2)
                    centred.wait(pe, l, 1)
                    for hh in range(4):
                        nc.tensor.matmul(ps[:, 6 + hh // 2, (hh % 2) * S:(hh % 2 + 1) * S], mqT[:, hh, tok(1)], mkT[:, hh, :],
                                         start=True, stop=True)
                        last = nc.tensor.matmul(ps[:, 4, tok(hh)], mqT[:, hh, tok(0)], mkT[:, hh, tok(0)], start=True, stop=True)
                    last.then_inc(msc_ps.sem, 1)
                if c == 15:
                    m_exp.wait(pe, l, 1)
                    for hh in range(4):
                        turn(ps[:, 5, tok(hh)], msc0[:, hh, :])
                        for k in range(T):
                            o = (hh % 2) * S + k * P
                            last = turn(ps[:, 6 + hh // 2, o:o + P], msc1[:, hh, tok(k)])
                    last.then_inc(mpt_ps.sem, 1)
                if c == 16:
                    mpt_out.wait(pe, l, 1)
                    for hh in range(4):
                        nc.tensor.matmul(ps[:, 4, tok(hh)], mpT0[:, hh, :], mv[:, 0, tok(hh)], start=True, stop=True)
                        for k in range(T):
                            last = nc.tensor.matmul(ps[:, 5, tok(hh)], mpT1[:, hh, tok(k)], mv[:, k, tok(hh)],
                                                    start=k == 0, stop=k == T - 1)
                    last.then_inc(mo_ps.sem, 1)
                if c == OUT2_AT:
                    rows2_to_cols(l, 1)
                if c == GATE_AT:
                    rows2_to_cols(l, 2)

            def chunk2(l, c):
                slot = c % RING
                if c + 1 in PAIRED2:
                    return
                k0 = OUT2_AT if c < GATE_AT else GATE_AT
                parts = [(x % RING, (2 * (x - k0), 2 * (x - k0) + 1)) for x in ((c - 1, c) if c in PAIRED2 else (c,))]
                pe.wait_ge(split_done, l * CHUNKS2 + (BASE2 + c + 1 + RING))
                if c < PLE_AT:
                    i, half = c // 2, c % 2
                    if i >= 2 and half == 0:
                        tile2_out.wait(pe, l, i - 1)
                    b = 2 * (i % 2)
                    for t in range(T):
                        if c == 0:
                            cols2_ready.wait(pe, l, 2 + 2 * t)
                        for k in range(4):
                            w = slice(k * W_COLS, (k + 1) * W_COLS)
                            kk = 4 * half + k
                            last = products(ps[:, b + t, :], uH[:, kk, tok(t)], uL[:, kk, tok(t)], WH[:, slot, w],
                                            WL[:, slot, w], kk == 0, kk == KD - 1)
                elif c < OUT2_AT:
                    k = int(c > PLE_AT)
                    if c == PLE_AT:
                        ple_split.wait(pe, l, 1)
                    for t in range(T):
                        if c == PLE_AT:
                            tile2_out.wait(pe, l, NT2 - 1 + t)
                        for half in ((0, 1) if c == PLE_AT else (c - PLE_AT - 1,)):
                            w = slice(half * 512, half * 512 + 512) if c == PLE_AT else slice(0, 512)
                            last = products(ps[:, 2 * t + half, :], bH[:, k, tok(t)], bL[:, k, tok(t)], WH[:, slot, w],
                                            WL[:, slot, w], k == 0, k == 1)
                elif c < GATE_AT:
                    def wait_for(t, ks):
                        if ks[0] == 0:
                            emb_out.wait(pe, l, t + 1)
                        cols2_ready.wait(pe, l, 4 + 2 * t + ks[0] // 4 + 1)
                    by_rows(parts, (0, 1, 2, 3), uH, uL, 0, 7, wait_for, t0_done2)
                else:
                    def wait_for(t, ks):
                        cols2_ready.wait(pe, l, 8 + 2 * t + ks[0] // 4 + 1)
                    by_rows(parts, (0, 1, 2, 3), uH, uL, 0, 7, wait_for, t0_done2)
                if c < OUT2_AT:
                    last.then_inc(products_done, 1)

            with pe.Fori(0, L) as l:
                for c in range(CHUNKS2):
                    before2(l, c)
                    chunk2(l, c)

        @block.scalar
        def _(act):
            chain = scalar_chain

            def done(l, c, base=0):
                act.wait_ge(products_done, l * CHUNKS1 + c + 1 + RING)

            def split_high(l, c):
                n = CH if c < FULL1 else D
                act.wait_ge(w_loaded[c % RING], (l * (CHUNKS1 // RING) + c // RING + 1) * 16)
                act.wait_ge(products_done, l * CHUNKS1 + c + 1)
                nc.scalar.activation(WH[:, c % RING, 0:n], W[:, c % RING, 0:n], ACT.Copy).then_inc(high_ready, 1)

            def root_table(n):
                nc.scalar.activation(spare[:, n:n + 1], eps1, ACT.Sqrt)

            def stats(l, n, t):
                chain.then(act, nc.scalar.activation(rows[:, t, :], h[:, t, :], ACT.Square, accum_out=ssum[:, t:t + 1]))
                nc.scalar.activation(ssum[:, t:t + 1], ssum[:, t:t + 1], ACT.Sqrt, bias=eps1, scale=1.0 / D).then_inc(roots.sem, 1)

            def cols(l, n, src):
                for j in range(4):
                    if n == 1:
                        cols_ps.wait(act, l, 4 * n + j + 1)
                    else:
                        cols_weighted.wait(act, l, 2 * n + j + 1)
                    t, q = j // 2, j % 2
                    nc.scalar.activation(uH[:, 4 * q:4 * q + 4, tok(t)], four(ps[:, 4 + j, :] if n == 1 else src[:, j, :]),
                                         ACT.Copy).then_inc(cols_high.sem, 1)

            act.wait_ge(con_loaded, 16)
            act.wait_ge(set_up, 1)
            act.wait_ge(rev_steps, 17)
            nc.scalar.activation(rev_rows, ps[:, 0:4, 0:REV], ACT.Copy).then_inc(rev_steps, 1)
            act.wait_ge(rev_steps, 18)
            act.dma_start(rev, rev_rows.rearrange("p h j -> p (h j)")).then_inc(rev_stored, 16)

            with act.Fori(0, L) as l:
                chain.start(l * SCH1)
                split_high(l, 0)
                root_table(0)
                for t in range(T):
                    h_ready.wait(act, l, t + 1)
                    stats(l, 0, t)
                cols(l, 0, colsF)
                split_high(l, 1)
                dtt_ps.wait(act, l, 1)
                nc.scalar.activation(dtT[0:HEADS, :], ps[0:HEADS, 4, 0:S], ACT.Copy).then_inc(dtt_out.sem, 1)
                split_high(l, 2)
                dt_given.wait(act, l, 1)
                act.wait_ge(par_loaded, (l + 1) * 16)
                nc.scalar.activation(nega, par[:, C_AL:C_AL + HEADS], ACT.Exp)
                nc.scalar.activation(dte, dta, ACT.Exp, scale=-1.0).then_inc(dt_steps.sem, 1)
                dt_given.wait(act, l, 2)
                nc.scalar.activation(dtl, dtu, ACT.Ln).then_inc(dt_steps.sem, 1)
                for c in range(3, CHUNKS1):
                    split_high(l, c)
                    if c == 5:
                        cum_out.wait(act, l, 1)
                        nc.scalar.activation(dec_in, acum[:, HEADS:2 * HEADS], ACT.Exp)
                        nc.scalar.activation(dec_out, acum[:, 2 * HEADS:3 * HEADS], ACT.Exp).then_inc(decays.sem, 1)
                    for n, i in enumerate((0, 1) + XT):
                        if c == 2 * i + 6:
                            conv_done.wait(act, l, n + 1)
                            o = BC[:, 4 * n:4 * n + 4, :] if n < 2 else conv
                            nc.scalar.activation(o, conv, ACT.Silu).then_inc(conv_act.sem, 1)
                    if c % 2 == 0 and c // 2 - 2 < NT1:
                        i = c // 2 - 2
                        done(l, 2 * i + 1)
                        two = ps[:, 2 * (i % 2):2 * (i % 2) + 2, :]
                        name = TILES1[i]
                        if name[0] in "xBC":
                            if i:
                                conv_done.wait(act, l, {1: 1, 2: 2, 5: 3, 8: 4, 11: 5}[i])
                            o, f = xpad[:, :, TAPS - 1:TAPS - 1 + S], ACT.Copy
                            two = two.rearrange("p b (j s) -> p (b j) s", j=2)
                        elif name[0] == "z":
                            g = int(name[1])
                            if g:
                                y_ready.wait(act, l, 2 * g)
                            o, f = ev[0], ACT.Silu
                        elif name[:2] == "gs":
                            if name == "gs0":
                                off_ps.wait(act, l, GROUPS)
                            o, f = gate_s[:, :, (i % 2 == 0) * 512:(i % 2 == 0) * 512 + 512], ACT.Sigmoid
                            assert (name == "gs1") == (i % 2 == 0)
                        elif name[:2] == "ga":
                            if name == "ga0":
                                qk_ps.wait(act, l, 7)
                            o, f = gate_a[:, :, int(name[2]) * 512:int(name[2]) * 512 + 512], ACT.Sigmoid
                        elif name[0] == "v":
                            o, f = vv[int(name[1])], ACT.Copy
                        else:
                            n = [q[0] for q in QK].index(name)
                            e = QK[n][2]
                            if n in (5, 6):
                                y_ready.wait(act, l, 2 * GROUPS)
                            elif n in (1, 2, 3, 4):
                                qk_ps.wait(act, l, n)
                            elif n == 7:
                                qk_ps.wait(act, l, 5)
                            o, f = ev[e], ACT.Copy
                        nc.scalar.activation(o, two, f).then_inc(tile_out.sem, 1)
                    if c == 8:
                        cumt_ps.wait(act, l, 1)
                        nc.scalar.activation(cumT, ps[:, 5, 0:P], ACT.Copy).then_inc(cumt_out.sem, 1)
                    if c == 10:
                        btok_ps.wait(act, l, 1)
                        nc.scalar.activation(btok, four(ps[:, 4, :]), ACT.Copy).then_inc(btok_out.sem, 1)
                    for n, at_c in enumerate(QK_OUT):
                        if c == at_c:
                            qk_ps.wait(act, l, n + 1)
                            if n == 1:
                                act.wait_ge(rev_stored, 32)
                            name, b = QK[n][0], QK_BANK[n]
                            o = kT if name[0] == "k" else qT[:, int(name[1]) // 2]
                            nc.scalar.activation(o, ps[:, b:b + 2, :].rearrange("p b (j s) -> p (b j) s", j=2), ACT.Copy)\
                                .then_inc(qk_out.sem, 1)
                    for g, i in enumerate(XT):
                        if c == 2 * i + 8:
                            state_ps.wait(act, l, g + 1)
                            if g:
                                off_ps.wait(act, l, g)
                            nc.scalar.activation(state, ps[:, 6, :], ACT.Copy).then_inc(state_out.sem, 1)
                        for t, at_c in ((0, 2 * i + 7), (1, 2 * i + 9)):
                            if c == at_c:
                                row_ps.wait(act, l, 2 * g + t + 1)
                                if g:
                                    yd_ps.wait(act, l, 2 * (g - 1) + t + 1)
                                for e in range(HPG):
                                    a = t * HEADS + g * HPG + e
                                    ins = nc.scalar.activation(EM[t][:, e, :], ps[:, 6 + e // 4, tok(e % 4)], ACT.Exp,
                                                               bias=nacum[:, a:a + 1])
                                ins.then_inc(ssd_exp.sem, 1)
                        if c == 2 * i + 13:
                            y_gated.wait(act, l, g + 1)
                            for t in range(T):
                                ins = nc.scalar.activation(E0[:, t * 512:(t + 1) * 512], Y[g % 2][:, t, :], ACT.Square,
                                                           accum_out=gsum[:, t:t + 1])
                            chain.then(act, ins)
                            nc.scalar.activation(gsum, gsum, ACT.Sqrt, bias=eps1, scale=GROUPS / INNER).then_inc(group_root.sem, 1)
                        if c == 2 * i + 15:
                            for t in range(T):
                                y_weighted.wait(act, l, 2 * g + t + 1)
                                nc.scalar.activation(bH[:, 4 * g:4 * g + 4, tok(t)], four(ev[0][:, t, :]), ACT.Copy)\
                                    .then_inc(y_high.sem, 1)
                    for n, s in enumerate(HEAD_AT):
                        if c == s + 2:
                            att_masked.wait(act, l, n + 1)
                            nc.scalar.activation(sc1, sc1, ACT.Exp, bias=anb[:, 1:2], scale=SCALE, accum_out=az[:, 1:2])
                            nc.scalar.activation(sc0, sc0, ACT.Exp, bias=anb[:, 0:1], scale=SCALE, accum_out=az[:, 0:1])\
                                .then_inc(att_exp.sem, 1)
                    for n, s in enumerate(HEAD_AT):
                        if c == s + 4:
                            pt_ps.wait(act, l, n + 1)
                            if n:
                                o_ps.wait(act, l, n)
                            nc.scalar.activation(pT, ps[:, 7, 0:S + P], ACT.Copy).then_inc(pt_out.sem, 1)
                        if c == s + 5:
                            o_ps.wait(act, l, n + 1)
                            nc.scalar.activation(bH[:, 16 + n, :], ps[:, 6, 0:S], ACT.Copy).then_inc(o_high.sem, 1)
                    if c == OUT_AT:
                        cols(l, 1, None)
                    if c == GU_AT:
                        root_table(1)
                        for t in range(T):
                            h_ready.wait(act, l, t + 3)
                            stats(l, 2, t)
                        cols(l, 2, colsF)
                    for j in range(NGU):
                        if c == GU_AT + 2 * j + 4:
                            done(l, GU_AT + 2 * j + 1)
                            if j >= 2:
                                act_rows.wait(act, l, j - 1)
                            b = 2 * (j % 2)
                            nc.scalar.activation(sg[:, j % 2], ps[:, b:b + 2, 0:256], ACT.Silu).then_inc(gate_act.sem, 1)
                        if c == GU_AT + 2 * j + 6:
                            act_ps.wait(act, l, j + 1)
                            nc.scalar.activation(bH[:, 2 * j:2 * j + 2, :], ps[:, 4 + j % 2, :].rearrange("p (i s) -> p i s", i=2),
                                                 ACT.Copy).then_inc(act_high.sem, 1)
                assert chain.n == SCH1, chain.n

            root_table(2)
            for t in range(T):
                chain.start(L * SCH1 + t)
                act.wait_ge(h_ready.sem, L * 4 + t + 1)
                chain.then(act, nc.scalar.activation(sq[:, t, :], h[:, t, :], ACT.Square, accum_out=ssum[:, t:t + 1]))
                nc.scalar.activation(ssum[:, t:t + 1], ssum[:, t:t + 1], ACT.Sqrt, bias=eps1, scale=1.0 / D).then_inc(final_root, 1)

            def split2_high(l, c):
                n = SIZE2.get(c, CH)
                act.wait_ge(w_loaded[c % RING], (l * (CHUNKS2 // RING) + (BASE2 // RING + c // RING + 1)) * 16)
                act.wait_ge(products_done, l * CHUNKS2 + (BASE2 + c + 1))
                nc.scalar.activation(WH[:, c % RING, 0:n], W[:, c % RING, 0:n], ACT.Copy).then_inc(high_ready, 1)

            def done2(l, c):
                act.wait_ge(products_done, l * CHUNKS2 + (BASE2 + c + 1 + RING))

            def stats2(l, n, t):
                chain.then(act, nc.scalar.activation(sq[:, t, :], h[:, t, :], ACT.Square, accum_out=ssum[:, t:t + 1]))
                nc.scalar.activation(ssum[:, t:t + 1], ssum[:, t:t + 1], ACT.Sqrt, bias=eps2, scale=1.0 / D).then_inc(roots2.sem, 1)

            def cols2_to_high(l, n, tiles=range(T)):
                for j in range(2 * tiles[0], 2 * tiles[-1] + 2):
                    t, q = j // 2, j % 2
                    if n == 2:
                        cols2_ps.wait(act, l, 4 * n + j + 1)
                    else:
                        cols2_weighted.wait(act, l, 4 * n + j + 1)
                    nc.scalar.activation(uH[:, 4 * q:4 * q + 4, tok(t)], four(ps[:, 4 + j, :] if n == 2 else cols2[:, j, :]),
                                         ACT.Copy).then_inc(cols2_high.sem, 1)

            with act.Fori(0, L) as l:
                chain.start(l * SCH2 + L * SCH1 + T)
                split2_high(l, 0)
                root_table(3)
                for t in range(T):
                    h2_ready.wait(act, l, t + 1)
                    stats2(l, 0, t)
                act.dma_start(ple_gain, ple_g[bass.ds(l * P, P), :]).then_inc(gain_loaded, 16)
                cols2_to_high(l, 0)
                for c in range(1, CHUNKS2):
                    split2_high(l, c)
                    if c % 2 == 0 and 0 <= c // 2 - 2 < NT2:
                        i = c // 2 - 2
                        name = TILES2[i]
                        done2(l, 2 * i + 1)
                        two = ps[:, 2 * (i % 2):2 * (i % 2) + 2, :]
                        o, f = {"rk": (ev2[0], ACT.Copy), "rq": (ev2[1], ACT.Copy), "rv": (rv, ACT.Copy),
                                "mk": (ev2[1], ACT.Copy), "mq": (ev2[0], ACT.Copy), "mv": (mv, ACT.Copy),
                                "rz": (ev2[1], ACT.Silu), "mz": (ev2[0], ACT.Silu)}[name]
                        if name == "mk":
                            ret_t_ps.wait(act, l, 2)
                        elif name == "mq":
                            ret_t_ps.wait(act, l, 1)
                            kdec_ready.wait(act, l, 1)
                        elif name in ("rz", "mz"):
                            mo_t_ps.wait(act, l, 1 + (name == "mz"))
                        ins = nc.scalar.activation(o, two, f)
                        if name in ("mk", "mq"):
                            q = name == "mq"
                            ins = nc.scalar.activation(sq[:, :, q * 512:q * 512 + 512], two, ACT.Square)
                        ins.then_inc(tile2_out.sem, 1)
                    for n, at_c in enumerate((7, 9)):
                        if c == at_c:
                            ret_t_ps.wait(act, l, n + 1)
                            b = 4 + 2 * n
                            nc.scalar.activation((rkT, rqT)[n], ps[:, b:b + 2, :].rearrange("p b (j s) -> p (b j) s", j=2), ACT.Copy)\
                                .then_inc(ret_t_out.sem, 1)
                    if c == 10:
                        kv_ps.wait(act, l, 1)
                        nc.scalar.activation(kvs, four(ps[:, 4, :]), ACT.Copy).then_inc(kv_out.sem, 1)
                    for n, at_c in enumerate((11, 13, 17)):
                        if c == at_c:
                            head_sum.wait(act, l, n + 1)
                            nc.scalar.activation(head_ss[n], head_ss[n], ACT.Sqrt, bias=eps2, scale=1.0 / P).then_inc(head_root.sem, 1)
                    if c == 15:
                        centred.wait(act, l, 1)
                        nc.scalar.activation(sq[:, :, 0:512], rt, ACT.Square).then_inc(ret_squared.sem, 1)
                    if c == 16:
                        m_masked.wait(act, l, 1)
                        for t, m in ((0, msc0), (1, msc1)):
                            for hh in range(4):
                                a = 4 * t + hh
                                ins = nc.scalar.activation(m[:, hh, :], m[:, hh, :], ACT.Exp, bias=mneg[:, a:a + 1],
                                                           accum_out=mz[:, a:a + 1])
                        ins.then_inc(m_exp.sem, 1)
                    if c == 17:
                        mpt_ps.wait(act, l, 1)
                        nc.scalar.activation(mpT0, four(ps[:, 5, :]), ACT.Copy)
                        nc.scalar.activation(mpT1, ps[:, 6:8, :].rearrange("p b (j s) -> p (b j) s", j=2), ACT.Copy).then_inc(mpt_out.sem, 1)
                    if c == OUT2_AT + 1:
                        done2(l, OUT2_AT - 1)
                        for t in range(T):
                            nc.scalar.activation(emb[:, t, :], ps[:, 2 * t:2 * t + 2, :].rearrange("p b n -> p (b n)"), ACT.Copy)\
                                .then_inc(emb_out.sem, 1)
                            cols2_to_high(l, 1, (t,))
                    if c == OUT2_AT + 2:
                        for t in range(T):
                            emb_out.wait(act, l, t + 1)
                            ins = nc.scalar.activation(sq[:, t, :], emb[:, t, :], ACT.Square, accum_out=ple_ss[:, t:t + 1])
                        chain.then(act, ins)
                        nc.scalar.activation(ple_ss, ple_ss, ACT.Sqrt, bias=eps2, scale=1.0 / D).then_inc(ple_root.sem, 1)
                    if c == GATE_AT:
                        root_table(4)
                        for t in range(T):
                            h2_ready.wait(act, l, t + 3)
                            stats2(l, 2, t)
                        cols2_to_high(l, 2)
                for t in range(T):
                    if t == 0:
                        t0_done2.wait(act, l, 2)
                    else:
                        done2(l, CHUNKS2 - 1)
                    nc.scalar.activation(sg2[:, t, :], ps[:, 2 * t:2 * t + 2, :].rearrange("p b n -> p (b n)"), ACT.Sigmoid)\
                        .then_inc(gate2_out.sem, 1)
                assert chain.n == SCH2, chain.n

        @block.gpsimd
        def _(pool):
            with pool.Fori(0, L) as l:
                def state_input(g):
                    xdt_ready.wait(pool, l, g + 1)
                    if g:
                        state_ps.wait(pool, l, g)
                    decays.wait(pool, l, 1)
                    nc.gpsimd.tensor_tensor(out=xds.rearrange("p (e d) -> p e d", e=HPG),
                                            in0=xdt[:, 0, :].rearrange("p (e d) -> p e d", e=HPG),
                                            in1=bc(dec_out[:, g * HPG:(g + 1) * HPG].unsqueeze(2), HPG, HD),
                                            op=ALU.mult).then_inc(xds_ready.sem, 1)

                def gate(g):
                    ssd_y.wait(pool, l, 2 * g + 2)
                    tile_out.wait(pool, l, ZT[g] + 1)
                    nc.gpsimd.tensor_tensor(out=Y[g % 2], in0=Y[g % 2], in1=ev[0], op=ALU.mult).then_inc(y_gated.sem, 1)

                def rows_of(g):
                    cumt_out.wait(pool, l, 1)
                    if g:
                        row_ps.wait(pool, l, 2 * g)
                    nc.gpsimd.tensor_tensor(out=DR[:, :].rearrange("p (e l) -> p e l", e=HPG), in0=bc(cumT.unsqueeze(1), HPG, P),
                                            in1=bc(head_of[:, g * HPG:(g + 1) * HPG].unsqueeze(2), HPG, P),
                                            op=ALU.mult).then_inc(decay_rows.sem, 1)

                rows_of(0)
                for g in range(GROUPS):
                    state_input(g)
                    if g < GROUPS - 1:
                        rows_of(g + 1)
                    gate(g)

            def by_head(a):
                return a.rearrange("p (h n) -> p h n", h=4)

            pool.wait_ge(tables_loaded, 32)
            with pool.Fori(0, L) as l:
                rotated.wait(pool, l, 1)
                nc.gpsimd.tensor_tensor(out=by_head(kdec), in0=by_head(ev2[0][:, 0, :]), in1=bc(kdec_c.unsqueeze(2), 4, P),
                                        op=ALU.mult).then_inc(kdec_ready.sem, 1)
                ret_t_out.wait(pool, l, 2)
                nc.gpsimd.tensor_tensor(out=qdT, in0=rqT[:, :, P:S], in1=qpow, op=ALU.mult).then_inc(qd_ready.sem, 1)
                normed.wait(pool, l, 3)
                tile2_out.wait(pool, l, NT2 - 1)
                nc.gpsimd.tensor_tensor(out=rows2[:, :, 0:512], in0=rt, in1=ev2[1], op=ALU.mult).then_inc(ret_gated.sem, 1)

        @block.vector
        def _(dve):
            chain = vector_chain

            def tt(o, a, b, op):
                return nc.vector.tensor_tensor(out=o, in0=a, in1=b, op=op)

            def split_low(l, c):
                n = CH if c < FULL1 else D
                dve.wait_ge(high_ready, l * CHUNKS1 + c + 1)
                tt(WL[:, c % RING, 0:n], W[:, c % RING, 0:n], WH[:, c % RING, 0:n].bitcast(F32), ALU.subtract).then_inc(split_done, 1)

            def tile_done(l, t, n, c):
                if t == 0:
                    t0_done.wait(dve, l, n + 1)
                else:
                    dve.wait_ge(products_done, l * CHUNKS1 + c + RING)

            def add_down(l, t):
                tile_done(l, t, 0, 0)
                b = 6 if t == 0 else 2
                tt(h[:, t, :], h[:, t, :], ps[:, b:b + 2, :].rearrange("p b n -> p (b n)"), ALU.add).then_inc(h_ready.sem, 1)

            def scaled_rows(l, n, t):
                roots.wait(dve, l, n + t + 1)
                chain.then(dve, nc.vector.reciprocal(rinv[:, t:t + 1], ssum[:, t:t + 1]))
                nc.vector.tensor_scalar(rows[:, t, :], h[:, t, :], rinv[:, t:t + 1], None, ALU.mult).then_inc(rows_ready.sem, 1)

            def weighted(l, n, col, t):
                for j in (2 * t, 2 * t + 1):
                    cols_ps.wait(dve, l, 4 * n + j + 1)
                    q = j % 2
                    tt(four(colsF[:, j, :]), four(ps[:, 4 + j, :]),
                       bc(par[:, col + 4 * q:col + 4 * q + 4].unsqueeze(2), 4, P), ALU.mult).then_inc(cols_weighted.sem, 1)

            def cols_low(l, n, t):
                for j in (2 * t, 2 * t + 1):
                    cols_high.wait(dve, l, 4 * n + j + 1)
                    t, q = j // 2, j % 2
                    src = ps[:, 4 + j, :] if n == 1 else colsF[:, j, :]
                    tt(uL[:, 4 * q:4 * q + 4, tok(t)], four(src), uH[:, 4 * q:4 * q + 4, tok(t)].bitcast(F32),
                       ALU.subtract).then_inc(cols_ready.sem, 1)

            def convolve(l, n):
                i = ((0, 1) + XT)[n]
                j0 = (16, 20, 0, 4, 8, 12)[n]
                tile_out.wait(dve, l, i + 1)
                if n == 0:
                    chain.then(dve, nc.vector.memset(xpad[:, :, 0:TAPS - 1], 0.0))
                elif n <= 2:
                    conv_act.wait(dve, l, n)
                else:
                    xt_ps.wait(dve, l, n - 2)
                for k in range(TAPS - 1, -1, -1):
                    for j in range(4):
                        w = C_CW + TAPS * (j0 + j) + k
                        if k == TAPS - 1:
                            ins = nc.vector.tensor_scalar(conv[:, j, :], xpad[:, j, k:k + S], par[:, w:w + 1],
                                                          par[:, C_CB + j0 + j:C_CB + j0 + j + 1], ALU.mult, ALU.add)
                        else:
                            ins = nc.vector.scalar_tensor_tensor(out=conv[:, j, :], in0=xpad[:, j, k:k + S],
                                                                 scalar=par[:, w:w + 1], in1=conv[:, j, :],
                                                                 op0=ALU.mult, op1=ALU.add)
                    if k:
                        chain.then(dve, ins)
                ins.then_inc(conv_done.sem, 1)

            nc.vector.memset(eps2, EPS2).then_inc(split_done, RING)
            nc.vector.memset(eps1, EPS1).then_inc(products_done, RING)
            dve.wait_ge(late_loaded, 16)
            nc.vector.tensor_copy(tri_r[:, :], tri)
            nc.vector.tensor_copy(ident_r[:, :], ident)
            nc.vector.tensor_scalar(never_r[:, :], later, NEG, None, ALU.mult)
            nc.vector.tensor_copy(later_r[:, :], later).then_inc(set_up, 1)
            dve.wait_ge(con_loaded, 16)
            dve.wait_ge(rev_steps, 18)
            nc.vector.memset(ps[:, 2:4, :], 0.0)
            nc.vector.memset(ps[:, 6:8, :], 0.0).then_inc(t0_done.sem, 1)

            with dve.Fori(0, L) as l:
                chain.start(l * VCH1)
                add_down(l, 0)
                split_low(l, 0)
                scaled_rows(l, 0, 0)
                add_down(l, 1)
                dve.wait_ge(par_loaded, (l + 1) * 16)
                weighted(l, 0, C_MIX, 0)
                scaled_rows(l, 0, 1)
                cols_low(l, 0, 0)
                weighted(l, 0, C_MIX, 1)
                cols_low(l, 0, 1)
                chain.then(dve, nc.vector.tensor_copy(dtw_h[:, :], par[:, C_WDT:C_WDT + KD * HEADS]))
                tt(dtw_l[:, :], par[:, C_WDT:C_WDT + KD * HEADS], dtw_h[:, :].bitcast(F32), ALU.subtract).then_inc(dtw_ready.sem, 1)
                split_low(l, 1)
                split_low(l, 2)
                dt_ps.wait(dve, l, 1)
                two = lambda a: a.rearrange("p (t n) -> p t n", t=T)
                chain.then(dve, tt(two(dtx), two(ps[:, 5, 0:T * HEADS]), bc(par[:, C_DTB:C_DTB + HEADS].unsqueeze(1), T, HEADS), ALU.add))
                nc.vector.scalar_tensor_tensor(out=dta, in0=dtx, scalar=-1.0, in1=dtx, op0=ALU.mult, op1=ALU.max).then_inc(dt_given.sem, 1)
                dt_steps.wait(dve, l, 1)
                chain.then(dve, nc.vector.tensor_scalar(dtu, dte, 1.0, None, ALU.add))
                chain.then(dve, nc.vector.tensor_scalar(dtd, dtu, -1.0, None, ALU.add))
                chain.then(dve, nc.vector.tensor_scalar(dtz, dtd, 0.0, None, ALU.is_equal))
                chain.then(dve, tt(dtd, dtd, dtz, ALU.add))
                nc.vector.reciprocal(dtd, dtd).then_inc(dt_given.sem, 1)
                dt_steps.wait(dve, l, 2)
                chain.then(dve, tt(dtl, dtl, dtz, ALU.add))
                chain.then(dve, tt(dtl, dtl, dtd, ALU.mult))
                chain.then(dve, tt(dtl, dtl, dte, ALU.mult))
                chain.then(dve, nc.vector.scalar_tensor_tensor(out=dt, in0=dtx, scalar=0.0, in1=dtl, op0=ALU.max, op1=ALU.add))
                chain.then(dve, nc.vector.scalar_tensor_tensor(out=two(adt), in0=two(dt), scalar=-1.0, in1=bc(nega.unsqueeze(1), T, HEADS),
                                                               op0=ALU.mult, op1=ALU.mult))
                chain.then(dve, nc.vector.tensor_copy(adt_h[:, :], adt))
                tt(adt_l[:, :], adt, adt_h[:, :].bitcast(F32), ALU.subtract).then_inc(adt_ready.sem, 1)

                for c in range(3, CHUNKS1):
                    split_low(l, c)
                    if c == 5:
                        cum_ps.wait(dve, l, 1)
                        nc.vector.tensor_scalar(nacum, ps[:, 5, 0:T * HEADS], -1.0, None, ALU.mult)
                        nc.vector.tensor_copy(acum, ps[:, 5, 0:3 * HEADS])
                        chain.then(dve, nc.vector.tensor_copy(cum_hl[:, :, 0:HEADS], two(ps[:, 5, 0:T * HEADS])))
                        tt(cum_hl[:, :, HEADS:2 * HEADS], two(ps[:, 5, 0:T * HEADS]), cum_hl[:, :, 0:HEADS].bitcast(F32), ALU.subtract)\
                            .then_inc(cum_out.sem, 1)
                    if c == 10:
                        cb_ps.wait(dve, l, 1)
                        for t in range(T):
                            ins = tt(cbm[:, t], four(ps[:, 6 + t, :]), bc(tri_r[:, :].bitcast(F32).unsqueeze(1), GROUPS, P), ALU.mult)
                        ins.then_inc(cb_masked.sem, 1)
                    for g, i in enumerate(XT):
                        hs = slice(g * HPG, (g + 1) * HPG)
                        y = Y[g % 2]

                        def heads(a):
                            return a.rearrange("p (e d) -> p e d", e=HPG)
                        if c == 2 * i + 7:
                            xt_ps.wait(dve, l, g + 1)
                            if g:
                                yd_ps.wait(dve, l, 2 * g)
                            for t in range(T):
                                tt(heads(y[:, t, :]), heads(ps[:, 4 + t, :]),
                                   bc(par[:, C_DS + g * HPG:C_DS + (g + 1) * HPG].unsqueeze(2), HPG, HD), ALU.mult)
                                ins = tt(heads(xdt[:, t, :]), heads(ps[:, 4 + t, :]),
                                         bc(dt[:, t * HEADS + g * HPG:t * HEADS + (g + 1) * HPG].unsqueeze(2), HPG, HD), ALU.mult)
                            ins.then_inc(xdt_ready.sem, 1)
                        for t, at_c in ((0, 2 * i + 8), (1, 2 * i + 10)):
                            if c == at_c:
                                ssd_exp.wait(dve, l, 2 * g + t + 1)
                                tt(EM[t], EM[t], bc(cbm[:, t, g, :].unsqueeze(1), HPG, P), ALU.mult).then_inc(ssd_m.sem, 1)
                        if c == 2 * i + 11:
                            yd_ps.wait(dve, l, 2 * g + 1)
                            tt(y[:, 0, :], y[:, 0, :], ps[:, 4, :], ALU.add).then_inc(ssd_y.sem, 1)
                        if c == 2 * i + 12:
                            yd_ps.wait(dve, l, 2 * g + 2)
                            tt(y[:, 1, :], y[:, 1, :], ps[:, 5, :], ALU.add)
                            off_ps.wait(dve, l, g + 1)
                            decays.wait(dve, l, 1)
                            chain.then(dve, tt(heads(yoff), heads(ps[:, 7, :]), bc(dec_in[:, hs].unsqueeze(2), HPG, HD), ALU.mult))
                            tt(y[:, 1, :], y[:, 1, :], yoff, ALU.add).then_inc(ssd_y.sem, 1)
                        if c == 2 * i + 13:
                            group_root.wait(dve, l, g + 1)
                            chain.then(dve, nc.vector.reciprocal(ginv, gsum))
                            for t in range(T):
                                ins = nc.vector.tensor_scalar(y[:, t, :], y[:, t, :], ginv[:, t:t + 1], None, ALU.mult)
                            ins.then_inc(y_scaled.sem, 1)
                        if c == 2 * i + 15:
                            for t in range(T):
                                yt_ps.wait(dve, l, 2 * g + t + 1)
                                tt(four(ev[0][:, t, :]), four(ps[:, 4 + t, :]),
                                   bc(par[:, C_SN + 4 * g:C_SN + 4 * g + 4].unsqueeze(2), 4, P), ALU.mult).then_inc(y_weighted.sem, 1)
                            for t in range(T):
                                y_high.wait(dve, l, 2 * g + t + 1)
                                tt(bL[:, 4 * g:4 * g + 4, tok(t)], four(ev[0][:, t, :]), bH[:, 4 * g:4 * g + 4, tok(t)].bitcast(F32),
                                   ALU.subtract).then_inc(y_ready.sem, 1)
                    for n, i in enumerate((0, 1) + XT):
                        if c == 2 * i + CONV_AT:
                            convolve(l, n)
                    for n, (name, i, e, _) in enumerate(QK):
                        if c == 2 * i + 5:
                            tile_out.wait(dve, l, i + 1)
                            for_h = ev[e].rearrange("p t (h j) -> p t h j", h=4)
                            half = 16
                            for t in range(T):
                                xx = for_h[:, t]
                                tt(rope_a[:, t], xx[:, :, 0:32], bc(rope_c[:, t, :].unsqueeze(1), 4, 32), ALU.mult)
                                tt(rope_b[:, t, :, 0:half], xx[:, :, half:32], bc(rope_s[:, t, 0:half].unsqueeze(1), 4, half), ALU.mult)
                                ins = tt(rope_b[:, t, :, half:32], xx[:, :, 0:half], bc(rope_s[:, t, half:32].unsqueeze(1), 4, half), ALU.mult)
                            chain.then(dve, ins)
                            for t in range(T):
                                ins = tt(for_h[:, t, :, 0:32], rope_a[:, t], rope_b[:, t], ALU.add)
                            ins.then_inc(roped.sem, 1)
                    for n, s in enumerate(HEAD_AT):
                        if c == s + 3:
                            att_exp.wait(dve, l, n + 1)
                            tt(sc1[:, 0:S], sc1[:, 0:S], sc1[:, S:2 * S], ALU.add)
                            tt(sc0[:, 0:P], sc0[:, 0:P], sc0[:, P:2 * P], ALU.add)
                            chain.then(dve, nc.vector.reciprocal(azi, az))
                            tt(sc1[:, 0:S], sc1[:, 0:S], sc1[:, 2 * S:3 * S], ALU.add)
                            chain.then(dve, tt(sc0[:, 0:P], sc0[:, 0:P], sc0[:, 2 * P:3 * P], ALU.add))
                            nc.vector.tensor_scalar(sc1[:, 0:S], sc1[:, 0:S], azi[:, 1:2], None, ALU.mult)
                            nc.vector.tensor_scalar(sc0[:, 0:P], sc0[:, 0:P], azi[:, 0:1], None, ALU.mult).then_inc(att_p.sem, 1)
                    for n, s in enumerate(HEAD_AT):
                        if c == s + 2:
                            dve.wait_ge(set_up, 1)
                            score_ps.wait(dve, l, n + 1)
                            if n:
                                pt_ps.wait(dve, l, n)
                            m1 = mask.rearrange("p g k -> p (g k)")
                            nc.vector.tensor_tensor_reduce(out=sc1, in0=ps[:, 4:6, :].rearrange("p b k -> p (b k)")[:, 0:768], in1=m1,
                                                           scale=1.0, scalar=NEG, op0=ALU.add, op1=ALU.max, accum_out=amax[:, 1:2])
                            chain.then(dve, nc.vector.tensor_tensor_reduce(
                                out=sc0.rearrange("p (g k) -> p g k", g=NPAT), in0=ps[:, 6, 0:384].rearrange("p (g k) -> p g k", g=NPAT),
                                in1=mask[:, :, P:S], scale=1.0, scalar=NEG, op0=ALU.add, op1=ALU.max, accum_out=amax[:, 0:1]))
                            nc.vector.tensor_scalar(anb, amax, -SCALE, None, ALU.mult).then_inc(att_masked.sem, 1)
                        if c == s + 5:
                            o_high.wait(dve, l, n + 1)
                            tt(bL[:, 16 + n, :], ps[:, 6, 0:S], bH[:, 16 + n, :].bitcast(F32), ALU.subtract).then_inc(o_ready.sem, 1)
                    if c == ATT_AT + 1:
                        for t in range(T):
                            tile_done(l, t, 1, ATT_AT)
                            tt(gate_s[:, t, :], gate_s[:, t, :], ps[:, 2 * t:2 * t + 2, :].rearrange("p b n -> p (b n)"), ALU.mult)\
                                .then_inc(ssd_gated.sem, 1)
                    if c == OUT_AT:
                        for t in range(T):
                            tile_done(l, t, 2, OUT_AT)
                            chain.then(dve, tt(gate_a[:, t, :], gate_a[:, t, :], ps[:, 2 * t:2 * t + 2, :].rearrange("p b n -> p (b n)"), ALU.mult))
                            tt(rows[:, t, :], gate_a[:, t, :], gate_s[:, t, :], ALU.add).then_inc(rows_ready.sem, 1)
                        for t in range(T):
                            cols_low(l, 1, t)
                    if c == GU_AT:
                        for t in range(T):
                            tile_done(l, t, 3, GU_AT)
                            tt(h[:, t, :], h[:, t, :], ps[:, 2 * t:2 * t + 2, :].rearrange("p b n -> p (b n)"), ALU.add)\
                                .then_inc(h_ready.sem, 1)
                            if t == 0:
                                scaled_rows(l, 2, 0)
                        weighted(l, 2, C_FFN, 0)
                        scaled_rows(l, 2, 1)
                        cols_low(l, 2, 0)
                        weighted(l, 2, C_FFN, 1)
                        cols_low(l, 2, 1)
                    for j in range(NGU):
                        if c == GU_AT + 2 * j + 4:
                            gate_act.wait(dve, l, j + 1)
                            if j >= 2:
                                act_ps.wait(dve, l, j - 1)
                            b = 2 * (j % 2)
                            tt(ac[:, j % 2], sg[:, j % 2], ps[:, b:b + 2, 256:512], ALU.mult).then_inc(act_rows.sem, 1)
                        if c == GU_AT + 2 * j + 6:
                            act_high.wait(dve, l, j + 1)
                            tt(bL[:, 2 * j:2 * j + 2, :], ps[:, 4 + j % 2, :].rearrange("p (i s) -> p i s", i=2),
                               bH[:, 2 * j:2 * j + 2, :].bitcast(F32), ALU.subtract).then_inc(act_ready.sem, 1)
                assert chain.n == VCH1, chain.n

            dve.wait_ge(final_loaded, 16)
            for t in range(T):
                add_down(L, t)
            for t in range(T):
                dve.wait_ge(final_root, t + 1)
                chain.start(L * VCH1 + t)
                chain.then(dve, nc.vector.reciprocal(rinv[:, t:t + 1], ssum[:, t:t + 1]))
                nc.vector.scalar_tensor_tensor(out=h[:, t, :], in0=h[:, t, :], scalar=rinv[:, t:t + 1], in1=M0,
                                               op0=ALU.mult, op1=ALU.mult).then_inc(h2_ready.sem, 1)
            dve.wait_ge(tables_loaded, 32)

            def heads8(a):
                return a.rearrange("p t (h n) -> p t h n", h=4)

            def by_head(a):
                return a.rearrange("p (t h) -> p t h", t=T)

            def split2_low(l, c):
                n = SIZE2.get(c, CH)
                dve.wait_ge(high_ready, l * CHUNKS2 + (BASE2 + c + 1))
                tt(WL[:, c % RING, 0:n], W[:, c % RING, 0:n], WH[:, c % RING, 0:n].bitcast(F32), ALU.subtract).then_inc(split_done, 1)

            def scaled_rows2(l, n, t):
                roots2.wait(dve, l, n + t + 1)
                chain.then(dve, nc.vector.reciprocal(rinv[:, t:t + 1], ssum[:, t:t + 1]))
                nc.vector.tensor_scalar(rows2[:, t, :], h[:, t, :], rinv[:, t:t + 1], None, ALU.mult).then_inc(rows2_ready.sem, 1)

            def weighted2(l, n, col, t):
                for j in (2 * t, 2 * t + 1):
                    cols2_ps.wait(dve, l, 4 * n + j + 1)
                    q = j % 2
                    tt(four(cols2[:, j, :]), four(ps[:, 4 + j, :]),
                       bc(par[:, col + 4 * q:col + 4 * q + 4].unsqueeze(2), 4, P), ALU.mult).then_inc(cols2_weighted.sem, 1)

            def cols2_to_low(l, n, t):
                for j in (2 * t, 2 * t + 1):
                    cols2_high.wait(dve, l, 4 * n + j + 1)
                    t, q = j // 2, j % 2
                    src = ps[:, 4 + j, :] if n == 2 else cols2[:, j, :]
                    tt(uL[:, 4 * q:4 * q + 4, tok(t)], four(src), uH[:, 4 * q:4 * q + 4, tok(t)].bitcast(F32),
                       ALU.subtract).then_inc(cols2_ready.sem, 1)

            def normalised(l, n, src):
                head_root.wait(dve, l, n + 1)
                chain.then(dve, nc.vector.reciprocal(head_ss[n], head_ss[n]))
                tt(heads8(src), heads8(src), bc(by_head(head_ss[n]).unsqueeze(3), T, 4, P), ALU.mult).then_inc(normed.sem, 1)

            with dve.Fori(0, L) as l:
                chain.start(l * VCH2 + L * VCH1 + T)
                for t in range(T):
                    scaled_rows2(l, 0, t)
                split2_low(l, 0)
                dve.wait_ge(par_loaded, (l + L + 1) * 16)
                for t in range(T):
                    weighted2(l, 0, C_NG, t)
                    cols2_to_low(l, 0, t)
                pt = par[:, C_PT:C_PT + 2 * S].rearrange("p (k s) -> p k s", k=2)
                chain.then(dve, nc.vector.tensor_copy(bH[:, 0:2, :], pt))
                tt(bL[:, 0:2, :], pt, bH[:, 0:2, :].bitcast(F32), ALU.subtract).then_inc(ple_split.sem, 1)
                for c in range(1, CHUNKS2):
                    split2_low(l, c)
                    for n, at_c in enumerate((5, 7)):
                        if c == at_c:
                            tile2_out.wait(dve, l, n + 1)
                            half = P // 2
                            for t in range(T):
                                xx, rr = four(ev2[n][:, t, :]), four(rt[:, t, :])
                                tt(rr[:, :, 0:half], xx[:, :, half:P], bc(rot_s[:, t, 0:half].unsqueeze(1), 4, half), ALU.mult)
                                chain.then(dve, tt(rr[:, :, half:P], xx[:, :, 0:half], bc(rot_s[:, t, half:P].unsqueeze(1), 4, half), ALU.mult))
                                chain.then(dve, tt(xx, xx, bc(rot_c[:, t, :].unsqueeze(1), 4, P), ALU.mult))
                                ins = tt(xx, xx, rr, ALU.add)
                            ins.then_inc(rotated.sem, 1)
                    if c == 12:
                        s_ps.wait(dve, l, 1)
                        for t in range(T):
                            ins = tt(sT[:, t], four(ps[:, 6 + t, :]), decay, ALU.mult)
                        ins.then_inc(s_decayed.sem, 1)
                    for n, at_c in enumerate((10, 12)):
                        if c == at_c:
                            tile2_out.wait(dve, l, 4 + n)
                            nc.vector.tensor_reduce(out=by_head(head_ss[n]), in_=heads8(sq[:, :, n * 512:n * 512 + 512]), axis=AX.X,
                                                    op=ALU.add).then_inc(head_sum.sem, 1)
                    for n, at_c in enumerate((11, 13)):
                        if c == at_c:
                            normalised(l, n, ev2[1 - n])
                    for n, at_c in enumerate((13, 14)):
                        if c == at_c:
                            mo_t_ps.wait(dve, l, n + 1)
                            src = ps[:, 4 + 2 * n:6 + 2 * n, :].rearrange("p b (j s) -> p (b j) s", j=2)
                            gain = par[:, C_KN:C_KN + 1] if n == 0 else par[:, C_QN:C_QN + 1]
                            nc.vector.tensor_scalar((mkT, mqT)[n], src, gain, 1.0 if n == 0 else SCALE, ALU.mult, ALU.mult)\
                                .then_inc(mo_t_out.sem, 1)
                    if c == 14:
                        inner_ps.wait(dve, l, 1)
                        chain.then(dve, nc.vector.tensor_reduce(out=by_head(head_mean), in_=heads8(ps[:, 4:6, :]), axis=AX.X, op=ALU.add))
                        chain.then(dve, nc.vector.tensor_scalar(head_mean, head_mean, -1.0 / P, None, ALU.mult))
                        tt(heads8(rt), heads8(ps[:, 4:6, :]), bc(by_head(head_mean).unsqueeze(3), T, 4, P), ALU.add).then_inc(centred.sem, 1)
                    if c == 15:
                        dve.wait_ge(set_up, 1)
                        msc_ps.wait(dve, l, 1)
                        for t in range(T):
                            for hh in range(4):
                                a = 4 * t + hh
                                o, b, i = ((msc0[:, hh, :], bias[:, hh, P:S], ps[:, 4, tok(hh)]),
                                           (msc1[:, hh, :], bias[:, hh, :], ps[:, 6 + hh // 2, (hh % 2) * S:(hh % 2 + 1) * S]))[t]
                                ins = nc.vector.tensor_tensor_reduce(out=o, in0=i, in1=b, scale=1.0, scalar=NEG, op0=ALU.add,
                                                                     op1=ALU.max, accum_out=mmax[:, a:a + 1])
                        chain.then(dve, ins)
                        nc.vector.tensor_scalar(mneg, mmax, -1.0, None, ALU.mult).then_inc(m_masked.sem, 1)
                    if c == 16:
                        ret_squared.wait(dve, l, 1)
                        nc.vector.tensor_reduce(out=by_head(head_ss[2]), in_=heads8(sq[:, :, 0:512]), axis=AX.X, op=ALU.add)\
                            .then_inc(head_sum.sem, 1)
                    if c == 17:
                        normalised(l, 2, rt)
                    if c == 18:
                        mo_ps.wait(dve, l, 1)
                        m_exp.wait(dve, l, 1)
                        chain.then(dve, nc.vector.reciprocal(mz, mz))
                        tile2_out.wait(dve, l, NT2)
                        for t in range(T):
                            for hh in range(4):
                                a = 4 * t + hh
                                ins = nc.vector.scalar_tensor_tensor(out=rows2[:, t, 512 + hh * P:512 + (hh + 1) * P],
                                                                     in0=ps[:, 4 + t, tok(hh)], scalar=mz[:, a:a + 1],
                                                                     in1=ev2[0][:, t, tok(hh)], op0=ALU.mult, op1=ALU.mult)
                            ins.then_inc(rows2_ready.sem, 1)
                    if c == OUT2_AT + 1:
                        for t in range(T):
                            weighted2(l, 1, C_YW, t)
                            cols2_to_low(l, 1, t)
                    if c == OUT2_AT + 2:
                        ple_root.wait(dve, l, 1)
                        dve.wait_ge(gain_loaded, (l + 1) * 16)
                        chain.then(dve, nc.vector.reciprocal(ple_ss, ple_ss))
                        for t in range(T):
                            ins = nc.vector.scalar_tensor_tensor(out=emb[:, t, :], in0=emb[:, t, :], scalar=ple_ss[:, t:t + 1],
                                                                 in1=ple_gain, op0=ALU.mult, op1=ALU.mult)
                        ins.then_inc(emb_ready.sem, 1)
                    if c == GATE_AT:
                        for t in range(T):
                            if t == 0:
                                t0_done2.wait(dve, l, 1)
                            else:
                                dve.wait_ge(products_done, l * CHUNKS2 + (BASE2 + GATE_AT + RING))
                            tt(h[:, t, :], h[:, t, :], ps[:, 2 * t:2 * t + 2, :].rearrange("p b n -> p (b n)"), ALU.add)\
                                .then_inc(h2_ready.sem, 1)
                            scaled_rows2(l, 2, t)
                        for t in range(T):
                            cols2_to_low(l, 2, t)
                for t in range(T):
                    gate2_out.wait(dve, l, t + 1)
                    chain.then(dve, tt(sg2[:, t, :], sg2[:, t, :], emb[:, t, :], ALU.mult))
                    tt(h[:, t, :], h[:, t, :], sg2[:, t, :], ALU.add).then_inc(h2_ready.sem, 1)
                assert chain.n == VCH2, chain.n


def constants():
    i = np.arange(P)
    c1 = np.zeros((P, N_CONST1), np.float32)
    c1[:, K_ID:K_ID + P] = np.eye(P)
    c1[:, K_TRI:K_TRI + P] = i[:, None] <= i[None, :]
    c1[:, K_LATER:K_LATER + P] = i[:, None] > i[None, :]
    c1[:, K_HEAD:K_HEAD + HEADS] = i[:, None] % HEADS == np.arange(HEADS)[None, :]
    dist = (P + i)[:, None] - np.arange(S)[None, :]
    for g, (window, dil) in enumerate(PATTERNS):
        ok = (dist >= 0) & (dist % dil == 0) & (dist // dil <= window // dil)
        c1[:, K_MASK + g * S:K_MASK + (g + 1) * S] = np.where(ok, 0.0, NEG)
    pos = np.arange(S, dtype=np.float32)

    def table(theta, width):
        half = width // 2
        inv = np.float32(theta) ** (-np.arange(half, dtype=np.float32) / np.float32(half))
        ang = (pos[:, None] * inv.astype(np.float32)[None, :]).astype(np.float32)
        c, s = np.cos(ang), np.sin(ang)
        both = [np.concatenate([c, c], 1), np.concatenate([-s, s], 1)]
        return [b.reshape(T, P, width).transpose(1, 0, 2).reshape(P, T * width) for b in both]

    c1[:, K_ROPE1:K_KDEC] = np.concatenate(table(500000.0, 32), 1)
    c2 = np.zeros((P, N_CONST2), np.float32)
    c2[:, K_ROPE2:K_DECAY] = np.concatenate(table(10000.0, P), 1)
    log_g = np.log1p(-np.power(2.0, -5.0 - np.arange(4)))
    rel = i[None, :] - i[:, None]
    for k in range(4):
        c2[:, K_DECAY + k * P:K_DECAY + (k + 1) * P] = np.where(rel >= 0, np.exp(log_g[k] * np.maximum(rel, 0)) * SCALE, 0)
        c2[:, K_QPOW + k * P:K_QPOW + (k + 1) * P] = np.exp(log_g[k] * (i + 1.0))[None, :]
        c1[:, K_KDEC + k] = np.exp(log_g[k] * (P - 1 - i)) * SCALE
    n = np.arange(S)
    exact = BUCKETS // 2
    nf = np.maximum(n, 1).astype(np.float32)
    large = exact + (np.log(nf / exact) / np.float32(np.log(MAX_DIST / exact)) * (BUCKETS - exact)).astype(np.int32)
    bucket = np.where(n < exact, n, np.minimum(large, BUCKETS - 1))
    onehot = np.zeros((BUCKETS + 1, REV), np.float32)
    for j in range(REV):
        onehot[bucket[S - 1 - j] if j < S else BUCKETS, j] = 1.0 if j < S else NEG
    return c1, c2, onehot


def by_tile(w, start):
    t = w[:, start:start + 512].reshape(2, 4, P, 512)
    return t.transpose(0, 2, 1, 3).reshape(2, P, CH)


def by_rows(w):
    return w.reshape(-1, 2, P, D).transpose(0, 2, 1, 3).reshape(-1, P, CH)


def by_pairs(w):
    t = w.reshape(2, 4, P, 2, NGU, 256).transpose(4, 0, 2, 1, 3, 5)
    return t.reshape(2 * NGU, P, CH)


def columns(v):
    return v.reshape(-1, P).T


def lay_out(a):
    first, second, pars = [], [], np.zeros((2 * L + 1, P, N_PAR), np.float32)
    for l in range(L):
        w = a["w_in"][l]
        for name in TILES1:
            kind = name.rstrip("0123456789")
            at = START1[kind] + 512 * (int(name[len(kind):]) if name[len(kind):] else 0)
            first.append(by_tile(w, at))
        first += [by_rows(a["w_ssd_branch"][l]), by_rows(a["w_attn_branch"][l]), by_rows(a["w_out"][l]),
                  by_pairs(a["w_gate_up"][l]), by_rows(a["w_down"][l])]
        p = pars[l]
        p[:, C_MIX:C_MIX + 8] = columns(a["norm_mix"][l])
        p[:, C_FFN:C_FFN + 8] = columns(a["norm_ffn"][l])
        p[:, C_CW:C_CB] = a["conv_w"][l].reshape(TAPS, 24, P).transpose(2, 1, 0).reshape(P, 24 * TAPS)
        p[:, C_CB:C_SN] = columns(a["conv_b"][l])
        p[:, C_SN:C_DTB] = columns(a["ssd_norm"][l])
        p[:, C_DTB:C_AL] = a["dt_bias"][l]
        p[:, C_AL:C_DS] = a["a_log"][l]
        p[:, C_DS:C_WDT] = a["d_skip"][l]
        p[:, C_WDT:N_PAR1] = w[:, DT_AT:DT_AT + HEADS].reshape(KD, P, HEADS).transpose(1, 0, 2).reshape(P, -1)
    for l in range(L):
        w = a["w_in_2"][l]
        second += [by_tile(w, START2[name]) for name in TILES2]
        second += [by_rows(a["w_ple_2"][l]), by_rows(a["w_out_2"][l]), by_rows(a["w_ple_gate_2"][l])]
        p = pars[L + l]
        p[:, C_NG:C_NG + 8] = columns(a["norm_g_2"][l])
        p[:, C_YW:C_YW + 4] = columns(a["ret_norm_g_2"][l])
        p[:, C_YW + 4:C_YW + 8] = 1.0
        p[:, C_QN] = a["q_norm_g_2"][l]
        p[:, C_KN] = a["k_norm_g_2"][l]
        p[:, C_PT:C_PT + 2 * S] = a["p_2"][l, 0].T.reshape(2, P, S).transpose(1, 0, 2).reshape(P, 2 * S)
    c1, c2, onehot = constants()
    return {
        "stream1": np.concatenate(first).reshape(-1, CH), "stream2": np.concatenate(second).reshape(-1, CH),
        "pars": pars.reshape(-1, N_PAR), "const1": c1, "const2": c2, "onehot": onehot,
        "relb": np.concatenate([a["rel_bias_2"], np.ones((1, 4), np.float32)]),
        "final_g": np.broadcast_to(a["norm_final"], (P, D)).copy(),
        "ple_g": np.broadcast_to(a["ple_norm_g_2"][:, None, :], (L, P, D)).reshape(L * P, D).copy(),
        "x": a["x"][0],
    }


def kernel(**inputs):
    import concourse.bacc as bacc
    from concourse.bass_utils import run_bass_kernel_spmd

    arrays = lay_out({k: np.asarray(v) for k, v in inputs.items()})
    nc = bacc.Bacc("TRN2", target_bir_lowering=False, num_devices=1, dynamic_dma_scratch_size=1024)
    args = {n: nc.dram_tensor(f"in_{n}", a.shape, F32, kind="ExternalInput").ap() for n, a in arrays.items()}
    out = nc.dram_tensor("out", (S, D), F32, kind="ExternalOutput").ap()
    rev = nc.dram_tensor("rev", (P, 4 * REV), F32, kind="Internal").ap()
    args["w_x"] = args.pop("x")
    build(nc, out=out, rev=rev, **args)
    r = run_bass_kernel_spmd(nc, [{f"in_{n}": a for n, a in arrays.items()}], core_ids=[0])
    return r.results[0]["out"].reshape(1, S, D)
```

```python
from contextlib import ExitStack

import numpy as np

import concourse.bass as bass
from concourse import mybir

F32 = mybir.dt.float32
F32R = mybir.dt.float32r
ALU = mybir.AluOpType
ACT = mybir.ActivationFunctionType
AX = mybir.AxisListType

P = 128
D = 1024
KD = D // P
S = 256
T = S // P
L = 2
INNER, GROUPS, STATE = 2048, 4, 128
HEADS = 32
HPG = HEADS // GROUPS
HD = INNER // HEADS
TAPS = 4
FFN = 2816
KF = FFN // P
EPS1, EPS2 = 1e-5, 1e-6
NEG = -1e30
SCALE = float(P) ** -0.5
PATTERNS = ((128, 1), (512, 4), (2048, 16))
NPAT = len(PATTERNS)
BUCKETS, MAX_DIST = 32, 2048
REV = S + P

RING = 3
CH = 2048
W_COLS = 512

TILES1 = ["B", "C", "x0", "k0", "v0", "x1", "z0", "q0", "x2", "z1", "q2", "x3", "z2", "q4", "z3",
          "gs0", "gs1", "k1", "v1", "q1", "q3", "q5", "ga0", "ga1"]
START1 = {"z": 0, "x": INNER, "B": 2 * INNER, "C": 2 * INNER + 512, "q": 5152, "k": 8224, "v": 9248,
          "gs": 10272, "ga": 11296}
DT_AT = 5120
NT1 = len(TILES1)
SSD_AT = 2 * NT1
ATT_AT = SSD_AT + INNER // 256
OUT_AT = ATT_AT + D // 256
GU_AT = OUT_AT + D // 256
NGU = FFN // 256
DOWN_AT = GU_AT + 2 * NGU
SINGLES = 4
DOWN_FULL = (KF - SINGLES) // 2
CHUNKS1 = DOWN_AT + DOWN_FULL + SINGLES
BLOCKS1 = DOWN_AT + KF // 2
assert CHUNKS1 % RING == 0
FULL1 = DOWN_AT + DOWN_FULL
PAIRED1 = (OUT_AT - 1, GU_AT - 1, CHUNKS1 - 1)

TILES2 = ["rk", "rq", "rv", "mk", "mq", "mv", "rz", "mz"]
START2 = {"rq": 0, "rk": 512, "rv": 1024, "rz": 1536, "mq": 2048, "mk": 2560, "mv": 3072, "mz": 3584}
NT2 = len(TILES2)
PLE_AT = 2 * NT2
SIZE2 = {PLE_AT: D, PLE_AT + 1: 512, PLE_AT + 2: 512}
OUT2_AT = PLE_AT + 3
GATE_AT = OUT2_AT + D // 256
CHUNKS2 = GATE_AT + D // 256
BLOCKS2 = CHUNKS2 - 2
assert CHUNKS2 % RING == 0
PAIRED2 = (GATE_AT - 1, CHUNKS2 - 1)
BASE2 = L * CHUNKS1

C_MIX, C_FFN, C_CW, C_CB, C_SN = 0, 8, 16, 112, 136
C_DTB, C_AL, C_DS, C_WDT = 152, 184, 216, 248
N_PAR1 = C_WDT + KD * HEADS
C_NG, C_YW, C_QN, C_KN, C_PT = 0, 8, 16, 17, 18
N_PAR2 = C_PT + 2 * S
N_PAR = max(N_PAR1, N_PAR2)

K_ID, K_TRI, K_LATER, K_MASK = 0, 128, 256, 384
K_ROPE1 = K_MASK + NPAT * S
K_KDEC = K_ROPE1 + 2 * T * 32
K_HEAD = K_KDEC + 4
N_CONST1 = K_HEAD + HEADS
K_ROPE2 = 0
K_DECAY = K_ROPE2 + 2 * T * P
K_QPOW = K_DECAY + 4 * P
N_CONST2 = K_QPOW + 4 * P

VCH1, SCH1 = 78, 8
VCH2, SCH2 = 23, 5


class Chain:

    def __init__(self, sem):
        self.sem, self.base, self.n = sem, 0, 0

    def start(self, base):
        self.base, self.n = base, 0

    def then(self, eng, ins):
        ins.then_inc(self.sem, 1)
        self.n += 1
        eng.wait_ge(self.sem, self.base + self.n)


class Signal:

    def __init__(self, sem, per):
        self.sem, self.per = sem, per

    def at(self, layer, n):
        return layer * self.per + n


def bc(ap, *shape):
    return ap.to_broadcast([P, *shape])


def build(nc, stream1, stream2, pars, const1, const2, onehot, relb, final_g, ple_g, w_x, out, rev):
    ctx = ExitStack()
    with ctx:
        def sb(name, shape, dt=F32):
            return ctx.enter_context(nc.sbuf_tensor(name, shape, dt))

        def sem(name):
            return ctx.enter_context(nc.semaphore(name))

        W = sb("w_raw", [P, RING, CH])
        WH = sb("w_high", [P, RING, CH], F32R)
        WL = sb("w_low", [P, RING, CH], F32R)
        h = sb("h", [P, T, D])
        uH = sb("u_high", [P, KD, S], F32R)
        uL = sb("u_low", [P, KD, S], F32R)
        b_at = nc.sbuf_base
        bH = sb("b_high", [P, 24, S], F32R)
        bL = sb("b_low", [P, 24, S], F32R)
        con_at = nc.sbuf_base
        con = sb("con", [P, N_CONST1])
        par = sb("par", [P, N_PAR])
        small = sb("small", [P, 1024])
        tri_r = nc.alloc_sbuf_tensor_at("tri_r", [P, P], F32R, offset=con_at + K_TRI * 4)
        later_r = nc.alloc_sbuf_tensor_at("later_r", [P, P], F32R, offset=con_at + K_LATER * 4)
        ident_r = sb("ident_r", [P, P], F32R)
        never_r = sb("never_r", [P, P], F32R)
        dtw_h = sb("dtw_h", [P, KD * HEADS], F32R)
        dtw_l = sb("dtw_l", [P, KD * HEADS], F32R)
        adt_h = sb("adt_h", [P, T * HEADS], F32R)
        adt_l = sb("adt_l", [P, T * HEADS], F32R)
        x_at = nc.sbuf_base
        X = sb("scratch", [P, 16384])
        ps = ctx.enter_context(nc.psum_tensor("ps", [P, 8, 512], F32))

        ident = con[:, K_ID:K_ID + P]
        tri = con[:, K_TRI:K_TRI + P]
        later = con[:, K_LATER:K_LATER + P]
        mask = con[:, K_MASK:K_MASK + NPAT * S].rearrange("p (g k) -> p g k", g=NPAT)
        rope_c = con[:, K_ROPE1:K_ROPE1 + T * 32].rearrange("p (t j) -> p t j", t=T)
        rope_s = con[:, K_ROPE1 + T * 32:K_ROPE1 + 2 * T * 32].rearrange("p (t j) -> p t j", t=T)

        head_of = con[:, K_HEAD:K_HEAD + HEADS]
        at = [0]

        def cut(n, start=None):
            if start is None:
                start, at[0] = at[0], at[0] + n
            return X[:, start:start + n]

        def early(name, part, tile, n, dt=F32):
            at_byte = b_at + (part * 24 + tile) * S * 4
            return nc.alloc_sbuf_tensor_at(name, [P, n], dt, offset=at_byte)

        xpad = early("xpad", 0, 8, 4 * (S + TAPS))[:, :].rearrange("p (j s) -> p j s", j=4)
        xdt = early("xdt", 0, 16, T * 512)[:, :].rearrange("p (t n) -> p t n", t=T)
        conv = early("conv", 0, 20, 4 * S)[:, :].rearrange("p (j s) -> p j s", j=4)
        EM = [early(f"ssd_decay{i}", 1, 16 + 4 * i, HPG * P)[:, :].rearrange("p (e l) -> p e l", e=HPG)
              for i in range(2)]
        DR = early("decay_rows", 1, 12, HPG * P, F32R)

        BC0 = cut(2048)
        BC = BC0.rearrange("p (j s) -> p j s", j=8)
        gate_s = BC0.rearrange("p (t n) -> p t n", t=T)
        Y0 = cut(2048)
        Y = [Y0[:, i * 1024:(i + 1) * 1024].rearrange("p (t n) -> p t n", t=T) for i in range(2)]
        gate_a = Y0.rearrange("p (t n) -> p t n", t=T)
        btok = cut(512).rearrange("p (g n) -> p g n", g=GROUPS)
        state = cut(512)
        xds = cut(512)
        yoff = cut(512)
        Q0 = cut(3072)
        qT = Q0.rearrange("p (g h s) -> p g h s", g=NPAT, h=4)
        sg = Q0[:, 0:1024].rearrange("p (i t n) -> p i t n", i=2, t=T)
        ac = Q0[:, 1024:2048].rearrange("p (i t n) -> p i t n", i=2, t=T)
        E_AT = at[0]
        E0 = cut(1536)
        dtT = E0[:, 1024:1280]
        cumT = E0[:, 1024:1024 + P]
        cum_hl = nc.alloc_sbuf_tensor_at("cum_high_low", [P, T, 2 * HEADS], F32R, offset=x_at + (E_AT + 1280) * 4)
        sc1, sc0 = E0[:, 0:768], E0[:, 768:1152]
        pT = E0[:, 1152:1536]
        V0 = cut(2048)
        ev = [V0[:, i * 1024:(i + 1) * 1024].rearrange("p (t n) -> p t n", t=T) for i in range(2)]
        ev.append(Y[0])
        colsF = V0.rearrange("p (j n) -> p j n", j=4)
        R0 = cut(2048)
        rows = R0.rearrange("p (t n) -> p t n", t=T)
        kT = R0[:, 0:1024].rearrange("p (h s) -> p h s", h=4)
        M0 = cut(1024)
        vv = [R0[:, 1024:2048].rearrange("p (t n) -> p t n", t=T),
              M0.rearrange("p (t n) -> p t n", t=T)]
        cbm = M0.rearrange("p (t g l) -> p t g l", t=T, g=GROUPS)
        rope_a = cut(256).rearrange("p (t h j) -> p t h j", t=T, h=4)
        rope_b = cut(256).rearrange("p (t h j) -> p t h j", t=T, h=4)
        used1 = at[0]

        at[0] = 0
        c2 = cut(N_CONST2)
        rot_c = c2[:, K_ROPE2:K_ROPE2 + T * P].rearrange("p (t j) -> p t j", t=T)
        rot_s = c2[:, K_ROPE2 + T * P:K_ROPE2 + 2 * T * P].rearrange("p (t j) -> p t j", t=T)
        decay = c2[:, K_DECAY:K_DECAY + 4 * P].rearrange("p (h n) -> p h n", h=4)
        qpow = c2[:, K_QPOW:K_QPOW + 4 * P].rearrange("p (h n) -> p h n", h=4)
        kdec_c = con[:, K_KDEC:K_KDEC + 4]
        bias = cut(4 * S).rearrange("p (h k) -> p h k", h=4)
        RK0 = cut(2048)
        rkT = RK0[:, 0:1024].rearrange("p (h s) -> p h s", h=4)
        rqT = RK0[:, 1024:2048].rearrange("p (h s) -> p h s", h=4)
        emb = RK0.rearrange("p (t n) -> p t n", t=T)
        rev_in = X[0:BUCKETS + 1, at[0]:at[0] + REV + 4]
        rev_rows = X[:, at[0] + 512:at[0] + 512 + 4 * REV].rearrange("p (h j) -> p h j", h=4)
        mkT = cut(1024).rearrange("p (h s) -> p h s", h=4)
        mqT = cut(1024).rearrange("p (h s) -> p h s", h=4)
        rv = cut(1024).rearrange("p (t n) -> p t n", t=T)
        mv = cut(1024).rearrange("p (t n) -> p t n", t=T)
        kdec = cut(512)
        qdT = cut(512).rearrange("p (h n) -> p h n", h=4)
        kvs = cut(512).rearrange("p (h n) -> p h n", h=4)
        sT = cut(1024).rearrange("p (t h n) -> p t h n", t=T, h=4)
        V2 = cut(2048)
        ev2 = [V2[:, i * 1024:(i + 1) * 1024].rearrange("p (t n) -> p t n", t=T) for i in range(2)]
        cols2 = V2.rearrange("p (j n) -> p j n", j=4)
        rt = cut(1024).rearrange("p (t n) -> p t n", t=T)
        rows2 = cut(2048).rearrange("p (t n) -> p t n", t=T)
        msc = early("block_scores", 0, 4, 4 * (S + P))
        msc1 = msc[:, 0:4 * S].rearrange("p (h k) -> p h k", h=4)
        msc0 = msc[:, 4 * S:4 * (S + P)].rearrange("p (h k) -> p h k", h=4)
        mpT = early("block_probs_t", 0, 10, 4 * (S + P))
        mpT1 = mpT[:, 0:4 * S].rearrange("p (h k) -> p h k", h=4)
        mpT0 = mpT[:, 4 * S:4 * (S + P)].rearrange("p (h k) -> p h k", h=4)
        sg2 = early("embed_gate", 0, 16, T * D)[:, :].rearrange("p (t n) -> p t n", t=T)
        ple_gain = early("ple_gain", 1, 4, D)[:, :]
        sq = early("squares", 1, 8, T * D)[:, :].rearrange("p (t n) -> p t n", t=T)
        assert max(used1, at[0]) <= 16384, (used1, at[0])

        sat = [0]

        def tiny(n):
            sat[0] += n
            return small[:, sat[0] - n:sat[0]]

        eps1, eps2 = tiny(1), tiny(1)
        ssum = tiny(T)
        rinv = tiny(T)
        gsum = tiny(T)
        ginv = tiny(T)
        dt = tiny(T * HEADS)
        dtx, dta, dte, dtu, dtd, dtz, dtl = (tiny(T * HEADS) for _ in range(7))
        nega = tiny(HEADS)
        adt = tiny(T * HEADS)
        acum = tiny(3 * HEADS)
        nacum = tiny(T * HEADS)
        spare = tiny(8)
        dec_in = tiny(HEADS)
        dec_out = tiny(HEADS)
        amax = tiny(T)
        anb = tiny(T)
        az = tiny(T)
        azi = tiny(T)
        head_ss = [tiny(T * 4) for _ in range(3)]
        head_mean = tiny(T * 4)
        mmax, mneg, mz = tiny(T * 4), tiny(T * 4), tiny(T * 4)
        ple_ss = tiny(T)
        assert sat[0] <= 1024

        w_loaded = [sem(f"w_loaded{i}") for i in range(RING)]
        high_ready = sem("high_ready")
        split_done = sem("split_done")
        products_done = sem("products_done")


        def signal(name, per):
            return Signal(sem(name), per)

        cols_ps = signal("cols_ps", 12)
        dtt_ps = signal("dtt_ps", 1)
        dt_ps = signal("dt_ps", 1)
        cumt_ps = signal("cumt_ps", 1)
        cum_ps = signal("cum_ps", 1)
        btok_ps = signal("btok_ps", 1)
        cb_ps = signal("cb_ps", 1)
        xt_ps = signal("xt_ps", GROUPS)
        row_ps = signal("row_ps", 2 * GROUPS)
        state_ps = signal("state_ps", GROUPS)
        yd_ps = signal("yd_ps", 2 * GROUPS)
        off_ps = signal("off_ps", GROUPS)
        yt_ps = signal("yt_ps", 2 * GROUPS)
        qk_ps = signal("qk_ps", 8)
        score_ps = signal("score_ps", 8)
        pt_ps = signal("pt_ps", 8)
        o_ps = signal("o_ps", 8)
        act_ps = signal("act_ps", NGU)
        t0_done = signal("t0_done", 4)
        tile_out = signal("tile_out", NT1)
        cols_high = signal("cols_high", 12)
        roots = signal("roots", 4)
        conv_act = signal("conv_act", 6)
        dt_steps = signal("dt_steps", 2)
        dtt_out = signal("dtt_out", 1)
        cumt_out = signal("cumt_out", 1)
        btok_out = signal("btok_out", 1)
        decays = signal("decays", 1)
        ssd_exp = signal("ssd_exp", 2 * GROUPS)
        state_out = signal("state_out", GROUPS)
        group_root = signal("group_root", GROUPS)
        y_high = signal("y_high", 2 * GROUPS)
        qk_out = signal("qk_out", 8)
        att_exp = signal("att_exp", 8)
        pt_out = signal("pt_out", 8)
        o_high = signal("o_high", 8)
        gate_act = signal("gate_act", NGU)
        act_high = signal("act_high", NGU)
        set_up = sem("set_up")
        h_ready = signal("h_ready", 4)
        rows_ready = signal("rows_ready", 6)
        cols_weighted = signal("cols_weighted", 8)
        cols_ready = signal("cols_ready", 12)
        dtw_ready = signal("dtw_ready", 1)
        dt_given = signal("dt_given", 2)
        adt_ready = signal("adt_ready", 1)
        cum_out = signal("cum_out", 1)
        cb_masked = signal("cb_masked", 1)
        xdt_ready = signal("xdt_ready", GROUPS)
        ssd_m = signal("ssd_m", 2 * GROUPS)
        ssd_y = signal("ssd_y", 2 * GROUPS)
        y_scaled = signal("y_scaled", GROUPS)
        y_weighted = signal("y_weighted", 2 * GROUPS)
        conv_done = signal("conv_done", 6)
        y_ready = signal("y_ready", 2 * GROUPS)
        roped = signal("roped", 8)
        att_masked = signal("att_masked", 8)
        att_p = signal("att_p", 8)
        o_ready = signal("o_ready", 8)
        ssd_gated = signal("ssd_gated", T)
        act_ready = signal("act_ready", NGU)
        act_rows = signal("act_rows", NGU)
        decay_rows = signal("decay_rows", GROUPS)
        xds_ready = signal("xds_ready", GROUPS)
        y_gated = signal("y_gated", GROUPS)
        cols2_ps = signal("cols2_ps", 12)
        ret_t_ps = signal("ret_t_ps", 2)
        rev_ps = sem("rev_ps")
        kv_ps = signal("kv_ps", 1)
        s_ps = signal("s_ps", 1)
        inner_ps = signal("inner_ps", 1)
        mo_t_ps = signal("mo_t_ps", 2)
        msc_ps = signal("msc_ps", 1)
        mpt_ps = signal("mpt_ps", 1)
        mo_ps = signal("mo_ps", 1)
        t0_done2 = signal("t0_done2", 2)
        final_root = sem("final_root")
        tile2_out = signal("tile2_out", NT2)
        cols2_high = signal("cols2_high", 12)
        roots2 = signal("roots2", 4)
        ret_t_out = signal("ret_t_out", 2)
        rev_out = sem("rev_out")
        kv_out = signal("kv_out", 1)
        ret_squared = signal("ret_squared", 1)
        head_root = signal("head_root", 3)
        m_exp = signal("m_exp", 1)
        mpt_out = signal("mpt_out", 1)
        emb_out = signal("emb_out", T)
        ple_root = signal("ple_root", 1)
        gate2_out = signal("gate2_out", T)
        h2_ready = signal("h2_ready", 4)
        rows2_ready = signal("rows2_ready", 6)
        cols2_weighted = signal("cols2_weighted", 8)
        cols2_ready = signal("cols2_ready", 12)
        ple_split = signal("ple_split", 1)
        rotated = signal("rotated", 2)
        s_decayed = signal("s_decayed", 1)
        head_sum = signal("head_sum", 3)
        normed = signal("normed", 3)
        mo_t_out = signal("mo_t_out", 2)
        centred = signal("centred", 1)
        m_masked = signal("m_masked", 1)
        emb_ready = signal("emb_ready", 1)
        kdec_ready = signal("kdec_ready", 1)
        qd_ready = signal("qd_ready", 1)
        ret_gated = signal("ret_gated", 1)
        final_loaded = sem("final_loaded")
        tables_loaded = sem("tables_loaded")
        gain_loaded = sem("gain_loaded")
        par_loaded = sem("par_loaded")
        h_loaded = sem("h_loaded")
        const_loaded = sem("const_loaded")
        rev_stored = sem("rev_stored")
        stored = sem("stored")
        rev_loaded = sem("rev_loaded")
        ones_ready = sem("ones_ready")
        bias_loaded = sem("bias_loaded")
        vector_chain, scalar_chain = Chain(sem("vector_chain")), Chain(sem("scalar_chain"))

        block = ctx.enter_context(nc.Block())

        XT = (2, 5, 8, 11)
        ZT = (6, 9, 12, 14)
        QK = (("k0", 3, 1, 15), ("q0", 7, 1, 21), ("q2", 10, 1, 27), ("q4", 13, 1, 33),
              ("k1", 17, 1, 44), ("q1", 19, 0, 46), ("q3", 20, 2, 46), ("q5", 21, 1, 47))
        QK_BANK = (6, 6, 6, 6, 4, 6, 4, 6)
        QK_OUT = (17, 23, 29, 35, 46, 48, 48, 49)
        CONV_AT = 4
        HEAD_AT = (36, 38, 40, 42, 48, 50, 52, 54)
        assert [TILES1.index(q[0]) for q in QK] == [q[1] for q in QK]
        assert all(TILES1[i] == f"x{g}" for g, i in enumerate(XT)) and all(TILES1[i] == f"z{g}" for g, i in enumerate(ZT))

        def tok(t):
            return slice(t * P, (t + 1) * P)

        def four(ap):
            return ap.rearrange("p (j n) -> p j n", j=4)

        @block.sync
        def _(sp):
            sp.dma_start(h[:, :, :], w_x.rearrange("(t p) n -> p t n", p=P)).then_inc(h_loaded, 16)

            def load(idx, slot, src, n):
                sp.wait_ge(split_done, idx + 1)
                sp.dma_start(W[:, slot, 0:n], src).then_inc(w_loaded[slot], 16)

            with sp.Fori(0, L) as l:
                with sp.Fori(0, 23) as r:
                    for j in range(RING):
                        load(l * CHUNKS1 + r * RING + j, j,
                             stream1[bass.ds((l * BLOCKS1 + r * RING + j) * P, P), :], CH)
                sp.wait_ge(cols_weighted.sem, cols_weighted.at(l, 8))
                sp.dma_start(par[:, :], pars[bass.ds((l + 1) * P, P), :]).then_inc(par_loaded, 16)
                with sp.Fori(0, 8) as r:
                    for j in range(RING):
                        load(l * CHUNKS1 + 69 + r * RING + j, j,
                             stream1[bass.ds((l * BLOCKS1 + 69 + r * RING + j) * P, P), :], CH)
                for c in range(93, CHUNKS1):
                    half = max(0, c - FULL1)
                    b, n, off = (c, CH, 0) if c < FULL1 else (FULL1 + half // 2, D, half % 2 * D)
                    load(l * CHUNKS1 + c, c % RING,
                         stream1[bass.ds((l * BLOCKS1 + b) * P, P), off:off + n], n)
            sp.wait_ge(rows_ready.sem, rows_ready.at(L - 1, 4))
            sp.dma_start(M0, final_g).then_inc(final_loaded, 16)
            sp.dma_start(c2, const2).then_inc(tables_loaded, 16)
            sp.dma_start(rev_in[:, 0:REV], onehot).then_inc(rev_loaded, 16)
            sp.dma_start(rev_in[:, REV:REV + 4], relb).then_inc(rev_loaded, 16)
            with sp.Fori(0, L) as l:
                with sp.Fori(0, PLE_AT // RING) as r:
                    for j in range(RING):
                        load(l * CHUNKS2 + BASE2 + r * RING + j, j,
                             stream2[bass.ds((l * BLOCKS2 + r * RING + j) * P, P), :], CH)
                for c in range(PLE_AT // RING * RING, CHUNKS2):
                    n = SIZE2.get(c, CH)
                    b, off = (c, 0) if c <= PLE_AT else (PLE_AT, D + (c - PLE_AT - 1) * 512) if c in SIZE2 else (c - 2, 0)
                    load(l * CHUNKS2 + BASE2 + c, c % RING,
                         stream2[bass.ds((l * BLOCKS2 + b) * P, P), off:off + n], n)
                    if c == GATE_AT + 1:
                        sp.wait_ge(cols2_weighted.sem, cols2_weighted.at(l, 8))
                        sp.dma_start(par[:, :], pars[bass.ds((l + L + 1) * P, P), :]).then_inc(par_loaded, 16)
            for t in range(T):
                sp.wait_ge(h2_ready.sem, h2_ready.at(L, t + 1))
                sp.dma_start(out[t * P:(t + 1) * P, :], h[:, t, :]).then_inc(stored, 16)
            sp.wait_ge(par_loaded, (2 * L + 1) * 16)
            sp.wait_ge(stored, T * 16)

        @block.tensor
        def _(pe):
            def products(o, hi, lo, whi, wlo, start, stop, **kw):
                nc.tensor.matmul(o, hi, whi, start=start, stop=False, **kw)
                nc.tensor.matmul(o, hi, wlo, start=False, stop=False, **kw)
                return nc.tensor.matmul(o, lo, whi, start=False, stop=stop, **kw)

            def turn(o, i):
                return nc.tensor.transpose(o, i, ident)

            pe.wait_ge(const_loaded, 16)
            pe.wait_ge(ones_ready, 1)

            def rows_to_cols(l, n, src):
                for t in range(T):
                    pe.wait_ge(rows_ready.sem, rows_ready.at(l, 2 * n + t + 1))
                    for q in range(2):
                        for j in range(4):
                            last = turn(ps[:, 4 + 2 * t + q, tok(j)], src[:, t, tok(4 * q + j)])
                        last.then_inc(cols_ps.sem, 1)

            def before(l, c):
                if c == 0:
                    rows_to_cols(l, 0, rows)
                    pe.wait_ge(dtw_ready.sem, dtw_ready.at(l, 1))
                    pe.wait_ge(cols_ready.sem, cols_ready.at(l, 4))
                    for k in range(KD):
                        w = slice(k * HEADS, (k + 1) * HEADS)
                        last = products(ps[0:HEADS, 4, 0:S], dtw_h[:, w], dtw_l[:, w], uH[:, k, :], uL[:, k, :],
                                        k == 0, k == KD - 1)
                    last.then_inc(dtt_ps.sem, 1)
                if c == 1:
                    pe.wait_ge(dtt_out.sem, dtt_out.at(l, 1))
                    for t in range(T):
                        last = nc.tensor.matmul(ps[:, 5, t * HEADS:(t + 1) * HEADS], dtT[0:HEADS, tok(t)],
                                                ident[0:HEADS, 0:HEADS], start=True, stop=True)
                    last.then_inc(dt_ps.sem, 1)
                if c == 3:
                    pe.wait_ge(adt_ready.sem, adt_ready.at(l, 1))
                    for i, (m, t) in enumerate(((tri_r, 0), (tri_r, 1), (later_r, 0))):
                        o, a = ps[:, 5, i * HEADS:(i + 1) * HEADS], slice(t * HEADS, (t + 1) * HEADS)
                        nc.tensor.matmul(o, m[:, :], adt_h[:, a], start=True, stop=False)
                        last = nc.tensor.matmul(o, m[:, :], adt_l[:, a], start=False, stop=True)
                    last.then_inc(cum_ps.sem, 1)
                if c == 6:
                    pe.wait_ge(cum_out.sem, cum_out.at(l, 1))
                    turn(ps[:, 5, 0:P], cum_hl[:, :, :].rearrange("p t n -> p (t n)").bitcast(F32)).then_inc(cumt_ps.sem, 1)
                if c == 8:
                    pe.wait_ge(conv_act.sem, conv_act.at(l, 2))
                    pe.wait_ge(dt_given.sem, dt_given.at(l, 1))
                    for g in range(GROUPS):
                        last = turn(ps[:, 4, tok(g)], BC[:, g, tok(0)])
                    last.then_inc(btok_ps.sem, 1)
                    for t in range(T):
                        for g in range(GROUPS):
                            last = nc.tensor.matmul(ps[:, 6 + t, tok(g)], BC[:, g, tok(t)], BC[:, 4 + g, tok(t)],
                                                    start=True, stop=True)
                    last.then_inc(cb_ps.sem, 1)
                for g, i in enumerate(XT):
                    if c == 2 * i + 5:
                        pe.wait_ge(conv_act.sem, conv_act.at(l, 3 + g))
                        if g == 0:
                            pe.wait_ge(btok_out.sem, btok_out.at(l, 1))
                            pe.wait_ge(cumt_out.sem, cumt_out.at(l, 1))
                        else:
                            pe.wait_ge(ssd_y.sem, ssd_y.at(l, 2 * g))
                        for t in range(T):
                            for j in range(4):
                                last = turn(ps[:, 4 + t, tok(j)], conv[:, j, tok(t)])
                        last.then_inc(xt_ps.sem, 1)
                    for t, at_c in ((0, 2 * i + 6), (1, 2 * i + 8)):
                        if c == at_c:
                            if t == 1:
                                pe.wait_ge(state_out.sem, state_out.at(l, g + 1))
                            elif g == 0:
                                pe.wait_ge(cb_masked.sem, cb_masked.at(l, 1))
                            else:
                                pe.wait_ge(ssd_y.sem, ssd_y.at(l, 2 * g))
                                pe.wait_ge(qk_out.sem, qk_out.at(l, g))
                            pe.wait_ge(decay_rows.sem, decay_rows.at(l, g + 1))
                            k = slice(t * 2 * HEADS, (t + 1) * 2 * HEADS)
                            ones = tri_r[k, P - 1:P].to_broadcast([2 * HEADS, P])
                            for b in range(2):
                                nc.tensor.matmul(four(ps[:, 6 + b, :]), ident_r[:, :], bc(never_r[:, :].unsqueeze(1), 4, P),
                                                 start=True, stop=False)
                                last = nc.tensor.matmul(ps[:, 6 + b, :], ones, DR[k, b * 512:(b + 1) * 512],
                                                        start=False, stop=True)
                            last.then_inc(row_ps.sem, 1)
                    if c == 2 * i + 7:
                        pe.wait_ge(xds_ready.sem, xds_ready.at(l, g + 1))
                        pe.wait_ge(ssd_exp.sem, ssd_exp.at(l, 2 * g + 1))
                        nc.tensor.matmul(ps[:, 6, :], btok[:, g, :], xds, start=True, stop=True).then_inc(state_ps.sem, 1)
                for g, i in enumerate(XT):
                    if c == 2 * i + 13:
                        pe.wait_ge(y_scaled.sem, y_scaled.at(l, g + 1))
                        if g < GROUPS - 1:
                            pe.wait_ge(xdt_ready.sem, xdt_ready.at(l, g + 2))
                        else:
                            pe.wait_ge(ssd_y.sem, ssd_y.at(l, 2 * GROUPS))
                        for t in range(T):
                            for j in range(4):
                                last = turn(ps[:, 4 + t, tok(j)], Y[g % 2][:, t, tok(j)])
                            last.then_inc(yt_ps.sem, 1)
                for g, i in enumerate(XT):
                    for t, at_c in ((0, 2 * i + 9), (1, 2 * i + 10)):
                        if c == at_c:
                            pe.wait_ge(ssd_m.sem, ssd_m.at(l, 2 * g + t + 1))
                            if g:
                                pe.wait_ge(y_weighted.sem, y_weighted.at(l, 2 * g))
                            for e in range(HPG):
                                last = nc.tensor.matmul(ps[:, 4 + t, e * HD:(e + 1) * HD], EM[t][:, e, :],
                                                        xdt[:, t, e * HD:(e + 1) * HD], start=True, stop=True)
                            last.then_inc(yd_ps.sem, 1)
                    if c == 2 * i + 10:
                        pe.wait_ge(ssd_exp.sem, ssd_exp.at(l, 2 * g + 2))
                        nc.tensor.matmul(ps[:, 7, :], BC[:, 4 + g, tok(1)], state, start=True, stop=True).then_inc(off_ps.sem, 1)
                for n, (name, i, e, at_c) in enumerate(QK):
                    if c == at_c:
                        pe.wait_ge(roped.sem, roped.at(l, n + 1))
                        b = QK_BANK[n]
                        if n < 4:
                            pe.wait_ge(ssd_y.sem, ssd_y.at(l, 2 * n + 2))
                        elif n == 4:
                            pe.wait_ge(att_masked.sem, att_masked.at(l, 4))
                        elif n == 5:
                            pe.wait_ge(o_ready.sem, o_ready.at(l, 4))
                        else:
                            pe.wait_ge(qk_out.sem, qk_out.at(l, n - 1))
                        for hh in range(4):
                            for t in range(T):
                                last = turn(ps[:, b + hh // 2, (hh % 2) * S + t * P:(hh % 2) * S + (t + 1) * P],
                                            ev[e][:, t, tok(hh)])
                        last.then_inc(qk_ps.sem, 1)
                for n, s in enumerate(HEAD_AT):
                    hh = n % 4
                    if c == s:
                        pe.wait_ge(qk_out.sem, qk_out.at(l, 4 if n < 4 else 8))
                        if n == 0:
                            pe.wait_ge(y_weighted.sem, y_weighted.at(l, 2 * GROUPS))
                        else:
                            pe.wait_ge(att_masked.sem, att_masked.at(l, n))
                        if n >= 2:
                            pe.wait_ge(o_ready.sem, o_ready.at(l, n - 1))
                        for g in range(NPAT):
                            nc.tensor.matmul(ps[:, 4 + g // 2, (g % 2) * S:(g % 2 + 1) * S], qT[:, g, hh, tok(1)],
                                             kT[:, hh, :], start=True, stop=True)
                            last = nc.tensor.matmul(ps[:, 6, tok(g)], qT[:, g, hh, tok(0)], kT[:, hh, tok(0)],
                                                    start=True, stop=True)
                        last.then_inc(score_ps.sem, 1)
                for n, s in enumerate(HEAD_AT):
                    hh = n % 4
                    if c == s + 2:
                        pe.wait_ge(att_p.sem, att_p.at(l, n + 1))
                        if n:
                            pe.wait_ge(pt_out.sem, pt_out.at(l, n))
                        turn(ps[:, 7, tok(0)], sc0[:, tok(0)])
                        turn(ps[:, 7, tok(1)], sc1[:, tok(0)])
                        turn(ps[:, 7, tok(2)], sc1[:, tok(1)]).then_inc(pt_ps.sem, 1)
                    if c == s + 3:
                        pe.wait_ge(pt_out.sem, pt_out.at(l, n + 1))
                        if hh < 3:
                            pe.wait_ge(att_masked.sem, att_masked.at(l, n + 2))
                        elif n:
                            pe.wait_ge(o_ready.sem, o_ready.at(l, n))
                        nc.tensor.matmul(ps[:, 6, 0:S], vv[n // 4][:, 0, tok(hh)], pT[:, 0:S], start=True, stop=False)
                        nc.tensor.matmul(ps[:, 6, P:S], vv[n // 4][:, 1, tok(hh)], pT[:, S:S + P], start=False,
                                         stop=True).then_inc(o_ps.sem, 1)
                if c == OUT_AT:
                    rows_to_cols(l, 1, rows)
                if c == GU_AT:
                    rows_to_cols(l, 2, rows)
                for j in range(NGU):
                    if c == GU_AT + 2 * j + 4:
                        pe.wait_ge(act_rows.sem, act_rows.at(l, j + 1))
                        if j >= 2:
                            pe.wait_ge(act_ready.sem, act_ready.at(l, j - 1))
                        for i in range(2):
                            for t in range(T):
                                last = turn(ps[:, 4 + j % 2, i * S + t * P:i * S + (t + 1) * P], ac[:, j % 2, t, tok(i)])
                        last.then_inc(act_ps.sem, 1)

            def by_rows(parts, banks, hi, lo, first, last_k, wait_for, t0_done):
                for t in range(T):
                    for slot, ks in parts:
                        wait_for(t, ks)
                        for half in range(2):
                            for kk, k in enumerate(ks):
                                w = slice(kk * D + half * 512, kk * D + half * 512 + 512)
                                last = products(ps[:, banks[2 * t + half], :], hi[:, k, tok(t)], lo[:, k, tok(t)],
                                                WH[:, slot, w], WL[:, slot, w], k == first, k == last_k)
                    if t == 0 and ks[-1] == last_k:
                        last.then_inc(t0_done.sem, 1)
                last.then_inc(products_done, len(parts))

            def tiles_of(c):
                if c < ATT_AT:
                    return 2 * (c - SSD_AT), 2 * (c - SSD_AT) + 1
                if c < OUT_AT:
                    return 16 + 2 * (c - ATT_AT), 17 + 2 * (c - ATT_AT)
                if c < GU_AT:
                    return 2 * (c - OUT_AT), 2 * (c - OUT_AT) + 1
                if c < FULL1:
                    return 2 * (c - DOWN_AT), 2 * (c - DOWN_AT) + 1
                return (2 * DOWN_FULL + c - FULL1,)

            def chunk(l, c):
                slot = c % RING
                if c + 1 in PAIRED1:
                    return
                parts = [(x % RING, tiles_of(x)) for x in ((c - 1, c) if c in PAIRED1 else (c,))] if c >= SSD_AT else None
                pe.wait_ge(split_done, l * CHUNKS1 + c + 1 + RING)
                if c < SSD_AT:
                    i, half = c // 2, c % 2
                    if i >= 2 and half == 0:
                        pe.wait_ge(tile_out.sem, tile_out.at(l, i - 1))
                    if c == 0:
                        pe.wait_ge(cols_ready.sem, cols_ready.at(l, 4))
                    b = 2 * (i % 2)
                    if TILES1[i][0] in "xBC":
                        for j in range(4):
                            for k in range(4):
                                w = slice(k * W_COLS + j * P, k * W_COLS + (j + 1) * P)
                                kk = 4 * half + k
                                o = ps[:, b + j // 2, (j % 2) * S:(j % 2 + 1) * S]
                                first = kk == 0 and j % 2 == 0
                                nc.tensor.matmul(o, WH[:, slot, w], uH[:, kk, :], start=first, stop=False, skip_group_check=True)
                                nc.tensor.matmul(o, WH[:, slot, w], uL[:, kk, :], start=False, stop=False, skip_group_check=True)
                                last = nc.tensor.matmul(o, WL[:, slot, w], uH[:, kk, :], start=False, stop=kk == KD - 1,
                                                        skip_group_check=True)
                    else:
                        for t in range(T):
                            for k in range(4):
                                w = slice(k * W_COLS, (k + 1) * W_COLS)
                                kk = 4 * half + k
                                last = products(ps[:, b + t, :], uH[:, kk, tok(t)], uL[:, kk, tok(t)], WH[:, slot, w],
                                                WL[:, slot, w], kk == 0, kk == KD - 1)
                elif c < ATT_AT:
                    def wait_for(t, ks):
                        if ks[0] == 0:
                            pe.wait_ge(tile_out.sem, tile_out.at(l, NT1 - 1 + t))
                        pe.wait_ge(y_ready.sem, y_ready.at(l, 2 * (ks[0] // 4) + t + 1))
                    by_rows(parts, (0, 1, 2, 3), bH, bL, 0, 15, wait_for, t0_done)
                elif c < OUT_AT:
                    def wait_for(t, ks):
                        if ks[0] == 16:
                            pe.wait_ge(ssd_gated.sem, ssd_gated.at(l, t + 1))
                        pe.wait_ge(o_ready.sem, o_ready.at(l, ks[1] - 15))
                    by_rows(parts, (0, 1, 2, 3), bH, bL, 16, 23, wait_for, t0_done)
                elif c < GU_AT:
                    def wait_for(t, ks):
                        pe.wait_ge(cols_ready.sem, cols_ready.at(l, 4 + 2 * t + ks[0] // 4 + 1))
                    by_rows(parts, (0, 1, 2, 3), uH, uL, 0, 7, wait_for, t0_done)
                elif c < DOWN_AT:
                    j, half = (c - GU_AT) // 2, (c - GU_AT) % 2
                    b = 2 * (j % 2)
                    if j >= 2 and half == 0:
                        pe.wait_ge(act_rows.sem, act_rows.at(l, j - 1))
                    for t in range(T):
                        if c == GU_AT:
                            pe.wait_ge(cols_ready.sem, cols_ready.at(l, 10 + 2 * t))
                        for k in range(4):
                            w = slice(k * W_COLS, (k + 1) * W_COLS)
                            kk = 4 * half + k
                            last = products(ps[:, b + t, :], uH[:, kk, tok(t)], uL[:, kk, tok(t)], WH[:, slot, w],
                                            WL[:, slot, w], kk == 0, kk == KD - 1)
                else:
                    def wait_for(t, ks):
                        if c == DOWN_AT and t == 1:
                            pe.wait_ge(act_rows.sem, act_rows.at(l, NGU - 1))
                        pe.wait_ge(act_ready.sem, act_ready.at(l, ks[-1] // 2 + 1))
                    by_rows(parts, (6, 7, 2, 3), bH, bL, 0, KF - 1, wait_for, t0_done)
                if c < SSD_AT or GU_AT <= c < DOWN_AT:
                    last.then_inc(products_done, 1)

            with pe.Fori(0, L) as l:
                for c in range(CHUNKS1):
                    before(l, c)
                    chunk(l, c)

            def heads_to_cols(o, src):
                for hh in range(4):
                    for t in range(T):
                        last = turn(ps[:, o + hh // 2, (hh % 2) * S + t * P:(hh % 2) * S + (t + 1) * P], src[:, t, tok(hh)])
                return last

            def rows2_to_cols(l, n):
                for t in range(T):
                    if n == 1:
                        pe.wait_ge(rows2_ready.sem, rows2_ready.at(l, 4))
                        pe.wait_ge(ret_gated.sem, ret_gated.at(l, 1))
                    else:
                        pe.wait_ge(rows2_ready.sem, rows2_ready.at(l, 2 * n + t + 1))
                    for q in range(2):
                        for j in range(4):
                            last = turn(ps[:, 4 + 2 * t + q, tok(j)], rows2[:, t, tok(4 * q + j)])
                        last.then_inc(cols2_ps.sem, 1)

            def before2(l, c):
                if c == 0:
                    rows2_to_cols(l, 0)
                if c == 5:
                    pe.wait_ge(rotated.sem, rotated.at(l, 1))
                    heads_to_cols(4, ev2[0]).then_inc(ret_t_ps.sem, 1)
                if c == 7:
                    pe.wait_ge(rotated.sem, rotated.at(l, 2))
                    heads_to_cols(6, ev2[1]).then_inc(ret_t_ps.sem, 1)
                if c == 9:
                    pe.wait_ge(kdec_ready.sem, kdec_ready.at(l, 1))
                    pe.wait_ge(ret_t_out.sem, ret_t_out.at(l, 1))
                    pe.wait_ge(tile2_out.sem, tile2_out.at(l, 3))
                    for hh in range(4):
                        last = nc.tensor.matmul(ps[:, 4, tok(hh)], kdec[:, tok(hh)], rv[:, 0, tok(hh)], start=True, stop=True)
                    last.then_inc(kv_ps.sem, 1)
                if c == 10:
                    pe.wait_ge(ret_t_out.sem, ret_t_out.at(l, 2))
                    for t in range(T):
                        for hh in range(4):
                            last = nc.tensor.matmul(ps[:, 6 + t, tok(hh)], rkT[:, hh, tok(t)], rqT[:, hh, tok(t)],
                                                    start=True, stop=True)
                    last.then_inc(s_ps.sem, 1)
                if c == 11:
                    pe.wait_ge(normed.sem, normed.at(l, 1))
                    pe.wait_ge(kv_out.sem, kv_out.at(l, 1))
                    heads_to_cols(4, ev2[1]).then_inc(mo_t_ps.sem, 1)
                if c == 12:
                    pe.wait_ge(normed.sem, normed.at(l, 2))
                    pe.wait_ge(s_decayed.sem, s_decayed.at(l, 1))
                    heads_to_cols(6, ev2[0]).then_inc(mo_t_ps.sem, 1)
                if c == 13:
                    pe.wait_ge(mo_t_out.sem, mo_t_out.at(l, 1))
                    pe.wait_ge(qd_ready.sem, qd_ready.at(l, 1))
                    for hh in range(4):
                        nc.tensor.matmul(ps[:, 4, tok(hh)], sT[:, 0, hh, :], rv[:, 0, tok(hh)], start=True, stop=True)
                        nc.tensor.matmul(ps[:, 5, tok(hh)], sT[:, 1, hh, :], rv[:, 1, tok(hh)], start=True, stop=False)
                        last = nc.tensor.matmul(ps[:, 5, tok(hh)], qdT[:, hh, :], kvs[:, hh, :], start=False, stop=True)
                    last.then_inc(inner_ps.sem, 1)
                if c == 14:
                    pe.wait_ge(mo_t_out.sem, mo_t_out.at(l, 2))
                    pe.wait_ge(centred.sem, centred.at(l, 1))
                    for hh in range(4):
                        nc.tensor.matmul(ps[:, 6 + hh // 2, (hh % 2) * S:(hh % 2 + 1) * S], mqT[:, hh, tok(1)], mkT[:, hh, :],
                                         start=True, stop=True)
                        last = nc.tensor.matmul(ps[:, 4, tok(hh)], mqT[:, hh, tok(0)], mkT[:, hh, tok(0)], start=True, stop=True)
                    last.then_inc(msc_ps.sem, 1)
                if c == 15:
                    pe.wait_ge(m_exp.sem, m_exp.at(l, 1))
                    for hh in range(4):
                        turn(ps[:, 5, tok(hh)], msc0[:, hh, :])
                        for k in range(T):
                            o = (hh % 2) * S + k * P
                            last = turn(ps[:, 6 + hh // 2, o:o + P], msc1[:, hh, tok(k)])
                    last.then_inc(mpt_ps.sem, 1)
                if c == 16:
                    pe.wait_ge(mpt_out.sem, mpt_out.at(l, 1))
                    for hh in range(4):
                        nc.tensor.matmul(ps[:, 4, tok(hh)], mpT0[:, hh, :], mv[:, 0, tok(hh)], start=True, stop=True)
                        for k in range(T):
                            last = nc.tensor.matmul(ps[:, 5, tok(hh)], mpT1[:, hh, tok(k)], mv[:, k, tok(hh)],
                                                    start=k == 0, stop=k == T - 1)
                    last.then_inc(mo_ps.sem, 1)
                if c == OUT2_AT:
                    rows2_to_cols(l, 1)
                if c == GATE_AT:
                    rows2_to_cols(l, 2)

            def chunk2(l, c):
                slot = c % RING
                if c + 1 in PAIRED2:
                    return
                k0 = OUT2_AT if c < GATE_AT else GATE_AT
                parts = [(x % RING, (2 * (x - k0), 2 * (x - k0) + 1)) for x in ((c - 1, c) if c in PAIRED2 else (c,))]
                pe.wait_ge(split_done, l * CHUNKS2 + (BASE2 + c + 1 + RING))
                if c < PLE_AT:
                    i, half = c // 2, c % 2
                    if i >= 2 and half == 0:
                        pe.wait_ge(tile2_out.sem, tile2_out.at(l, i - 1))
                    b = 2 * (i % 2)
                    for t in range(T):
                        if c == 0:
                            pe.wait_ge(cols2_ready.sem, cols2_ready.at(l, 2 + 2 * t))
                        for k in range(4):
                            w = slice(k * W_COLS, (k + 1) * W_COLS)
                            kk = 4 * half + k
                            last = products(ps[:, b + t, :], uH[:, kk, tok(t)], uL[:, kk, tok(t)], WH[:, slot, w],
                                            WL[:, slot, w], kk == 0, kk == KD - 1)
                elif c < OUT2_AT:
                    k = int(c > PLE_AT)
                    if c == PLE_AT:
                        pe.wait_ge(ple_split.sem, ple_split.at(l, 1))
                    for t in range(T):
                        if c == PLE_AT:
                            pe.wait_ge(tile2_out.sem, tile2_out.at(l, NT2 - 1 + t))
                        for half in ((0, 1) if c == PLE_AT else (c - PLE_AT - 1,)):
                            w = slice(half * 512, half * 512 + 512) if c == PLE_AT else slice(0, 512)
                            last = products(ps[:, 2 * t + half, :], bH[:, k, tok(t)], bL[:, k, tok(t)], WH[:, slot, w],
                                            WL[:, slot, w], k == 0, k == 1)
                elif c < GATE_AT:
                    def wait_for(t, ks):
                        if ks[0] == 0:
                            pe.wait_ge(emb_out.sem, emb_out.at(l, t + 1))
                        pe.wait_ge(cols2_ready.sem, cols2_ready.at(l, 4 + 2 * t + ks[0] // 4 + 1))
                    by_rows(parts, (0, 1, 2, 3), uH, uL, 0, 7, wait_for, t0_done2)
                else:
                    def wait_for(t, ks):
                        pe.wait_ge(cols2_ready.sem, cols2_ready.at(l, 8 + 2 * t + ks[0] // 4 + 1))
                    by_rows(parts, (0, 1, 2, 3), uH, uL, 0, 7, wait_for, t0_done2)
                if c < OUT2_AT:
                    last.then_inc(products_done, 1)

            pe.wait_ge(rev_loaded, 32)
            pe.wait_ge(act_rows.sem, act_rows.at(L - 1, NGU))
            pe.wait_ge(act_ready.sem, act_ready.at(L - 1, NGU))
            for hh in range(4):
                last = nc.tensor.matmul(ps[:, (0, 1, 4, 5)[hh], 0:REV], rev_in[:, REV + hh:REV + hh + 1].to_broadcast([BUCKETS + 1, P]),
                                        rev_in[:, 0:REV], start=True, stop=True)
            last.then_inc(rev_ps, 1)
            pe.wait_ge(rev_out, 1)

            with pe.Fori(0, L) as l:
                for c in range(CHUNKS2):
                    before2(l, c)
                    chunk2(l, c)

        @block.scalar
        def _(act):
            chain = scalar_chain

            def done(l, c, base=0):
                act.wait_ge(products_done, l * CHUNKS1 + c + 1 + RING)

            def split_high(l, c):
                n = CH if c < FULL1 else D
                act.wait_ge(w_loaded[c % RING], (l * (CHUNKS1 // RING) + c // RING + 1) * 16)
                act.wait_ge(products_done, l * CHUNKS1 + c + 1)
                nc.scalar.activation(WH[:, c % RING, 0:n], W[:, c % RING, 0:n], ACT.Copy).then_inc(high_ready, 1)

            def root_table(n):
                nc.scalar.activation(spare[:, n:n + 1], eps1, ACT.Sqrt)

            def stats(l, n, t):
                chain.then(act, nc.scalar.activation(rows[:, t, :], h[:, t, :], ACT.Square, accum_out=ssum[:, t:t + 1]))
                nc.scalar.activation(ssum[:, t:t + 1], ssum[:, t:t + 1], ACT.Sqrt, bias=eps1, scale=1.0 / D).then_inc(roots.sem, 1)

            def cols(l, n, src):
                for j in range(4):
                    if n == 1:
                        act.wait_ge(cols_ps.sem, cols_ps.at(l, 4 * n + j + 1))
                    else:
                        act.wait_ge(cols_weighted.sem, cols_weighted.at(l, 2 * n + j + 1))
                    t, q = j // 2, j % 2
                    nc.scalar.activation(uH[:, 4 * q:4 * q + 4, tok(t)], four(ps[:, 4 + j, :] if n == 1 else src[:, j, :]),
                                         ACT.Copy).then_inc(cols_high.sem, 1)

            act.dma_start(con[:, :], const1).then_inc(const_loaded, 16)
            act.dma_start(par[:, :], pars[0:P, :]).then_inc(par_loaded, 16)
            act.wait_ge(h_loaded, 16)
            act.wait_ge(set_up, 1)

            with act.Fori(0, L) as l:
                chain.start(l * SCH1)
                root_table(0)
                split_high(l, 0)
                for t in range(T):
                    act.wait_ge(h_ready.sem, h_ready.at(l, t + 1))
                    stats(l, 0, t)
                cols(l, 0, colsF)
                split_high(l, 1)
                act.wait_ge(dtt_ps.sem, dtt_ps.at(l, 1))
                nc.scalar.activation(dtT[0:HEADS, :], ps[0:HEADS, 4, 0:S], ACT.Copy).then_inc(dtt_out.sem, 1)
                split_high(l, 2)
                act.wait_ge(dt_given.sem, dt_given.at(l, 1))
                act.wait_ge(par_loaded, (l + 1) * 16)
                nc.scalar.activation(nega, par[:, C_AL:C_AL + HEADS], ACT.Exp)
                nc.scalar.activation(dte, dta, ACT.Exp, scale=-1.0).then_inc(dt_steps.sem, 1)
                act.wait_ge(dt_given.sem, dt_given.at(l, 2))
                nc.scalar.activation(dtl, dtu, ACT.Ln).then_inc(dt_steps.sem, 1)
                for c in range(3, CHUNKS1):
                    split_high(l, c)
                    if c == 5:
                        act.wait_ge(cum_out.sem, cum_out.at(l, 1))
                        nc.scalar.activation(dec_in, acum[:, HEADS:2 * HEADS], ACT.Exp)
                        nc.scalar.activation(dec_out, acum[:, 2 * HEADS:3 * HEADS], ACT.Exp).then_inc(decays.sem, 1)
                    for n, i in enumerate((0, 1) + XT):
                        if c == 2 * i + 6:
                            act.wait_ge(conv_done.sem, conv_done.at(l, n + 1))
                            o = BC[:, 4 * n:4 * n + 4, :] if n < 2 else conv
                            nc.scalar.activation(o, conv, ACT.Silu).then_inc(conv_act.sem, 1)
                    if c % 2 == 0 and c // 2 - 2 < NT1:
                        i = c // 2 - 2
                        done(l, 2 * i + 1)
                        two = ps[:, 2 * (i % 2):2 * (i % 2) + 2, :]
                        name = TILES1[i]
                        if name[0] in "xBC":
                            if i:
                                act.wait_ge(conv_done.sem, conv_done.at(l, {1: 1, 2: 2, 5: 3, 8: 4, 11: 5}[i]))
                            o, f = xpad[:, :, TAPS - 1:TAPS - 1 + S], ACT.Copy
                            two = two.rearrange("p b (j s) -> p (b j) s", j=2)
                        elif name[0] == "z":
                            g = int(name[1])
                            if g:
                                act.wait_ge(y_ready.sem, y_ready.at(l, 2 * g))
                            o, f = ev[0], ACT.Silu
                        elif name[:2] == "gs":
                            if name == "gs0":
                                act.wait_ge(off_ps.sem, off_ps.at(l, GROUPS))
                            o, f = gate_s[:, :, (i % 2 == 0) * 512:(i % 2 == 0) * 512 + 512], ACT.Sigmoid
                            assert (name == "gs1") == (i % 2 == 0)
                        elif name[:2] == "ga":
                            if name == "ga0":
                                act.wait_ge(qk_ps.sem, qk_ps.at(l, 7))
                            o, f = gate_a[:, :, int(name[2]) * 512:int(name[2]) * 512 + 512], ACT.Sigmoid
                        elif name[0] == "v":
                            o, f = vv[int(name[1])], ACT.Copy
                        else:
                            n = [q[0] for q in QK].index(name)
                            e = QK[n][2]
                            if n in (5, 6):
                                act.wait_ge(y_ready.sem, y_ready.at(l, 2 * GROUPS))
                            elif n in (1, 2, 3, 4):
                                act.wait_ge(qk_ps.sem, qk_ps.at(l, n))
                            elif n == 7:
                                act.wait_ge(qk_ps.sem, qk_ps.at(l, 5))
                            o, f = ev[e], ACT.Copy
                        nc.scalar.activation(o, two, f).then_inc(tile_out.sem, 1)
                    if c == 8:
                        act.wait_ge(cumt_ps.sem, cumt_ps.at(l, 1))
                        nc.scalar.activation(cumT, ps[:, 5, 0:P], ACT.Copy).then_inc(cumt_out.sem, 1)
                    if c == 10:
                        act.wait_ge(btok_ps.sem, btok_ps.at(l, 1))
                        nc.scalar.activation(btok, four(ps[:, 4, :]), ACT.Copy).then_inc(btok_out.sem, 1)
                    for n, at_c in enumerate(QK_OUT):
                        if c == at_c:
                            act.wait_ge(qk_ps.sem, qk_ps.at(l, n + 1))
                            name, b = QK[n][0], QK_BANK[n]
                            o = kT if name[0] == "k" else qT[:, int(name[1]) // 2]
                            nc.scalar.activation(o, ps[:, b:b + 2, :].rearrange("p b (j s) -> p (b j) s", j=2), ACT.Copy)\
                                .then_inc(qk_out.sem, 1)
                    for g, i in enumerate(XT):
                        if c == 2 * i + 8:
                            act.wait_ge(state_ps.sem, state_ps.at(l, g + 1))
                            if g:
                                act.wait_ge(off_ps.sem, off_ps.at(l, g))
                            nc.scalar.activation(state, ps[:, 6, :], ACT.Copy).then_inc(state_out.sem, 1)
                        for t, at_c in ((0, 2 * i + 7), (1, 2 * i + 9)):
                            if c == at_c:
                                act.wait_ge(row_ps.sem, row_ps.at(l, 2 * g + t + 1))
                                if g:
                                    act.wait_ge(yd_ps.sem, yd_ps.at(l, 2 * (g - 1) + t + 1))
                                for e in range(HPG):
                                    a = t * HEADS + g * HPG + e
                                    ins = nc.scalar.activation(EM[t][:, e, :], ps[:, 6 + e // 4, tok(e % 4)], ACT.Exp,
                                                               bias=nacum[:, a:a + 1])
                                ins.then_inc(ssd_exp.sem, 1)
                        if c == 2 * i + 13:
                            act.wait_ge(y_gated.sem, y_gated.at(l, g + 1))
                            for t in range(T):
                                ins = nc.scalar.activation(E0[:, t * 512:(t + 1) * 512], Y[g % 2][:, t, :], ACT.Square,
                                                           accum_out=gsum[:, t:t + 1])
                            chain.then(act, ins)
                            nc.scalar.activation(gsum, gsum, ACT.Sqrt, bias=eps1, scale=GROUPS / INNER).then_inc(group_root.sem, 1)
                        if c == 2 * i + 15:
                            for t in range(T):
                                act.wait_ge(y_weighted.sem, y_weighted.at(l, 2 * g + t + 1))
                                nc.scalar.activation(bH[:, 4 * g:4 * g + 4, tok(t)], four(ev[0][:, t, :]), ACT.Copy)\
                                    .then_inc(y_high.sem, 1)
                    for n, s in enumerate(HEAD_AT):
                        if c == s + 2:
                            act.wait_ge(att_masked.sem, att_masked.at(l, n + 1))
                            nc.scalar.activation(sc1, sc1, ACT.Exp, bias=anb[:, 1:2], scale=SCALE, accum_out=az[:, 1:2])
                            nc.scalar.activation(sc0, sc0, ACT.Exp, bias=anb[:, 0:1], scale=SCALE, accum_out=az[:, 0:1])\
                                .then_inc(att_exp.sem, 1)
                    for n, s in enumerate(HEAD_AT):
                        if c == s + 4:
                            act.wait_ge(pt_ps.sem, pt_ps.at(l, n + 1))
                            if n:
                                act.wait_ge(o_ps.sem, o_ps.at(l, n))
                            nc.scalar.activation(pT, ps[:, 7, 0:S + P], ACT.Copy).then_inc(pt_out.sem, 1)
                        if c == s + 5:
                            act.wait_ge(o_ps.sem, o_ps.at(l, n + 1))
                            nc.scalar.activation(bH[:, 16 + n, :], ps[:, 6, 0:S], ACT.Copy).then_inc(o_high.sem, 1)
                    if c == OUT_AT:
                        cols(l, 1, None)
                    if c == GU_AT:
                        root_table(1)
                        for t in range(T):
                            act.wait_ge(h_ready.sem, h_ready.at(l, t + 3))
                            stats(l, 2, t)
                        cols(l, 2, colsF)
                    for j in range(NGU):
                        if c == GU_AT + 2 * j + 4:
                            done(l, GU_AT + 2 * j + 1)
                            if j >= 2:
                                act.wait_ge(act_rows.sem, act_rows.at(l, j - 1))
                            b = 2 * (j % 2)
                            nc.scalar.activation(sg[:, j % 2], ps[:, b:b + 2, 0:256], ACT.Silu).then_inc(gate_act.sem, 1)
                        if c == GU_AT + 2 * j + 6:
                            act.wait_ge(act_ps.sem, act_ps.at(l, j + 1))
                            nc.scalar.activation(bH[:, 2 * j:2 * j + 2, :], ps[:, 4 + j % 2, :].rearrange("p (i s) -> p i s", i=2),
                                                 ACT.Copy).then_inc(act_high.sem, 1)
                assert chain.n == SCH1, chain.n

            root_table(2)
            for t in range(T):
                chain.start(L * SCH1 + t)
                act.wait_ge(h_ready.sem, L * 4 + t + 1)
                chain.then(act, nc.scalar.activation(sq[:, t, :], h[:, t, :], ACT.Square, accum_out=ssum[:, t:t + 1]))
                nc.scalar.activation(ssum[:, t:t + 1], ssum[:, t:t + 1], ACT.Sqrt, bias=eps1, scale=1.0 / D).then_inc(final_root, 1)

            act.wait_ge(rev_ps, 1)
            for b in range(2):
                ins = nc.scalar.activation(rev_rows[:, 2 * b:2 * b + 2, :], ps[:, 4 * b:4 * b + 2, 0:REV], ACT.Copy)
            ins.then_inc(rev_out, 1)
            act.wait_ge(rev_out, 1)
            act.dma_start(rev, rev_rows.rearrange("p h j -> p (h j)")).then_inc(rev_stored, 16)

            def split2_high(l, c):
                n = SIZE2.get(c, CH)
                act.wait_ge(w_loaded[c % RING], (l * (CHUNKS2 // RING) + (BASE2 // RING + c // RING + 1)) * 16)
                act.wait_ge(products_done, l * CHUNKS2 + (BASE2 + c + 1))
                nc.scalar.activation(WH[:, c % RING, 0:n], W[:, c % RING, 0:n], ACT.Copy).then_inc(high_ready, 1)

            def done2(l, c):
                act.wait_ge(products_done, l * CHUNKS2 + (BASE2 + c + 1 + RING))

            def stats2(l, n, t):
                chain.then(act, nc.scalar.activation(sq[:, t, :], h[:, t, :], ACT.Square, accum_out=ssum[:, t:t + 1]))
                nc.scalar.activation(ssum[:, t:t + 1], ssum[:, t:t + 1], ACT.Sqrt, bias=eps2, scale=1.0 / D).then_inc(roots2.sem, 1)

            def cols2_to_high(l, n, tiles=range(T)):
                for j in range(2 * tiles[0], 2 * tiles[-1] + 2):
                    t, q = j // 2, j % 2
                    if n == 2:
                        act.wait_ge(cols2_ps.sem, cols2_ps.at(l, 4 * n + j + 1))
                    else:
                        act.wait_ge(cols2_weighted.sem, cols2_weighted.at(l, 4 * n + j + 1))
                    nc.scalar.activation(uH[:, 4 * q:4 * q + 4, tok(t)], four(ps[:, 4 + j, :] if n == 2 else cols2[:, j, :]),
                                         ACT.Copy).then_inc(cols2_high.sem, 1)

            with act.Fori(0, L) as l:
                chain.start(l * SCH2 + L * SCH1 + T)
                root_table(3)
                split2_high(l, 0)
                for t in range(T):
                    act.wait_ge(h2_ready.sem, h2_ready.at(l, t + 1))
                    stats2(l, 0, t)
                act.dma_start(ple_gain, ple_g[bass.ds(l * P, P), :]).then_inc(gain_loaded, 16)
                cols2_to_high(l, 0)
                for c in range(1, CHUNKS2):
                    split2_high(l, c)
                    if c == 3:
                        act.wait_ge(rev_stored, 16)
                        act.dma_start(bias, bass.AP(rev.tensor, P - 1, [[4 * REV - 1, P], [REV, 4], [1, S]])).then_inc(bias_loaded, 16)
                    if c % 2 == 0 and 0 <= c // 2 - 2 < NT2:
                        i = c // 2 - 2
                        name = TILES2[i]
                        done2(l, 2 * i + 1)
                        two = ps[:, 2 * (i % 2):2 * (i % 2) + 2, :]
                        o, f = {"rk": (ev2[0], ACT.Copy), "rq": (ev2[1], ACT.Copy), "rv": (rv, ACT.Copy),
                                "mk": (ev2[1], ACT.Copy), "mq": (ev2[0], ACT.Copy), "mv": (mv, ACT.Copy),
                                "rz": (ev2[1], ACT.Silu), "mz": (ev2[0], ACT.Silu)}[name]
                        if name == "mk":
                            act.wait_ge(ret_t_ps.sem, ret_t_ps.at(l, 2))
                        elif name == "mq":
                            act.wait_ge(ret_t_ps.sem, ret_t_ps.at(l, 1))
                            act.wait_ge(kdec_ready.sem, kdec_ready.at(l, 1))
                        elif name in ("rz", "mz"):
                            act.wait_ge(mo_t_ps.sem, mo_t_ps.at(l, 1 + (name == "mz")))
                        ins = nc.scalar.activation(o, two, f)
                        if name in ("mk", "mq"):
                            q = name == "mq"
                            ins = nc.scalar.activation(sq[:, :, q * 512:q * 512 + 512], two, ACT.Square)
                        ins.then_inc(tile2_out.sem, 1)
                    for n, at_c in enumerate((7, 9)):
                        if c == at_c:
                            act.wait_ge(ret_t_ps.sem, ret_t_ps.at(l, n + 1))
                            b = 4 + 2 * n
                            nc.scalar.activation((rkT, rqT)[n], ps[:, b:b + 2, :].rearrange("p b (j s) -> p (b j) s", j=2), ACT.Copy)\
                                .then_inc(ret_t_out.sem, 1)
                    if c == 10:
                        act.wait_ge(kv_ps.sem, kv_ps.at(l, 1))
                        nc.scalar.activation(kvs, four(ps[:, 4, :]), ACT.Copy).then_inc(kv_out.sem, 1)
                    for n, at_c in enumerate((11, 13, 17)):
                        if c == at_c:
                            act.wait_ge(head_sum.sem, head_sum.at(l, n + 1))
                            nc.scalar.activation(head_ss[n], head_ss[n], ACT.Sqrt, bias=eps2, scale=1.0 / P).then_inc(head_root.sem, 1)
                    if c == 15:
                        act.wait_ge(centred.sem, centred.at(l, 1))
                        nc.scalar.activation(sq[:, :, 0:512], rt, ACT.Square).then_inc(ret_squared.sem, 1)
                    if c == 16:
                        act.wait_ge(m_masked.sem, m_masked.at(l, 1))
                        for t, m in ((0, msc0), (1, msc1)):
                            for hh in range(4):
                                a = 4 * t + hh
                                ins = nc.scalar.activation(m[:, hh, :], m[:, hh, :], ACT.Exp, bias=mneg[:, a:a + 1],
                                                           accum_out=mz[:, a:a + 1])
                        ins.then_inc(m_exp.sem, 1)
                    if c == 17:
                        act.wait_ge(mpt_ps.sem, mpt_ps.at(l, 1))
                        nc.scalar.activation(mpT0, four(ps[:, 5, :]), ACT.Copy)
                        nc.scalar.activation(mpT1, ps[:, 6:8, :].rearrange("p b (j s) -> p (b j) s", j=2), ACT.Copy).then_inc(mpt_out.sem, 1)
                    if c == OUT2_AT:
                        done2(l, OUT2_AT - 1)
                        for t in range(T):
                            nc.scalar.activation(emb[:, t, :], ps[:, 2 * t:2 * t + 2, :].rearrange("p b n -> p (b n)"), ACT.Copy)\
                                .then_inc(emb_out.sem, 1)
                            cols2_to_high(l, 1, (t,))
                    if c == OUT2_AT + 2:
                        for t in range(T):
                            act.wait_ge(emb_out.sem, emb_out.at(l, t + 1))
                            ins = nc.scalar.activation(sq[:, t, :], emb[:, t, :], ACT.Square, accum_out=ple_ss[:, t:t + 1])
                        chain.then(act, ins)
                        nc.scalar.activation(ple_ss, ple_ss, ACT.Sqrt, bias=eps2, scale=1.0 / D).then_inc(ple_root.sem, 1)
                    if c == GATE_AT:
                        root_table(4)
                        for t in range(T):
                            act.wait_ge(h2_ready.sem, h2_ready.at(l, t + 3))
                            stats2(l, 2, t)
                        cols2_to_high(l, 2)
                for t in range(T):
                    if t == 0:
                        act.wait_ge(t0_done2.sem, t0_done2.at(l, 2))
                    else:
                        done2(l, CHUNKS2 - 1)
                    nc.scalar.activation(sg2[:, t, :], ps[:, 2 * t:2 * t + 2, :].rearrange("p b n -> p (b n)"), ACT.Sigmoid)\
                        .then_inc(gate2_out.sem, 1)
                assert chain.n == SCH2, chain.n

        @block.gpsimd
        def _(pool):
            pool.wait_ge(const_loaded, 16)
            nc.gpsimd.tensor_copy(ident_r[:, :], ident)
            nc.gpsimd.tensor_scalar(never_r[:, :], later, NEG, None, ALU.mult)
            nc.gpsimd.tensor_copy(tri_r[:, :], tri)
            nc.gpsimd.tensor_copy(later_r[:, :], later).then_inc(ones_ready, 1)

            with pool.Fori(0, L) as l:
                def state_input(g):
                    pool.wait_ge(xdt_ready.sem, xdt_ready.at(l, g + 1))
                    if g:
                        pool.wait_ge(state_ps.sem, state_ps.at(l, g))
                    pool.wait_ge(decays.sem, decays.at(l, 1))
                    nc.gpsimd.tensor_tensor(out=xds.rearrange("p (e d) -> p e d", e=HPG),
                                            in0=xdt[:, 0, :].rearrange("p (e d) -> p e d", e=HPG),
                                            in1=bc(dec_out[:, g * HPG:(g + 1) * HPG].unsqueeze(2), HPG, HD),
                                            op=ALU.mult).then_inc(xds_ready.sem, 1)

                def gate(g):
                    pool.wait_ge(ssd_y.sem, ssd_y.at(l, 2 * g + 2))
                    pool.wait_ge(tile_out.sem, tile_out.at(l, ZT[g] + 1))
                    nc.gpsimd.tensor_tensor(out=Y[g % 2], in0=Y[g % 2], in1=ev[0], op=ALU.mult).then_inc(y_gated.sem, 1)

                def rows_of(g):
                    pool.wait_ge(cumt_out.sem, cumt_out.at(l, 1))
                    if g:
                        pool.wait_ge(row_ps.sem, row_ps.at(l, 2 * g))
                    nc.gpsimd.tensor_tensor(out=DR[:, :].rearrange("p (e l) -> p e l", e=HPG), in0=bc(cumT.unsqueeze(1), HPG, P),
                                            in1=bc(head_of[:, g * HPG:(g + 1) * HPG].unsqueeze(2), HPG, P),
                                            op=ALU.mult).then_inc(decay_rows.sem, 1)

                rows_of(0)
                for g in range(GROUPS):
                    state_input(g)
                    if g < GROUPS - 1:
                        rows_of(g + 1)
                    gate(g)

            def by_head(a):
                return a.rearrange("p (h n) -> p h n", h=4)

            pool.wait_ge(tables_loaded, 16)
            with pool.Fori(0, L) as l:
                pool.wait_ge(rotated.sem, rotated.at(l, 1))
                nc.gpsimd.tensor_tensor(out=by_head(kdec), in0=by_head(ev2[0][:, 0, :]), in1=bc(kdec_c.unsqueeze(2), 4, P),
                                        op=ALU.mult).then_inc(kdec_ready.sem, 1)
                pool.wait_ge(ret_t_out.sem, ret_t_out.at(l, 2))
                nc.gpsimd.tensor_tensor(out=qdT, in0=rqT[:, :, P:S], in1=qpow, op=ALU.mult).then_inc(qd_ready.sem, 1)
                pool.wait_ge(normed.sem, normed.at(l, 3))
                pool.wait_ge(tile2_out.sem, tile2_out.at(l, NT2 - 1))
                nc.gpsimd.tensor_tensor(out=rows2[:, :, 0:512], in0=rt, in1=ev2[1], op=ALU.mult).then_inc(ret_gated.sem, 1)

        @block.vector
        def _(dve):
            chain = vector_chain

            def tt(o, a, b, op):
                return nc.vector.tensor_tensor(out=o, in0=a, in1=b, op=op)

            def split_low(l, c):
                n = CH if c < FULL1 else D
                dve.wait_ge(high_ready, l * CHUNKS1 + c + 1)
                tt(WL[:, c % RING, 0:n], W[:, c % RING, 0:n], WH[:, c % RING, 0:n].bitcast(F32), ALU.subtract).then_inc(split_done, 1)

            def tile_done(l, t, n, c):
                if t == 0:
                    dve.wait_ge(t0_done.sem, t0_done.at(l, n + 1))
                else:
                    dve.wait_ge(products_done, l * CHUNKS1 + c + RING)

            def add_down(l, t):
                tile_done(l, t, 0, 0)
                b = 6 if t == 0 else 2
                tt(h[:, t, :], h[:, t, :], ps[:, b:b + 2, :].rearrange("p b n -> p (b n)"), ALU.add).then_inc(h_ready.sem, 1)

            def scaled_rows(l, n, t):
                dve.wait_ge(roots.sem, roots.at(l, n + t + 1))
                chain.then(dve, nc.vector.reciprocal(rinv[:, t:t + 1], ssum[:, t:t + 1]))
                nc.vector.tensor_scalar(rows[:, t, :], h[:, t, :], rinv[:, t:t + 1], None, ALU.mult).then_inc(rows_ready.sem, 1)

            def weighted(l, n, col, t):
                for j in (2 * t, 2 * t + 1):
                    dve.wait_ge(cols_ps.sem, cols_ps.at(l, 4 * n + j + 1))
                    q = j % 2
                    tt(four(colsF[:, j, :]), four(ps[:, 4 + j, :]),
                       bc(par[:, col + 4 * q:col + 4 * q + 4].unsqueeze(2), 4, P), ALU.mult).then_inc(cols_weighted.sem, 1)

            def cols_low(l, n, t):
                for j in (2 * t, 2 * t + 1):
                    dve.wait_ge(cols_high.sem, cols_high.at(l, 4 * n + j + 1))
                    t, q = j // 2, j % 2
                    src = ps[:, 4 + j, :] if n == 1 else colsF[:, j, :]
                    tt(uL[:, 4 * q:4 * q + 4, tok(t)], four(src), uH[:, 4 * q:4 * q + 4, tok(t)].bitcast(F32),
                       ALU.subtract).then_inc(cols_ready.sem, 1)

            def convolve(l, n):
                i = ((0, 1) + XT)[n]
                j0 = (16, 20, 0, 4, 8, 12)[n]
                dve.wait_ge(tile_out.sem, tile_out.at(l, i + 1))
                if n == 0:
                    chain.then(dve, nc.vector.memset(xpad[:, :, 0:TAPS - 1], 0.0))
                elif n <= 2:
                    dve.wait_ge(conv_act.sem, conv_act.at(l, n))
                else:
                    dve.wait_ge(xt_ps.sem, xt_ps.at(l, n - 2))
                for k in range(TAPS - 1, -1, -1):
                    for j in range(4):
                        w = C_CW + TAPS * (j0 + j) + k
                        if k == TAPS - 1:
                            ins = nc.vector.tensor_scalar(conv[:, j, :], xpad[:, j, k:k + S], par[:, w:w + 1],
                                                          par[:, C_CB + j0 + j:C_CB + j0 + j + 1], ALU.mult, ALU.add)
                        else:
                            ins = nc.vector.scalar_tensor_tensor(out=conv[:, j, :], in0=xpad[:, j, k:k + S],
                                                                 scalar=par[:, w:w + 1], in1=conv[:, j, :],
                                                                 op0=ALU.mult, op1=ALU.add)
                    if k:
                        chain.then(dve, ins)
                ins.then_inc(conv_done.sem, 1)

            nc.vector.memset(eps2, EPS2).then_inc(split_done, RING)
            nc.vector.memset(eps1, EPS1).then_inc(products_done, RING)
            nc.vector.memset(mneg, 0.0).then_inc(set_up, 1)
            nc.vector.memset(ps[:, 2:4, :], 0.0)
            nc.vector.memset(ps[:, 6:8, :], 0.0).then_inc(t0_done.sem, 1)
            dve.wait_ge(h_loaded, 16)

            with dve.Fori(0, L) as l:
                chain.start(l * VCH1)
                add_down(l, 0)
                split_low(l, 0)
                scaled_rows(l, 0, 0)
                add_down(l, 1)
                dve.wait_ge(par_loaded, (l + 1) * 16)
                weighted(l, 0, C_MIX, 0)
                scaled_rows(l, 0, 1)
                cols_low(l, 0, 0)
                weighted(l, 0, C_MIX, 1)
                cols_low(l, 0, 1)
                chain.then(dve, nc.vector.tensor_copy(dtw_h[:, :], par[:, C_WDT:C_WDT + KD * HEADS]))
                tt(dtw_l[:, :], par[:, C_WDT:C_WDT + KD * HEADS], dtw_h[:, :].bitcast(F32), ALU.subtract).then_inc(dtw_ready.sem, 1)
                split_low(l, 1)
                split_low(l, 2)
                dve.wait_ge(dt_ps.sem, dt_ps.at(l, 1))
                two = lambda a: a.rearrange("p (t n) -> p t n", t=T)
                chain.then(dve, tt(two(dtx), two(ps[:, 5, 0:T * HEADS]), bc(par[:, C_DTB:C_DTB + HEADS].unsqueeze(1), T, HEADS), ALU.add))
                nc.vector.scalar_tensor_tensor(out=dta, in0=dtx, scalar=-1.0, in1=dtx, op0=ALU.mult, op1=ALU.max).then_inc(dt_given.sem, 1)
                dve.wait_ge(dt_steps.sem, dt_steps.at(l, 1))
                chain.then(dve, nc.vector.tensor_scalar(dtu, dte, 1.0, None, ALU.add))
                chain.then(dve, nc.vector.tensor_scalar(dtd, dtu, -1.0, None, ALU.add))
                chain.then(dve, nc.vector.tensor_scalar(dtz, dtd, 0.0, None, ALU.is_equal))
                chain.then(dve, tt(dtd, dtd, dtz, ALU.add))
                nc.vector.reciprocal(dtd, dtd).then_inc(dt_given.sem, 1)
                dve.wait_ge(dt_steps.sem, dt_steps.at(l, 2))
                chain.then(dve, tt(dtl, dtl, dtz, ALU.add))
                chain.then(dve, tt(dtl, dtl, dtd, ALU.mult))
                chain.then(dve, tt(dtl, dtl, dte, ALU.mult))
                chain.then(dve, nc.vector.scalar_tensor_tensor(out=dt, in0=dtx, scalar=0.0, in1=dtl, op0=ALU.max, op1=ALU.add))
                chain.then(dve, nc.vector.scalar_tensor_tensor(out=two(adt), in0=two(dt), scalar=-1.0, in1=bc(nega.unsqueeze(1), T, HEADS),
                                                               op0=ALU.mult, op1=ALU.mult))
                chain.then(dve, nc.vector.tensor_copy(adt_h[:, :], adt))
                tt(adt_l[:, :], adt, adt_h[:, :].bitcast(F32), ALU.subtract).then_inc(adt_ready.sem, 1)

                for c in range(3, CHUNKS1):
                    split_low(l, c)
                    if c == 5:
                        dve.wait_ge(cum_ps.sem, cum_ps.at(l, 1))
                        nc.vector.tensor_scalar(nacum, ps[:, 5, 0:T * HEADS], -1.0, None, ALU.mult)
                        nc.vector.tensor_copy(acum, ps[:, 5, 0:3 * HEADS])
                        chain.then(dve, nc.vector.tensor_copy(cum_hl[:, :, 0:HEADS], two(ps[:, 5, 0:T * HEADS])))
                        tt(cum_hl[:, :, HEADS:2 * HEADS], two(ps[:, 5, 0:T * HEADS]), cum_hl[:, :, 0:HEADS].bitcast(F32), ALU.subtract)\
                            .then_inc(cum_out.sem, 1)
                    if c == 10:
                        dve.wait_ge(cb_ps.sem, cb_ps.at(l, 1))
                        for t in range(T):
                            ins = tt(cbm[:, t], four(ps[:, 6 + t, :]), bc(tri_r[:, :].bitcast(F32).unsqueeze(1), GROUPS, P), ALU.mult)
                        ins.then_inc(cb_masked.sem, 1)
                    for g, i in enumerate(XT):
                        hs = slice(g * HPG, (g + 1) * HPG)
                        y = Y[g % 2]

                        def heads(a):
                            return a.rearrange("p (e d) -> p e d", e=HPG)
                        if c == 2 * i + 7:
                            dve.wait_ge(xt_ps.sem, xt_ps.at(l, g + 1))
                            if g:
                                dve.wait_ge(yd_ps.sem, yd_ps.at(l, 2 * g))
                            for t in range(T):
                                tt(heads(y[:, t, :]), heads(ps[:, 4 + t, :]),
                                   bc(par[:, C_DS + g * HPG:C_DS + (g + 1) * HPG].unsqueeze(2), HPG, HD), ALU.mult)
                                ins = tt(heads(xdt[:, t, :]), heads(ps[:, 4 + t, :]),
                                         bc(dt[:, t * HEADS + g * HPG:t * HEADS + (g + 1) * HPG].unsqueeze(2), HPG, HD), ALU.mult)
                            ins.then_inc(xdt_ready.sem, 1)
                        for t, at_c in ((0, 2 * i + 8), (1, 2 * i + 10)):
                            if c == at_c:
                                dve.wait_ge(ssd_exp.sem, ssd_exp.at(l, 2 * g + t + 1))
                                tt(EM[t], EM[t], bc(cbm[:, t, g, :].unsqueeze(1), HPG, P), ALU.mult).then_inc(ssd_m.sem, 1)
                        if c == 2 * i + 11:
                            dve.wait_ge(yd_ps.sem, yd_ps.at(l, 2 * g + 1))
                            tt(y[:, 0, :], y[:, 0, :], ps[:, 4, :], ALU.add).then_inc(ssd_y.sem, 1)
                        if c == 2 * i + 12:
                            dve.wait_ge(yd_ps.sem, yd_ps.at(l, 2 * g + 2))
                            tt(y[:, 1, :], y[:, 1, :], ps[:, 5, :], ALU.add)
                            dve.wait_ge(off_ps.sem, off_ps.at(l, g + 1))
                            dve.wait_ge(decays.sem, decays.at(l, 1))
                            chain.then(dve, tt(heads(yoff), heads(ps[:, 7, :]), bc(dec_in[:, hs].unsqueeze(2), HPG, HD), ALU.mult))
                            tt(y[:, 1, :], y[:, 1, :], yoff, ALU.add).then_inc(ssd_y.sem, 1)
                        if c == 2 * i + 13:
                            dve.wait_ge(group_root.sem, group_root.at(l, g + 1))
                            chain.then(dve, nc.vector.reciprocal(ginv, gsum))
                            for t in range(T):
                                ins = nc.vector.tensor_scalar(y[:, t, :], y[:, t, :], ginv[:, t:t + 1], None, ALU.mult)
                            ins.then_inc(y_scaled.sem, 1)
                        if c == 2 * i + 15:
                            for t in range(T):
                                dve.wait_ge(yt_ps.sem, yt_ps.at(l, 2 * g + t + 1))
                                tt(four(ev[0][:, t, :]), four(ps[:, 4 + t, :]),
                                   bc(par[:, C_SN + 4 * g:C_SN + 4 * g + 4].unsqueeze(2), 4, P), ALU.mult).then_inc(y_weighted.sem, 1)
                            for t in range(T):
                                dve.wait_ge(y_high.sem, y_high.at(l, 2 * g + t + 1))
                                tt(bL[:, 4 * g:4 * g + 4, tok(t)], four(ev[0][:, t, :]), bH[:, 4 * g:4 * g + 4, tok(t)].bitcast(F32),
                                   ALU.subtract).then_inc(y_ready.sem, 1)
                    for n, i in enumerate((0, 1) + XT):
                        if c == 2 * i + CONV_AT:
                            convolve(l, n)
                    for n, (name, i, e, _) in enumerate(QK):
                        if c == 2 * i + 5:
                            dve.wait_ge(tile_out.sem, tile_out.at(l, i + 1))
                            for_h = ev[e].rearrange("p t (h j) -> p t h j", h=4)
                            half = 16
                            for t in range(T):
                                xx = for_h[:, t]
                                tt(rope_a[:, t], xx[:, :, 0:32], bc(rope_c[:, t, :].unsqueeze(1), 4, 32), ALU.mult)
                                tt(rope_b[:, t, :, 0:half], xx[:, :, half:32], bc(rope_s[:, t, 0:half].unsqueeze(1), 4, half), ALU.mult)
                                ins = tt(rope_b[:, t, :, half:32], xx[:, :, 0:half], bc(rope_s[:, t, half:32].unsqueeze(1), 4, half), ALU.mult)
                            chain.then(dve, ins)
                            for t in range(T):
                                ins = tt(for_h[:, t, :, 0:32], rope_a[:, t], rope_b[:, t], ALU.add)
                            ins.then_inc(roped.sem, 1)
                    for n, s in enumerate(HEAD_AT):
                        if c == s + 3:
                            dve.wait_ge(att_exp.sem, att_exp.at(l, n + 1))
                            tt(sc1[:, 0:S], sc1[:, 0:S], sc1[:, S:2 * S], ALU.add)
                            tt(sc0[:, 0:P], sc0[:, 0:P], sc0[:, P:2 * P], ALU.add)
                            chain.then(dve, nc.vector.reciprocal(azi, az))
                            tt(sc1[:, 0:S], sc1[:, 0:S], sc1[:, 2 * S:3 * S], ALU.add)
                            chain.then(dve, tt(sc0[:, 0:P], sc0[:, 0:P], sc0[:, 2 * P:3 * P], ALU.add))
                            nc.vector.tensor_scalar(sc1[:, 0:S], sc1[:, 0:S], azi[:, 1:2], None, ALU.mult)
                            nc.vector.tensor_scalar(sc0[:, 0:P], sc0[:, 0:P], azi[:, 0:1], None, ALU.mult).then_inc(att_p.sem, 1)
                    for n, s in enumerate(HEAD_AT):
                        if c == s + 2:
                            dve.wait_ge(set_up, 1)
                            dve.wait_ge(score_ps.sem, score_ps.at(l, n + 1))
                            if n:
                                dve.wait_ge(pt_ps.sem, pt_ps.at(l, n))
                            m1 = mask.rearrange("p g k -> p (g k)")
                            nc.vector.tensor_tensor_reduce(out=sc1, in0=ps[:, 4:6, :].rearrange("p b k -> p (b k)")[:, 0:768], in1=m1,
                                                           scale=1.0, scalar=NEG, op0=ALU.add, op1=ALU.max, accum_out=amax[:, 1:2])
                            chain.then(dve, nc.vector.tensor_tensor_reduce(
                                out=sc0.rearrange("p (g k) -> p g k", g=NPAT), in0=ps[:, 6, 0:384].rearrange("p (g k) -> p g k", g=NPAT),
                                in1=mask[:, :, P:S], scale=1.0, scalar=NEG, op0=ALU.add, op1=ALU.max, accum_out=amax[:, 0:1]))
                            nc.vector.tensor_scalar(anb, amax, -SCALE, None, ALU.mult).then_inc(att_masked.sem, 1)
                        if c == s + 5:
                            dve.wait_ge(o_high.sem, o_high.at(l, n + 1))
                            tt(bL[:, 16 + n, :], ps[:, 6, 0:S], bH[:, 16 + n, :].bitcast(F32), ALU.subtract).then_inc(o_ready.sem, 1)
                    if c == ATT_AT + 1:
                        for t in range(T):
                            tile_done(l, t, 1, ATT_AT)
                            tt(gate_s[:, t, :], gate_s[:, t, :], ps[:, 2 * t:2 * t + 2, :].rearrange("p b n -> p (b n)"), ALU.mult)\
                                .then_inc(ssd_gated.sem, 1)
                    if c == OUT_AT:
                        for t in range(T):
                            tile_done(l, t, 2, OUT_AT)
                            chain.then(dve, tt(gate_a[:, t, :], gate_a[:, t, :], ps[:, 2 * t:2 * t + 2, :].rearrange("p b n -> p (b n)"), ALU.mult))
                            tt(rows[:, t, :], gate_a[:, t, :], gate_s[:, t, :], ALU.add).then_inc(rows_ready.sem, 1)
                        for t in range(T):
                            cols_low(l, 1, t)
                    if c == GU_AT:
                        for t in range(T):
                            tile_done(l, t, 3, GU_AT)
                            tt(h[:, t, :], h[:, t, :], ps[:, 2 * t:2 * t + 2, :].rearrange("p b n -> p (b n)"), ALU.add)\
                                .then_inc(h_ready.sem, 1)
                            if t == 0:
                                scaled_rows(l, 2, 0)
                        weighted(l, 2, C_FFN, 0)
                        scaled_rows(l, 2, 1)
                        cols_low(l, 2, 0)
                        weighted(l, 2, C_FFN, 1)
                        cols_low(l, 2, 1)
                    for j in range(NGU):
                        if c == GU_AT + 2 * j + 4:
                            dve.wait_ge(gate_act.sem, gate_act.at(l, j + 1))
                            if j >= 2:
                                dve.wait_ge(act_ps.sem, act_ps.at(l, j - 1))
                            b = 2 * (j % 2)
                            tt(ac[:, j % 2], sg[:, j % 2], ps[:, b:b + 2, 256:512], ALU.mult).then_inc(act_rows.sem, 1)
                        if c == GU_AT + 2 * j + 6:
                            dve.wait_ge(act_high.sem, act_high.at(l, j + 1))
                            tt(bL[:, 2 * j:2 * j + 2, :], ps[:, 4 + j % 2, :].rearrange("p (i s) -> p i s", i=2),
                               bH[:, 2 * j:2 * j + 2, :].bitcast(F32), ALU.subtract).then_inc(act_ready.sem, 1)
                assert chain.n == VCH1, chain.n

            dve.wait_ge(final_loaded, 16)
            for t in range(T):
                add_down(L, t)
            for t in range(T):
                dve.wait_ge(final_root, t + 1)
                chain.start(L * VCH1 + t)
                chain.then(dve, nc.vector.reciprocal(rinv[:, t:t + 1], ssum[:, t:t + 1]))
                nc.vector.scalar_tensor_tensor(out=h[:, t, :], in0=h[:, t, :], scalar=rinv[:, t:t + 1], in1=M0,
                                               op0=ALU.mult, op1=ALU.mult).then_inc(h2_ready.sem, 1)
            dve.wait_ge(tables_loaded, 16)

            def heads8(a):
                return a.rearrange("p t (h n) -> p t h n", h=4)

            def by_head(a):
                return a.rearrange("p (t h) -> p t h", t=T)

            def split2_low(l, c):
                n = SIZE2.get(c, CH)
                dve.wait_ge(high_ready, l * CHUNKS2 + (BASE2 + c + 1))
                tt(WL[:, c % RING, 0:n], W[:, c % RING, 0:n], WH[:, c % RING, 0:n].bitcast(F32), ALU.subtract).then_inc(split_done, 1)

            def scaled_rows2(l, n, t):
                dve.wait_ge(roots2.sem, roots2.at(l, n + t + 1))
                chain.then(dve, nc.vector.reciprocal(rinv[:, t:t + 1], ssum[:, t:t + 1]))
                nc.vector.tensor_scalar(rows2[:, t, :], h[:, t, :], rinv[:, t:t + 1], None, ALU.mult).then_inc(rows2_ready.sem, 1)

            def weighted2(l, n, col, t):
                for j in (2 * t, 2 * t + 1):
                    dve.wait_ge(cols2_ps.sem, cols2_ps.at(l, 4 * n + j + 1))
                    q = j % 2
                    tt(four(cols2[:, j, :]), four(ps[:, 4 + j, :]),
                       bc(par[:, col + 4 * q:col + 4 * q + 4].unsqueeze(2), 4, P), ALU.mult).then_inc(cols2_weighted.sem, 1)

            def cols2_to_low(l, n, t):
                for j in (2 * t, 2 * t + 1):
                    dve.wait_ge(cols2_high.sem, cols2_high.at(l, 4 * n + j + 1))
                    t, q = j // 2, j % 2
                    src = ps[:, 4 + j, :] if n == 2 else cols2[:, j, :]
                    tt(uL[:, 4 * q:4 * q + 4, tok(t)], four(src), uH[:, 4 * q:4 * q + 4, tok(t)].bitcast(F32),
                       ALU.subtract).then_inc(cols2_ready.sem, 1)

            def normalised(l, n, src):
                dve.wait_ge(head_root.sem, head_root.at(l, n + 1))
                chain.then(dve, nc.vector.reciprocal(head_ss[n], head_ss[n]))
                tt(heads8(src), heads8(src), bc(by_head(head_ss[n]).unsqueeze(3), T, 4, P), ALU.mult).then_inc(normed.sem, 1)

            with dve.Fori(0, L) as l:
                chain.start(l * VCH2 + L * VCH1 + T)
                split2_low(l, 0)
                scaled_rows2(l, 0, 0)
                scaled_rows2(l, 0, 1)
                dve.wait_ge(par_loaded, (l + L + 1) * 16)
                for t in range(T):
                    weighted2(l, 0, C_NG, t)
                    cols2_to_low(l, 0, t)
                pt = par[:, C_PT:C_PT + 2 * S].rearrange("p (k s) -> p k s", k=2)
                chain.then(dve, nc.vector.tensor_copy(bH[:, 0:2, :], pt))
                tt(bL[:, 0:2, :], pt, bH[:, 0:2, :].bitcast(F32), ALU.subtract).then_inc(ple_split.sem, 1)
                for c in range(1, CHUNKS2):
                    split2_low(l, c)
                    for n, at_c in enumerate((5, 7)):
                        if c == at_c:
                            dve.wait_ge(tile2_out.sem, tile2_out.at(l, n + 1))
                            half = P // 2
                            for t in range(T):
                                xx, rr = four(ev2[n][:, t, :]), four(rt[:, t, :])
                                tt(rr[:, :, 0:half], xx[:, :, half:P], bc(rot_s[:, t, 0:half].unsqueeze(1), 4, half), ALU.mult)
                                chain.then(dve, tt(rr[:, :, half:P], xx[:, :, 0:half], bc(rot_s[:, t, half:P].unsqueeze(1), 4, half), ALU.mult))
                                chain.then(dve, tt(xx, xx, bc(rot_c[:, t, :].unsqueeze(1), 4, P), ALU.mult))
                                ins = tt(xx, xx, rr, ALU.add)
                            ins.then_inc(rotated.sem, 1)
                    if c == 12:
                        dve.wait_ge(s_ps.sem, s_ps.at(l, 1))
                        for t in range(T):
                            ins = tt(sT[:, t], four(ps[:, 6 + t, :]), decay, ALU.mult)
                        ins.then_inc(s_decayed.sem, 1)
                    for n, at_c in enumerate((10, 12)):
                        if c == at_c:
                            dve.wait_ge(tile2_out.sem, tile2_out.at(l, 4 + n))
                            nc.vector.tensor_reduce(out=by_head(head_ss[n]), in_=heads8(sq[:, :, n * 512:n * 512 + 512]), axis=AX.X,
                                                    op=ALU.add).then_inc(head_sum.sem, 1)
                    for n, at_c in enumerate((11, 13)):
                        if c == at_c:
                            normalised(l, n, ev2[1 - n])
                    for n, at_c in enumerate((13, 14)):
                        if c == at_c:
                            dve.wait_ge(mo_t_ps.sem, mo_t_ps.at(l, n + 1))
                            src = ps[:, 4 + 2 * n:6 + 2 * n, :].rearrange("p b (j s) -> p (b j) s", j=2)
                            gain = par[:, C_KN:C_KN + 1] if n == 0 else par[:, C_QN:C_QN + 1]
                            nc.vector.tensor_scalar((mkT, mqT)[n], src, gain, 1.0 if n == 0 else SCALE, ALU.mult, ALU.mult)\
                                .then_inc(mo_t_out.sem, 1)
                    if c == 14:
                        dve.wait_ge(bias_loaded, (l + 1) * 16)
                        dve.wait_ge(inner_ps.sem, inner_ps.at(l, 1))
                        chain.then(dve, nc.vector.tensor_reduce(out=by_head(head_mean), in_=heads8(ps[:, 4:6, :]), axis=AX.X, op=ALU.add))
                        chain.then(dve, nc.vector.tensor_scalar(head_mean, head_mean, -1.0 / P, None, ALU.mult))
                        tt(heads8(rt), heads8(ps[:, 4:6, :]), bc(by_head(head_mean).unsqueeze(3), T, 4, P), ALU.add).then_inc(centred.sem, 1)
                    if c == 15:
                        dve.wait_ge(set_up, 1)
                        dve.wait_ge(msc_ps.sem, msc_ps.at(l, 1))
                        for t in range(T):
                            for hh in range(4):
                                a = 4 * t + hh
                                o, b, i = ((msc0[:, hh, :], bias[:, hh, P:S], ps[:, 4, tok(hh)]),
                                           (msc1[:, hh, :], bias[:, hh, :], ps[:, 6 + hh // 2, (hh % 2) * S:(hh % 2 + 1) * S]))[t]
                                ins = nc.vector.tensor_tensor_reduce(out=o, in0=i, in1=b, scale=1.0, scalar=NEG, op0=ALU.add,
                                                                     op1=ALU.max, accum_out=mmax[:, a:a + 1])
                        chain.then(dve, ins)
                        nc.vector.tensor_scalar(mneg, mmax, -1.0, None, ALU.mult).then_inc(m_masked.sem, 1)
                    if c == 16:
                        dve.wait_ge(ret_squared.sem, ret_squared.at(l, 1))
                        nc.vector.tensor_reduce(out=by_head(head_ss[2]), in_=heads8(sq[:, :, 0:512]), axis=AX.X, op=ALU.add)\
                            .then_inc(head_sum.sem, 1)
                    if c == 17:
                        normalised(l, 2, rt)
                    if c == 18:
                        dve.wait_ge(mo_ps.sem, mo_ps.at(l, 1))
                        dve.wait_ge(m_exp.sem, m_exp.at(l, 1))
                        chain.then(dve, nc.vector.reciprocal(mz, mz))
                        dve.wait_ge(tile2_out.sem, tile2_out.at(l, NT2))
                        for t in range(T):
                            for hh in range(4):
                                a = 4 * t + hh
                                ins = nc.vector.scalar_tensor_tensor(out=rows2[:, t, 512 + hh * P:512 + (hh + 1) * P],
                                                                     in0=ps[:, 4 + t, tok(hh)], scalar=mz[:, a:a + 1],
                                                                     in1=ev2[0][:, t, tok(hh)], op0=ALU.mult, op1=ALU.mult)
                            ins.then_inc(rows2_ready.sem, 1)
                    if c == OUT2_AT:
                        for t in range(T):
                            weighted2(l, 1, C_YW, t)
                            cols2_to_low(l, 1, t)
                    if c == OUT2_AT + 2:
                        dve.wait_ge(ple_root.sem, ple_root.at(l, 1))
                        dve.wait_ge(gain_loaded, (l + 1) * 16)
                        chain.then(dve, nc.vector.reciprocal(ple_ss, ple_ss))
                        for t in range(T):
                            ins = nc.vector.scalar_tensor_tensor(out=emb[:, t, :], in0=emb[:, t, :], scalar=ple_ss[:, t:t + 1],
                                                                 in1=ple_gain, op0=ALU.mult, op1=ALU.mult)
                        ins.then_inc(emb_ready.sem, 1)
                    if c == GATE_AT:
                        for t in range(T):
                            if t == 0:
                                dve.wait_ge(t0_done2.sem, t0_done2.at(l, 1))
                            else:
                                dve.wait_ge(products_done, l * CHUNKS2 + (BASE2 + GATE_AT + RING))
                            tt(h[:, t, :], h[:, t, :], ps[:, 2 * t:2 * t + 2, :].rearrange("p b n -> p (b n)"), ALU.add)\
                                .then_inc(h2_ready.sem, 1)
                            scaled_rows2(l, 2, t)
                        for t in range(T):
                            cols2_to_low(l, 2, t)
                for t in range(T):
                    dve.wait_ge(gate2_out.sem, gate2_out.at(l, t + 1))
                    chain.then(dve, tt(sg2[:, t, :], sg2[:, t, :], emb[:, t, :], ALU.mult))
                    tt(h[:, t, :], h[:, t, :], sg2[:, t, :], ALU.add).then_inc(h2_ready.sem, 1)
                assert chain.n == VCH2, chain.n


def constants():
    i = np.arange(P)
    c1 = np.zeros((P, N_CONST1), np.float32)
    c1[:, K_ID:K_ID + P] = np.eye(P)
    c1[:, K_TRI:K_TRI + P] = i[:, None] <= i[None, :]
    c1[:, K_LATER:K_LATER + P] = i[:, None] > i[None, :]
    c1[:, K_HEAD:K_HEAD + HEADS] = i[:, None] % HEADS == np.arange(HEADS)[None, :]
    dist = (P + i)[:, None] - np.arange(S)[None, :]
    for g, (window, dil) in enumerate(PATTERNS):
        ok = (dist >= 0) & (dist % dil == 0) & (dist // dil <= window // dil)
        c1[:, K_MASK + g * S:K_MASK + (g + 1) * S] = np.where(ok, 0.0, NEG)
    pos = np.arange(S, dtype=np.float32)

    def table(theta, width):
        half = width // 2
        inv = np.float32(theta) ** (-np.arange(half, dtype=np.float32) / np.float32(half))
        ang = (pos[:, None] * inv.astype(np.float32)[None, :]).astype(np.float32)
        c, s = np.cos(ang), np.sin(ang)
        both = [np.concatenate([c, c], 1), np.concatenate([-s, s], 1)]
        return [b.reshape(T, P, width).transpose(1, 0, 2).reshape(P, T * width) for b in both]

    c1[:, K_ROPE1:K_KDEC] = np.concatenate(table(500000.0, 32), 1)
    c2 = np.zeros((P, N_CONST2), np.float32)
    c2[:, K_ROPE2:K_DECAY] = np.concatenate(table(10000.0, P), 1)
    log_g = np.log1p(-np.power(2.0, -5.0 - np.arange(4)))
    rel = i[None, :] - i[:, None]
    for k in range(4):
        c2[:, K_DECAY + k * P:K_DECAY + (k + 1) * P] = np.where(rel >= 0, np.exp(log_g[k] * np.maximum(rel, 0)) * SCALE, 0)
        c2[:, K_QPOW + k * P:K_QPOW + (k + 1) * P] = np.exp(log_g[k] * (i + 1.0))[None, :]
        c1[:, K_KDEC + k] = np.exp(log_g[k] * (P - 1 - i)) * SCALE
    n = np.arange(S)
    exact = BUCKETS // 2
    nf = np.maximum(n, 1).astype(np.float32)
    large = exact + (np.log(nf / exact) / np.float32(np.log(MAX_DIST / exact)) * (BUCKETS - exact)).astype(np.int32)
    bucket = np.where(n < exact, n, np.minimum(large, BUCKETS - 1))
    onehot = np.zeros((BUCKETS + 1, REV), np.float32)
    for j in range(REV):
        onehot[bucket[S - 1 - j] if j < S else BUCKETS, j] = 1.0 if j < S else NEG
    return c1, c2, onehot


def by_tile(w, start):
    t = w[:, start:start + 512].reshape(2, 4, P, 512)
    return t.transpose(0, 2, 1, 3).reshape(2, P, CH)


def by_rows(w):
    return w.reshape(-1, 2, P, D).transpose(0, 2, 1, 3).reshape(-1, P, CH)


def by_pairs(w):
    t = w.reshape(2, 4, P, 2, NGU, 256).transpose(4, 0, 2, 1, 3, 5)
    return t.reshape(2 * NGU, P, CH)


def columns(v):
    return v.reshape(-1, P).T


def lay_out(a):
    first, second, pars = [], [], np.zeros((2 * L + 1, P, N_PAR), np.float32)
    for l in range(L):
        w = a["w_in"][l]
        for name in TILES1:
            kind = name.rstrip("0123456789")
            at = START1[kind] + 512 * (int(name[len(kind):]) if name[len(kind):] else 0)
            first.append(by_tile(w, at))
        first += [by_rows(a["w_ssd_branch"][l]), by_rows(a["w_attn_branch"][l]), by_rows(a["w_out"][l]),
                  by_pairs(a["w_gate_up"][l]), by_rows(a["w_down"][l])]
        p = pars[l]
        p[:, C_MIX:C_MIX + 8] = columns(a["norm_mix"][l])
        p[:, C_FFN:C_FFN + 8] = columns(a["norm_ffn"][l])
        p[:, C_CW:C_CB] = a["conv_w"][l].reshape(TAPS, 24, P).transpose(2, 1, 0).reshape(P, 24 * TAPS)
        p[:, C_CB:C_SN] = columns(a["conv_b"][l])
        p[:, C_SN:C_DTB] = columns(a["ssd_norm"][l])
        p[:, C_DTB:C_AL] = a["dt_bias"][l]
        p[:, C_AL:C_DS] = a["a_log"][l]
        p[:, C_DS:C_WDT] = a["d_skip"][l]
        p[:, C_WDT:N_PAR1] = w[:, DT_AT:DT_AT + HEADS].reshape(KD, P, HEADS).transpose(1, 0, 2).reshape(P, -1)
    for l in range(L):
        w = a["w_in_2"][l]
        second += [by_tile(w, START2[name]) for name in TILES2]
        second += [by_rows(a["w_ple_2"][l]), by_rows(a["w_out_2"][l]), by_rows(a["w_ple_gate_2"][l])]
        p = pars[L + l]
        p[:, C_NG:C_NG + 8] = columns(a["norm_g_2"][l])
        p[:, C_YW:C_YW + 4] = columns(a["ret_norm_g_2"][l])
        p[:, C_YW + 4:C_YW + 8] = 1.0
        p[:, C_QN] = a["q_norm_g_2"][l]
        p[:, C_KN] = a["k_norm_g_2"][l]
        p[:, C_PT:C_PT + 2 * S] = a["p_2"][l, 0].T.reshape(2, P, S).transpose(1, 0, 2).reshape(P, 2 * S)
    c1, c2, onehot = constants()
    return {
        "stream1": np.concatenate(first).reshape(-1, CH), "stream2": np.concatenate(second).reshape(-1, CH),
        "pars": pars.reshape(-1, N_PAR), "const1": c1, "const2": c2, "onehot": onehot,
        "relb": np.concatenate([a["rel_bias_2"], np.ones((1, 4), np.float32)]),
        "final_g": np.broadcast_to(a["norm_final"], (P, D)).copy(),
        "ple_g": np.broadcast_to(a["ple_norm_g_2"][:, None, :], (L, P, D)).reshape(L * P, D).copy(),
        "x": a["x"][0],
    }


def kernel(**inputs):
    import concourse.bacc as bacc
    from concourse.bass_utils import run_bass_kernel_spmd

    arrays = lay_out({k: np.asarray(v) for k, v in inputs.items()})
    nc = bacc.Bacc("TRN2", target_bir_lowering=False, num_devices=1, dynamic_dma_scratch_size=1024)
    args = {n: nc.dram_tensor(f"in_{n}", a.shape, F32, kind="ExternalInput").ap() for n, a in arrays.items()}
    out = nc.dram_tensor("out", (S, D), F32, kind="ExternalOutput").ap()
    rev = nc.dram_tensor("rev", (P, 4 * REV), F32, kind="Internal").ap()
    args["w_x"] = args.pop("x")
    build(nc, out=out, rev=rev, **args)
    r = run_bass_kernel_spmd(nc, [{f"in_{n}": a for n, a in arrays.items()}], core_ids=[0])
    return r.results[0]["out"].reshape(1, S, D)
```
